# Optimizing a Trainium2 kernel written in Bass

```python
import math
import jax
import jax.numpy as jnp
from jax import lax
import numpy as np
import jax, jax.numpy as jnp

D_MODEL = 1024
BATCH = 1
SEQ = 512
DEPTH = 2

N_A_LAYERS = (DEPTH + 1) // 2
N_B_LAYERS = DEPTH - N_A_LAYERS

GDN_HEADS = 8
GDN_HEAD_DIM = 128
GDN_WIDTH = GDN_HEADS * GDN_HEAD_DIM
GDN_CONV = 4
GDN_CHUNK = 64

NSA_HEADS = 16
NSA_GROUPS = 4
NSA_HPG = NSA_HEADS // NSA_GROUPS
NSA_HEAD_DIM = 64
NSA_WIDTH = NSA_HEADS * NSA_HEAD_DIM
CMP_BLOCK = 32
CMP_STRIDE = 16
CMP_HIDDEN = 2 * NSA_HEAD_DIM
SEL_BLOCK = 64
TOP_N = 16
WINDOW = 512
Q_BLOCK = 128
N_BRANCHES = 3
N_KV_PARTS = 2 * N_BRANCHES

REL_BUCKETS = 32
REL_MAX_DIST = 128

MOE_GROUPS = 4
MOE_EXPERTS_PER_GROUP = 4
MOE_EXPERTS = MOE_GROUPS * MOE_EXPERTS_PER_GROUP
MOE_TOP_K = 2
MOE_HIDDEN = 256

DEEPNORM_ALPHA = (2 * DEPTH) ** 0.25
DEEPNORM_BETA = (8 * DEPTH) ** -0.25
LN_EPS = 1e-5
NORM_EPS = 1e-6
NEG_INF = -1e30


def layer_norm(x, g, b):
    xf = x.astype(jnp.float32)
    mu = jnp.mean(xf, -1, keepdims=True)
    var = jnp.mean(jnp.square(xf - mu), -1, keepdims=True)
    return ((xf - mu) * lax.rsqrt(var + LN_EPS) * g.astype(jnp.float32) + b.astype(jnp.float32)).astype(x.dtype)

def rms_norm(x, g):
    xf = x.astype(jnp.float32)
    return xf * lax.rsqrt(jnp.mean(xf * xf, -1, keepdims=True) + NORM_EPS) * g.astype(jnp.float32)

def l2_normalize(x):
    xf = x.astype(jnp.float32)
    return xf * lax.rsqrt(jnp.sum(xf * xf, -1, keepdims=True) + NORM_EPS)

def causal_depthwise_conv(x, w):
    k, c = w.shape
    return lax.conv_general_dilated(x, w[:, None, :].astype(x.dtype), window_strides=(1,),
                                    padding=[(k - 1, 0)], dimension_numbers=('NWC', 'WIO', 'NWC'),
                                    feature_group_count=c)

def masked_softmax(s, mask):
    return jax.nn.softmax(jnp.where(mask, s, NEG_INF), axis=-1) * mask

def gated_delta_rule_chunked(q, k, v, g, beta):
    b, t, h, dk = q.shape
    dv = v.shape[-1]
    c = GDN_CHUNK
    n = t // c

    def chunks(a):
        a = jnp.moveaxis(a.astype(jnp.float32), 1, 2)
        return a.reshape((b, h, n, c) + a.shape[3:])

    q, k, v, g, beta = chunks(q), chunks(k), chunks(v), chunks(g), chunks(beta)
    gc = jnp.cumsum(g, axis=-1)
    idx = jnp.arange(c)
    causal = idx[:, None] >= idx[None, :]
    decay = jnp.exp(jnp.where(causal, gc[..., :, None] - gc[..., None, :], -jnp.inf))
    k_beta = k * beta[..., None]
    a_strict = jnp.where(idx[:, None] > idx[None, :],
                         jnp.einsum('bhncd,bhnsd->bhncs', k_beta, k) * decay, 0.0)
    tri = a_strict + jnp.eye(c, dtype=jnp.float32)
    u = lax.linalg.triangular_solve(tri, v * beta[..., None], left_side=True, lower=True, unit_diagonal=True)
    w = lax.linalg.triangular_solve(tri, k_beta * jnp.exp(gc)[..., None], left_side=True, lower=True,
                                    unit_diagonal=True)
    qk = jnp.einsum('bhncd,bhnsd->bhncs', q, k) * decay
    g_last = gc[..., -1:]
    q_dec = q * jnp.exp(gc)[..., None]
    k_dec = k * jnp.exp(g_last - gc)[..., None]
    d_last = jnp.exp(g_last[..., 0])
    xs = (jnp.moveaxis(q_dec, 2, 0), jnp.moveaxis(qk, 2, 0), jnp.moveaxis(u, 2, 0),
          jnp.moveaxis(w, 2, 0), jnp.moveaxis(k_dec, 2, 0), jnp.moveaxis(d_last, 2, 0))

    def step(state, inp):
        q_c, qk_c, u_c, w_c, k_c, d_c = inp
        v_new = u_c - jnp.einsum('bhcd,bhde->bhce', w_c, state)
        o_c = jnp.einsum('bhcd,bhde->bhce', q_c, state) + jnp.einsum('bhcs,bhse->bhce', qk_c, v_new)
        state = state * d_c[..., None, None] + jnp.einsum('bhcd,bhce->bhde', k_c, v_new)
        return state, o_c

    _, o = lax.scan(step, jnp.zeros((b, h, dk, dv), jnp.float32), xs)
    return jnp.moveaxis(o, 0, 2).reshape(b, h, t, dv).transpose(0, 2, 1, 3)

def gdn_mixer(x, w_in, conv_w, a_log, dt_bias, norm_w, w_o):
    b, t, _ = x.shape
    hk = GDN_WIDTH
    proj = x @ w_in
    qkv = jax.nn.silu(causal_depthwise_conv(proj[..., :3 * hk], conv_w))
    shp = (b, t, GDN_HEADS, GDN_HEAD_DIM)
    q = l2_normalize(qkv[..., :hk].reshape(shp)) * (GDN_HEAD_DIM ** -0.5)
    k = l2_normalize(qkv[..., hk:2 * hk].reshape(shp))
    v = qkv[..., 2 * hk:3 * hk].reshape(shp)
    z = proj[..., 3 * hk:4 * hk].reshape(shp).astype(jnp.float32)
    a = proj[..., 4 * hk:4 * hk + GDN_HEADS].astype(jnp.float32)
    bt = proj[..., 4 * hk + GDN_HEADS:].astype(jnp.float32)
    g = -jnp.exp(a_log.astype(jnp.float32)) * jax.nn.softplus(a + dt_bias.astype(jnp.float32))
    beta = jax.nn.sigmoid(bt)
    o = gated_delta_rule_chunked(q, k, v, g, beta)
    o = rms_norm(o, norm_w) * jax.nn.silu(z)
    return o.reshape(b, t, hk).astype(x.dtype) @ w_o

def t5_bucket(dist):
    n = jnp.maximum(dist, 0)
    max_exact = REL_BUCKETS // 2
    nf = jnp.maximum(n, 1).astype(jnp.float32)
    large = max_exact + (jnp.log(nf / max_exact) / math.log(REL_MAX_DIST / max_exact)
                         * (REL_BUCKETS - max_exact)).astype(jnp.int32)
    large = jnp.minimum(large, REL_BUCKETS - 1)
    return jnp.where(n < max_exact, n, large)

def t5_bias(dist, rel_tbl):
    dist = jnp.broadcast_to(dist, (NSA_GROUPS,) + dist.shape[-2:])
    tbl = rel_tbl.astype(jnp.float32).reshape(REL_BUCKETS, NSA_GROUPS, NSA_HPG)
    bias = tbl[t5_bucket(dist), jnp.arange(NSA_GROUPS)[:, None, None]]
    return bias.transpose(0, 3, 1, 2)

def compress_blocks(x, pos, w1, w2):
    b, t, g, dk = x.shape
    nc = (t - CMP_BLOCK) // CMP_STRIDE + 1
    idx = jnp.arange(nc)[:, None] * CMP_STRIDE + jnp.arange(CMP_BLOCK)[None, :]
    blk = x[:, idx] + pos[None, None, :, None, :]
    blk = blk.transpose(0, 3, 1, 2, 4).reshape(b, g, nc, CMP_BLOCK * dk)
    return jax.nn.silu(blk @ w1) @ w2

def nsa_shared_kv(h, w_kv, cmp_k_pos, cmp_k_w1, cmp_k_w2, cmp_v_pos, cmp_v_w1, cmp_v_w2):
    b, t, _ = h.shape
    kv = (h @ w_kv).reshape(b, t, N_KV_PARTS, NSA_GROUPS, NSA_HEAD_DIM)
    kc_raw, vc_raw, ks, vs, kw, vw = jnp.moveaxis(kv, 2, 0)
    kc = compress_blocks(kc_raw, cmp_k_pos, cmp_k_w1, cmp_k_w2)
    vc = compress_blocks(vc_raw, cmp_v_pos, cmp_v_w1, cmp_v_w2)
    nb = t // SEL_BLOCK

    def to_blocks(a):
        return a.transpose(0, 2, 1, 3).reshape(b, NSA_GROUPS, nb, SEL_BLOCK, NSA_HEAD_DIM)

    def pad_front(a):
        return jnp.pad(a.transpose(0, 2, 1, 3), ((0, 0), (0, 0), (WINDOW, 0), (0, 0)))

    return (kc, vc, to_blocks(ks), to_blocks(vs), pad_front(kw), pad_front(vw))

def nsa_attention(q, gates, kc, vc, ks, vs, kw, vw, rel_tbl):
    b, t = q.shape[:2]
    nc = kc.shape[2]
    nb = ks.shape[2]
    nq = t // Q_BLOCK
    n_sel = min(TOP_N, nb)
    scale = NSA_HEAD_DIM ** -0.5
    cmp_end = jnp.arange(nc) * CMP_STRIDE + CMP_BLOCK - 1
    cmp_start = jnp.arange(nc) * CMP_STRIDE
    sel_start = jnp.arange(nb) * SEL_BLOCK
    overlap = ((cmp_start[:, None] < sel_start[None, :] + SEL_BLOCK)
               & (cmp_end[:, None] >= sel_start[None, :])).astype(jnp.float32)
    g_ix = jnp.arange(NSA_GROUPS)[:, None, None]

    def per_batch(args):
        q_b, gate_b, kc_b, vc_b, ks_b, vs_b, kw_b, vw_b = args
        kc_f, vc_f = kc_b.astype(jnp.float32), vc_b.astype(jnp.float32)
        qb = q_b.reshape(nq, Q_BLOCK, NSA_GROUPS, NSA_HPG, NSA_HEAD_DIM)
        gb = gate_b.reshape(nq, Q_BLOCK, NSA_GROUPS, NSA_HPG, N_BRANCHES)

        def per_block(blk):
            q_c, gate_c, c = blk
            tq = c * Q_BLOCK + jnp.arange(Q_BLOCK)
            qf = q_c.astype(jnp.float32)
            s = jnp.einsum('qghd,gnd->ghqn', qf, kc_f) * scale + t5_bias(tq[:, None] - cmp_end[None, :], rel_tbl)
            p_cmp = masked_softmax(s, cmp_end[None, :] <= tq[:, None])
            o_cmp = jnp.einsum('ghqn,gnd->qghd', p_cmp, vc_f)
            imp = jnp.einsum('ghqn,nj->gqj', p_cmp, overlap)
            jq = (tq // SEL_BLOCK)[:, None]
            jb = jnp.arange(nb)[None, :]
            forced = (jb == 0) | (jb == jq) | (jb == jq - 1)
            imp = jnp.where(forced, jnp.inf, jnp.where(jb <= jq, imp, -jnp.inf))
            _, sel = lax.top_k(imp, n_sel)
            k_sel = ks_b[g_ix, sel].reshape(NSA_GROUPS, Q_BLOCK, n_sel * SEL_BLOCK, NSA_HEAD_DIM)
            v_sel = vs_b[g_ix, sel].reshape(NSA_GROUPS, Q_BLOCK, n_sel * SEL_BLOCK, NSA_HEAD_DIM)
            kpos = (sel[..., None] * SEL_BLOCK + jnp.arange(SEL_BLOCK)).reshape(NSA_GROUPS, Q_BLOCK, -1)
            dist = tq[None, :, None] - kpos
            s = jnp.einsum('qghd,gqkd->ghqk', qf, k_sel.astype(jnp.float32)) * scale + t5_bias(dist, rel_tbl)
            p = masked_softmax(s, (dist >= 0)[:, None])
            o_sel = jnp.einsum('ghqk,gqkd->qghd', p, v_sel.astype(jnp.float32))
            k_win = lax.dynamic_slice_in_dim(kw_b, c * Q_BLOCK, WINDOW + Q_BLOCK, axis=1).astype(jnp.float32)
            v_win = lax.dynamic_slice_in_dim(vw_b, c * Q_BLOCK, WINDOW + Q_BLOCK, axis=1).astype(jnp.float32)
            kp = c * Q_BLOCK - WINDOW + jnp.arange(WINDOW + Q_BLOCK)
            dist = tq[:, None] - kp[None, :]
            mask = (dist >= 0) & (dist < WINDOW) & (kp[None, :] >= 0)
            s = jnp.einsum('qghd,gkd->ghqk', qf, k_win) * scale + t5_bias(dist, rel_tbl)
            p = masked_softmax(s, mask)
            o_win = jnp.einsum('ghqk,gkd->qghd', p, v_win)
            gt = jax.nn.sigmoid(gate_c.astype(jnp.float32))
            return gt[..., 0:1] * o_cmp + gt[..., 1:2] * o_sel + gt[..., 2:3] * o_win

        o = lax.map(per_block, (qb, gb, jnp.arange(nq)))
        return o.reshape(t, NSA_WIDTH)

    return lax.map(per_batch, (q, gates, kc, vc, ks, vs, kw, vw))

def nsa_mixer(h, shared, w_in, w_o, rel_tbl):
    b, t, _ = h.shape
    proj = h @ w_in
    q = proj[..., :NSA_WIDTH].reshape(b, t, NSA_GROUPS, NSA_HPG, NSA_HEAD_DIM)
    gates = proj[..., NSA_WIDTH:].reshape(b, t, NSA_GROUPS, NSA_HPG, N_BRANCHES)
    kc, vc, ks, vs, kw, vw = shared
    o = nsa_attention(q, gates, kc, vc, ks, vs, kw, vw, rel_tbl)
    return o.astype(h.dtype) @ w_o

def hier_moe(x, w_grp, b_grp, w_rt, b_rt, w_gate, w_up, w_down):
    b, t, d = x.shape
    xt = x.reshape(b * t, d)
    grp_p = jax.nn.softmax((xt @ w_grp + b_grp).astype(jnp.float32), axis=-1)
    grp_prob, grp_idx = lax.top_k(grp_p, 1)
    e_logits = (xt @ w_rt + b_rt).astype(jnp.float32).reshape(-1, MOE_GROUPS, MOE_EXPERTS_PER_GROUP)
    e_logits = jnp.take_along_axis(e_logits, grp_idx[:, :, None], axis=1)[:, 0]
    top_p, top_i = lax.top_k(jax.nn.softmax(e_logits, axis=-1), MOE_TOP_K)
    top_w = grp_prob * top_p / jnp.sum(top_p, -1, keepdims=True)
    expert_id = grp_idx * MOE_EXPERTS_PER_GROUP + top_i
    gate = jnp.sum(jax.nn.one_hot(expert_id, MOE_EXPERTS, dtype=jnp.float32) * top_w[..., None], axis=1)

    def step(acc, e_in):
        wg, wu, wd, ge = e_in
        hdn = jax.nn.silu(xt @ wg) * (xt @ wu)
        return acc + ge[:, None] * (hdn @ wd).astype(jnp.float32), None

    y, _ = lax.scan(step, jnp.zeros((b * t, d), jnp.float32), (w_gate, w_up, w_down, gate.T))
    return y.astype(x.dtype).reshape(b, t, d)

def first_inputs(seed: int = 0) -> dict:
    key = jax.random.key(seed)
    keys = iter(jax.random.split(key, 40))

    def nrm(shape, scale):
        return jax.random.normal(next(keys), shape, jnp.float32) * scale

    na, nb_l, d = N_A_LAYERS, N_B_LAYERS, D_MODEL
    dt = jnp.exp(jax.random.uniform(next(keys), (na, GDN_HEADS), jnp.float32,
                                    minval=math.log(1e-3), maxval=math.log(0.1)))
    return {
        'x': nrm((BATCH, SEQ, d), 1.0),
        'gdn_w_in': nrm((na, d, 4 * GDN_WIDTH + 2 * GDN_HEADS), d ** -0.5),
        'gdn_conv_w': nrm((na, GDN_CONV, 3 * GDN_WIDTH), GDN_CONV ** -0.5),
        'gdn_a_log': jnp.log(jax.random.uniform(next(keys), (na, GDN_HEADS), jnp.float32, minval=1.0, maxval=16.0)),
        'gdn_dt_bias': dt + jnp.log(-jnp.expm1(-dt)),
        'gdn_norm_w': 1.0 + nrm((na, GDN_HEAD_DIM), 0.01),
        'gdn_w_o': nrm((na, GDN_WIDTH, d), GDN_WIDTH ** -0.5 * DEEPNORM_BETA),
        'nsa_w_kv': nrm((d, N_KV_PARTS * NSA_GROUPS * NSA_HEAD_DIM), d ** -0.5),
        'cmp_k_pos': nrm((CMP_BLOCK, NSA_HEAD_DIM), 0.1),
        'cmp_k_w1': nrm((CMP_BLOCK * NSA_HEAD_DIM, CMP_HIDDEN), (CMP_BLOCK * NSA_HEAD_DIM) ** -0.5),
        'cmp_k_w2': nrm((CMP_HIDDEN, NSA_HEAD_DIM), CMP_HIDDEN ** -0.5),
        'cmp_v_pos': nrm((CMP_BLOCK, NSA_HEAD_DIM), 0.1),
        'cmp_v_w1': nrm((CMP_BLOCK * NSA_HEAD_DIM, CMP_HIDDEN), (CMP_BLOCK * NSA_HEAD_DIM) ** -0.5),
        'cmp_v_w2': nrm((CMP_HIDDEN, NSA_HEAD_DIM), CMP_HIDDEN ** -0.5),
        'nsa_w_in': nrm((nb_l, d, NSA_WIDTH + N_BRANCHES * NSA_HEADS), d ** -0.5),
        'nsa_w_o': nrm((nb_l, NSA_WIDTH, d), NSA_WIDTH ** -0.5 * DEEPNORM_BETA),
        'rel_bias': nrm((REL_BUCKETS, NSA_HEADS), 0.5),
        'ln_mix_g': 1.0 + nrm((DEPTH, d), 0.01),
        'ln_mix_b': nrm((DEPTH, d), 0.01),
        'ln_ffn_g': 1.0 + nrm((DEPTH, d), 0.01),
        'ln_ffn_b': nrm((DEPTH, d), 0.01),
        'moe_w_grp': nrm((DEPTH, d, MOE_GROUPS), d ** -0.5),
        'moe_b_grp': nrm((DEPTH, MOE_GROUPS), 0.01),
        'moe_w_rt': nrm((DEPTH, d, MOE_EXPERTS), d ** -0.5),
        'moe_b_rt': nrm((DEPTH, MOE_EXPERTS), 0.01),
        'moe_w_gate': nrm((DEPTH, MOE_EXPERTS, d, MOE_HIDDEN), d ** -0.5),
        'moe_w_up': nrm((DEPTH, MOE_EXPERTS, d, MOE_HIDDEN), d ** -0.5),
        'moe_w_down': nrm((DEPTH, MOE_EXPERTS, MOE_HIDDEN, d), MOE_HIDDEN ** -0.5 * DEEPNORM_BETA),
    }

def first_block(x, gdn_w_in, gdn_conv_w, gdn_a_log, gdn_dt_bias, gdn_norm_w, gdn_w_o,
              nsa_w_kv, cmp_k_pos, cmp_k_w1, cmp_k_w2, cmp_v_pos, cmp_v_w1, cmp_v_w2,
              nsa_w_in, nsa_w_o, rel_bias,
              ln_mix_g, ln_mix_b, ln_ffn_g, ln_ffn_b,
              moe_w_grp, moe_b_grp, moe_w_rt, moe_b_rt, moe_w_gate, moe_w_up, moe_w_down):
    h = x
    shared = None
    for layer in range(DEPTH):
        if layer < N_A_LAYERS:
            i = layer
            mix = gdn_mixer(h, gdn_w_in[i], gdn_conv_w[i], gdn_a_log[i], gdn_dt_bias[i], gdn_norm_w[i], gdn_w_o[i])
        else:
            i = layer - N_A_LAYERS
            mix = nsa_mixer(h, shared, nsa_w_in[i], nsa_w_o[i], rel_bias)
        h = layer_norm(DEEPNORM_ALPHA * h + mix, ln_mix_g[layer], ln_mix_b[layer])
        ffn = hier_moe(h, moe_w_grp[layer], moe_b_grp[layer], moe_w_rt[layer], moe_b_rt[layer],
                       moe_w_gate[layer], moe_w_up[layer], moe_w_down[layer])
        h = layer_norm(DEEPNORM_ALPHA * h + ffn, ln_ffn_g[layer], ln_ffn_b[layer])
        if layer == N_A_LAYERS - 1:
            shared = nsa_shared_kv(h, nsa_w_kv, cmp_k_pos, cmp_k_w1, cmp_k_w2, cmp_v_pos, cmp_v_w1, cmp_v_w2)
    return h


CHUNK = 64
EPS = 1e-6
NEG_INF_2 = -1e30
N_BRANCH = 3
BR_WIDTH = 512

SGU_BLOCK = 128
SGU_GROUPS = 8
SGU_GROUP_DIM = BR_WIDTH // SGU_GROUPS

MLA_HEADS = 8
MLA_NOPE = 64
MLA_ROPE = 32
MLA_V = 64
MLA_QK = MLA_NOPE + MLA_ROPE
MLA_Q_RANK = 256
MLA_KV_RANK = 128
ROPE_BASE = 10000.0

CA_HEADS = 8
CA_HEAD_DIM = BR_WIDTH // CA_HEADS
LEFT_CHUNKS = 8
BAND = (LEFT_CHUNKS + 1) * CHUNK
REL_CLIP = 128

IN_WIDTHS = (BR_WIDTH, BR_WIDTH, BR_WIDTH,
             MLA_Q_RANK, MLA_KV_RANK, MLA_ROPE, BR_WIDTH,
             BR_WIDTH, BR_WIDTH, BR_WIDTH, BR_WIDTH,
             N_BRANCH * D_MODEL)
D_IN = sum(IN_WIDTHS)


def rmsnorm(x, g):
    xf = x.astype(jnp.float32)
    y = xf * lax.rsqrt(jnp.mean(xf * xf, axis=-1, keepdims=True) + EPS)
    return (y * g.astype(jnp.float32)).astype(x.dtype)

def layernorm(x, g, b):
    xf = x.astype(jnp.float32)
    mu = jnp.mean(xf, axis=-1, keepdims=True)
    xc = xf - mu
    y = xc * lax.rsqrt(jnp.mean(xc * xc, axis=-1, keepdims=True) + EPS)
    return (y * g.astype(jnp.float32) + b.astype(jnp.float32)).astype(x.dtype)

def apply_rope(x, pos):
    half = x.shape[-1] // 2
    inv = ROPE_BASE ** (-jnp.arange(half, dtype=jnp.float32) / half)
    ang = pos.astype(jnp.float32)[:, None] * inv[None, :]
    cos = jnp.cos(ang)[:, None, :]
    sin = jnp.sin(ang)[:, None, :]
    xf = x.astype(jnp.float32)
    x1, x2 = xf[..., :half], xf[..., half:]
    return jnp.concatenate([x1 * cos - x2 * sin, x1 * sin + x2 * cos], axis=-1).astype(x.dtype)

def sgu_mixer(u, v, ln_g, ln_b, w_s, b_s):
    B, S, _ = u.shape
    nb = S // SGU_BLOCK
    v = layernorm(v, ln_g, ln_b)
    vb = v.reshape(B, nb, SGU_BLOCK, SGU_GROUPS, SGU_GROUP_DIM)
    tri = jnp.tril(jnp.ones((SGU_BLOCK, SGU_BLOCK), dtype=bool))
    ws = jnp.where(tri[None], w_s, 0.0).astype(v.dtype)
    mixed = jnp.einsum('gts,bnsgc->bntgc', ws, vb) + b_s.T.astype(v.dtype)[None, None, :, :, None]
    return u * mixed.reshape(B, S, BR_WIDTH)

def mla_mixer(q_down, kv_down, k_rope_in, q_norm_g, kv_norm_g, w_uq, w_ukv, pos):
    B, S, _ = q_down.shape
    cq = rmsnorm(q_down, q_norm_g)
    q = (cq @ w_uq).reshape(B, S, MLA_HEADS, MLA_QK)
    q = jnp.concatenate([q[..., :MLA_NOPE], apply_rope(q[..., MLA_NOPE:], pos)], axis=-1)
    ckv = rmsnorm(kv_down, kv_norm_g)
    kv = (ckv @ w_ukv).reshape(B, S, MLA_HEADS, MLA_NOPE + MLA_V)
    k_nope, v = kv[..., :MLA_NOPE], kv[..., MLA_NOPE:]
    k_r = apply_rope(k_rope_in[:, :, None, :], pos)
    k = jnp.concatenate([k_nope, jnp.broadcast_to(k_r, (B, S, MLA_HEADS, MLA_ROPE))], axis=-1)
    scale = MLA_QK ** -0.5
    nqb = S // Q_BLOCK
    qb = q.reshape(B, nqb, Q_BLOCK, MLA_HEADS, MLA_QK).transpose(1, 0, 2, 3, 4)
    key_chunk = jnp.arange(S) // CHUNK

    def block(args):
        qi, bi = args
        s = jnp.einsum('bqhd,bkhd->bhqk', qi, k).astype(jnp.float32) * scale
        q_chunk = (bi * Q_BLOCK + jnp.arange(Q_BLOCK)) // CHUNK
        mask = key_chunk[None, :] <= q_chunk[:, None]
        s = jnp.where(mask[None, None], s, NEG_INF_2)
        p = jax.nn.softmax(s, axis=-1).astype(v.dtype)
        return jnp.einsum('bhqk,bkhd->bqhd', p, v)

    o = lax.map(block, (qb, jnp.arange(nqb)))
    return o.transpose(1, 0, 2, 3, 4).reshape(B, S, MLA_HEADS * MLA_V)

def chunk_band_mixer(q, k, v, rel_table):
    B, S, _ = q.shape
    nc = S // CHUNK
    pad = LEFT_CHUNKS * CHUNK
    q = q.reshape(B, S, CA_HEADS, CA_HEAD_DIM)
    k = k.reshape(B, S, CA_HEADS, CA_HEAD_DIM)
    v = v.reshape(B, S, CA_HEADS, CA_HEAD_DIM)
    kp = jnp.pad(k, ((0, 0), (pad, 0), (0, 0), (0, 0)))
    vp = jnp.pad(v, ((0, 0), (pad, 0), (0, 0), (0, 0)))
    qc = q.reshape(B, nc, CHUNK, CA_HEADS, CA_HEAD_DIM).transpose(1, 0, 2, 3, 4)
    i = jnp.arange(CHUNK)
    j = jnp.arange(BAND)
    dist = i[:, None] + pad - j[None, :]
    idx = jnp.clip(dist, -REL_CLIP, REL_CLIP) + REL_CLIP
    bias = rel_table[:, idx].astype(jnp.float32)
    scale = CA_HEAD_DIM ** -0.5

    def chunk(args):
        qi, ci = args
        kb = lax.dynamic_slice_in_dim(kp, ci * CHUNK, BAND, axis=1)
        vb = lax.dynamic_slice_in_dim(vp, ci * CHUNK, BAND, axis=1)
        s = jnp.einsum('bqhd,bkhd->bhqk', qi, kb).astype(jnp.float32) * scale + bias[None]
        valid = j >= (LEFT_CHUNKS - ci) * CHUNK
        s = jnp.where(valid[None, None, None, :], s, NEG_INF_2)
        p = jax.nn.softmax(s, axis=-1).astype(vb.dtype)
        return jnp.einsum('bhqk,bkhd->bqhd', p, vb)

    o = lax.map(chunk, (qc, jnp.arange(nc)))
    return o.transpose(1, 0, 2, 3, 4).reshape(B, S, BR_WIDTH)

def second_inputs(seed: int = 0) -> dict:
    key = jax.random.key(seed)
    ks = jax.random.split(key, 16)
    f32 = jnp.float32
    L, D = DEPTH, D_MODEL
    nrm = lambda k, shape, s: jax.random.normal(k, shape, f32) * s
    return {
        "x": jax.random.normal(ks[0], (BATCH, SEQ, D), f32),
        "w_in": nrm(ks[1], (L, D, D_IN), D ** -0.5),
        "pre_g": 1.0 + nrm(ks[2], (L, D), 0.1),
        "post_g": 1.0 + nrm(ks[3], (L, D), 0.1),
        "sgu_ln_g": 1.0 + nrm(ks[4], (L, BR_WIDTH), 0.1),
        "sgu_ln_b": nrm(ks[5], (L, BR_WIDTH), 0.02),
        "sgu_w": nrm(ks[6], (L, SGU_GROUPS, SGU_BLOCK, SGU_BLOCK), SGU_BLOCK ** -0.5),
        "sgu_b": 1.0 + nrm(ks[7], (L, SGU_GROUPS, SGU_BLOCK), 0.1),
        "mla_q_norm_g": 1.0 + nrm(ks[8], (L, MLA_Q_RANK), 0.1),
        "mla_kv_norm_g": 1.0 + nrm(ks[9], (L, MLA_KV_RANK), 0.1),
        "mla_w_uq": nrm(ks[10], (L, MLA_Q_RANK, MLA_HEADS * MLA_QK), MLA_Q_RANK ** -0.5),
        "mla_w_ukv": nrm(ks[11], (L, MLA_KV_RANK, MLA_HEADS * (MLA_NOPE + MLA_V)), MLA_KV_RANK ** -0.5),
        "ca_rel_bias": nrm(ks[12], (L, CA_HEADS, 2 * REL_CLIP + 1), 0.5),
        "w_branch": nrm(ks[13], (L, N_BRANCH, BR_WIDTH, D), BR_WIDTH ** -0.5),
        "gate_b": nrm(ks[14], (L, N_BRANCH, D), 0.1),
        "w_out": nrm(ks[15], (L, D, D), D ** -0.5),
    }

def second_block(x, w_in, pre_g, post_g, sgu_ln_g, sgu_ln_b, sgu_w, sgu_b,
              mla_q_norm_g, mla_kv_norm_g, mla_w_uq, mla_w_ukv, ca_rel_bias,
              w_branch, gate_b, w_out):
    B, S, D = x.shape
    pos = jnp.arange(S)
    offsets = [0]
    for w in IN_WIDTHS:
        offsets.append(offsets[-1] + w)
    for l in range(DEPTH):
        xn = rmsnorm(x, pre_g[l])
        proj = xn @ w_in[l]
        (u_a, v_a, z_a, qd_b, kvd_b, kr_b, z_b,
         q_c, k_c, v_c, z_c, g_logits) = [proj[..., offsets[n]:offsets[n + 1]] for n in range(len(IN_WIDTHS))]
        y_a = sgu_mixer(u_a, v_a, sgu_ln_g[l], sgu_ln_b[l], sgu_w[l], sgu_b[l]) * jax.nn.silu(z_a)
        y_b = mla_mixer(qd_b, kvd_b, kr_b, mla_q_norm_g[l], mla_kv_norm_g[l],
                        mla_w_uq[l], mla_w_ukv[l], pos) * jax.nn.silu(z_b)
        y_c = chunk_band_mixer(q_c, k_c, v_c, ca_rel_bias[l]) * jax.nn.silu(z_c)
        ys = jnp.stack([y_a, y_b, y_c], axis=2)
        br = jnp.einsum('bsnc,ncd->bsnd', ys, w_branch[l])
        gates = jax.nn.sigmoid(g_logits.reshape(B, S, N_BRANCH, D) + gate_b[l])
        merged = jnp.sum(gates * br, axis=2)
        x = x + rmsnorm(merged @ w_out[l], post_g[l])
    return x


def setup_inputs(seed=0):
    out = dict(first_inputs(seed))
    for name, value in second_inputs(seed + 1).items():
        if name != "x":
            out[name + "_2"] = value
    return out


def reference(
    x, gdn_w_in, gdn_conv_w, gdn_a_log, gdn_dt_bias, gdn_norm_w, gdn_w_o, nsa_w_kv, cmp_k_pos,
    cmp_k_w1, cmp_k_w2, cmp_v_pos, cmp_v_w1, cmp_v_w2, nsa_w_in, nsa_w_o, rel_bias, ln_mix_g,
    ln_mix_b, ln_ffn_g, ln_ffn_b, moe_w_grp, moe_b_grp, moe_w_rt, moe_b_rt, moe_w_gate,
    moe_w_up, moe_w_down, w_in_2, pre_g_2, post_g_2, sgu_ln_g_2, sgu_ln_b_2, sgu_w_2, sgu_b_2,
    mla_q_norm_g_2, mla_kv_norm_g_2, mla_w_uq_2, mla_w_ukv_2, ca_rel_bias_2, w_branch_2,
    gate_b_2, w_out_2,
):
    x = first_block(
        x, gdn_w_in, gdn_conv_w, gdn_a_log, gdn_dt_bias, gdn_norm_w, gdn_w_o, nsa_w_kv,
        cmp_k_pos, cmp_k_w1, cmp_k_w2, cmp_v_pos, cmp_v_w1, cmp_v_w2, nsa_w_in, nsa_w_o,
        rel_bias, ln_mix_g, ln_mix_b, ln_ffn_g, ln_ffn_b, moe_w_grp, moe_b_grp, moe_w_rt,
        moe_b_rt, moe_w_gate, moe_w_up, moe_w_down,
    )
    return second_block(
        x, w_in_2, pre_g_2, post_g_2, sgu_ln_g_2, sgu_ln_b_2, sgu_w_2, sgu_b_2, mla_q_norm_g_2,
        mla_kv_norm_g_2, mla_w_uq_2, mla_w_ukv_2, ca_rel_bias_2, w_branch_2, gate_b_2, w_out_2,
    )


_drawn_inputs = setup_inputs


def setup_inputs(seed=0):
    import zlib

    import numpy as np

    out = dict(_drawn_inputs(seed))
    spreads = {}
    factors = {'gdn_norm_w': 6.586,
     'cmp_k_pos': 8.0,
     'cmp_v_pos': 2.831,
     'moe_b_grp': 3.454,
     'moe_b_rt': 6.01,
     'sgu_ln_b_2': 4.929,
     'mla_q_norm_g_2': 4.828,
     'mla_kv_norm_g_2': 3.101}
    for name, (base, spread) in spreads.items():
        noise = np.random.default_rng([zlib.crc32(name.encode()), seed]).standard_normal(out[name].shape)
        drawn = base * np.exp(spread * noise) if base else spread * noise
        out[name] = jnp.asarray(drawn.astype(out[name].dtype))
    for name, factor in factors.items():
        out[name] = (out[name] * factor).astype(out[name].dtype)
    return out
```

```python
import math
from contextlib import ExitStack

import concourse.bass as bass
import numpy as np
from concourse import mybir

F32 = mybir.dt.float32
F32R = mybir.dt.float32r
I32 = mybir.dt.int32
U32 = mybir.dt.uint32
ALU = mybir.AluOpType
ACT = mybir.ActivationFunctionType
AX = mybir.AxisListType

P = 128
T = 512
TT = T // P
D = 1024
KT = D // P
HALF = KT // 2
NEG = -1e30

GDN_H = 8
GDN_EPS = 1e-6
LN_EPS = 1e-5
ALPHA = 4 ** 0.25
LEVELS = 7

NSA_H = 16
NSA_G = 4
DH = 64
N_CMP = (T - 32) // 16 + 1

N_EXP = 16
HID = 256


class Stage:

    def __init__(self, nc, name):
        self.nc, self.name, self.sems, self.ctx = nc, name, [], ExitStack()

    def sem(self, name):
        s = self.nc.alloc_semaphore(f"{self.name}_{name}")
        self.sems.append(s)
        return s

    def sb(self, name, shape, dt=F32):
        return self.ctx.enter_context(self.nc.sbuf_tensor(f"{self.name}_{name}", shape, dt))

    def ps(self, name, banks):
        return self.ctx.enter_context(self.nc.psum_tensor(f"{self.name}_{name}", [P, banks, 512], F32))

    def __enter__(self):
        return self

    def __exit__(self, *e):
        if e[0] is None:
            self.nc.clear_and_free_semaphores(self.sems)
            self.nc.all_engine_barrier()
        self.ctx.close()
        return False


class Link:

    def __init__(self, eng, sem):
        self.eng, self.sem, self.n = eng, sem, 0

    def __call__(self, *instructions):
        for ins in instructions:
            ins.then_inc(self.sem, 1)
            self.n += 1
        self.eng.wait_ge(self.sem, self.n)


def rows_of(ap, start, n, repeat=P):
    return bass.AP(ap.tensor, ap.offset + start, [[0, repeat], [1, n]])


def over(eng, n, body):
    body(0)
    if n > 1:
        with eng.Fori(1, n) as i:
            body(i)


class WeightStream:

    def __init__(self, st, banks=4):
        self.f = [st.sb(f"wf{u}", [P, HALF, 512]) for u in range(2)]
        self.h = [st.sb(f"wh{u}", [P, HALF, 512], F32R) for u in range(2)]
        self.l = [st.sb(f"wl{u}", [P, HALF, 512], F32R) for u in range(2)]
        self.acc = st.ps("acc", banks)
        self.loaded = [st.sem(f"w_loaded{u}") for u in range(2)]
        self.hi_ready = st.sem("w_hi_ready")
        self.lo_ready = st.sem("w_lo_ready")
        self.unit0_used = st.sem("w_unit0_used")
        self.acc_ready = st.sem("acc_ready")
        self.evicted = st.sem("acc_evicted")

    def load(self, sp, b, src):
        for u in range(2):
            if not (isinstance(b, int) and b == 0):
                sp.wait_ge(self.lo_ready, 2 * (b - 1) + u + 1)
            for col, ap in src(u):
                sp.dma_start(self.f[u][:, :, col:col + ap.shape[2]], ap).then_inc(self.loaded[u], 16)

    def split_hi(self, act, b, parts=1, cols=512):
        for u in range(2):
            act.wait_ge(self.loaded[u], (b + 1) * (16 * parts))
            if not (isinstance(b, int) and b == 0):
                if u == 0:
                    act.wait_ge(self.unit0_used, b)
                else:
                    act.wait_ge(self.acc_ready, b * 4)
            act.activation(self.h[u][:, :, 0:cols], self.f[u][:, :, 0:cols], ACT.Copy).then_inc(self.hi_ready, 1)

    def split_lo(self, pool, b, cols=512):
        for u in range(2):
            pool.wait_ge(self.hi_ready, b * 2 + (u + 1))
            pool.tensor_tensor(self.l[u][:, :, 0:cols], self.f[u][:, :, 0:cols],
                               self.h[u][:, :, 0:cols].bitcast(F32),
                               ALU.subtract).then_inc(self.lo_ready, 1)

    def multiply(self, pe, b, xh, xl, weights_stationary, cols=512):
        for u in range(2):
            pe.wait_ge(self.lo_ready, b * 2 + (u + 1))
            for s in range(4):
                if u == 0 and not (isinstance(b, int) and b == 0):
                    pe.wait_ge(self.evicted, (b - 1) * 4 + (s + 1))
                for k in range(HALF):
                    for n, (w, x) in enumerate(((self.h, xh), (self.h, xl), (self.l, xh))):
                        wk, xk = w[u][:, k, :], x[:, HALF * u + k, :]
                        lhs, rhs = (wk, xk) if weights_stationary else (xk, wk[:, 0:cols])
                        mm = pe.matmul(self.acc[:, s, 0:cols], lhs[:, P * s:P * s + P], rhs,
                                       start=(u == 0 and k == 0 and n == 0),
                                       stop=(u == 1 and k == HALF - 1 and n == 2))
                if u == 1:
                    mm.then_inc(self.acc_ready, 1)
            if u == 0:
                mm.then_inc(self.unit0_used, 1)


def column_block(w, row0, col):
    def src(u):
        part = w[row0 + HALF * P * u:row0 + HALF * P * (u + 1), bass.ds(col, 512)]
        return [(0, part.rearrange("(k p) n -> p k n", p=P))]
    return src


def to_feature_major(g, st, src, pe_after, act_after=None):
    banks = st.ps("turn", 8)
    turned, hi_done, lo_done = st.sem("turned"), st.sem("turn_hi"), st.sem("turn_lo")

    def pe_part(pe):
        pe_after(pe)
        for k in range(KT):
            for t in range(TT):
                mm = pe.transpose(banks[:, k, P * t:P * t + P], src[:, t, P * k:P * k + P], g.ident[:])
            mm.then_inc(turned, 1)

    def act_part(act):
        for k in range(KT):
            act.wait_ge(turned, k + 1)
            act.activation(g.xh[:, k, :], banks[:, k, :], ACT.Copy).then_inc(hi_done, 1)

    def dve_part(dve):
        for k in range(KT):
            dve.wait_ge(hi_done, k + 1)
            dve.tensor_tensor(g.xl[:, k, :], banks[:, k, :], g.xh[:, k, :].bitcast(F32),
                              ALU.subtract).then_inc(lo_done, 1)
    return pe_part, act_part, dve_part


def stage_load(g, a):
    nc = g.nc
    with Stage(nc, "load") as st:
        ld = st.sem("loaded")
        turn = to_feature_major(g, st, g.h, lambda pe: pe.wait_ge(ld, 16 * 6))
        zero, zero_set, zero_stored = st.sb("zero", [P, D]), st.sem("zero_set"), st.sem("zero_stored")
        with nc.Block() as block:
            @block.sync
            def _(sp):
                sp.dma_start(g.h[:], a["x"][0].rearrange("(t p) d -> p t d", p=P)).then_inc(ld, 16)
                sp.dma_start(g.ident[:], a["c_ident"]).then_inc(ld, 16)
                sp.dma_start(g.ones[:], a["c_ones"]).then_inc(ld, 16)
                sp.dma_start(g.triu[:], a["c_triu"]).then_inc(ld, 16)
                sp.dma_start(g.neg_below[:], a["c_neg_below"]).then_inc(ld, 16)
                sp.dma_start(g.striu[:], a["c_striu"]).then_inc(ld, 16)
                sp.wait_ge(ld, 16 * 6)
                sp.wait_ge(zero_set, 1)
                for b in range(MAX_BLOCKS):
                    sp.dma_start(g.moe_rows[P * b:P * b + P, :], zero[:]).then_inc(zero_stored, 16)
                sp.wait_ge(zero_stored, 16 * MAX_BLOCKS)

            @block.gpsimd
            def _(pool):
                pool.memset(zero[:], 0.0).then_inc(zero_set, 1)

            @block.tensor
            def _(pe):
                turn[0](pe)

            @block.scalar
            def _(act):
                turn[1](act)

            @block.vector
            def _(dve):
                turn[2](dve)


def stage_gdn_project(g, a, qkvz, ab):
    nc = g.nc
    w_in = a["gdn_w_in"][0]
    with Stage(nc, "gproj") as st:
        ws = WeightStream(st)
        small = st.ps("small", 1)
        convw = st.sb("convw", [P, 24, 4])
        wab = st.sb("wab", [P, KT, 16])
        padded = [st.sb(f"padded{i}", [P, 3 + T]) for i in range(2)]
        mixed = [st.sb(f"mixed{i}", [P, T]) for i in range(2)]
        ld, zero = st.sem("small_loaded"), st.sem("pad_zeroed")
        conv_done, silu_done, step = st.sem("conv_done"), st.sem("silu_done"), st.sem("conv_step")
        in_pad, ab_ready, ab_done = st.sem("in_pad"), st.sem("ab_ready"), st.sem("ab_done")
        with nc.Block() as block:
            @block.sync
            def _(sp):
                for j in range(4):
                    sp.dma_start(convw[:, :, j], a["gdn_conv_w"][0][j].rearrange("(f p) -> p f", p=P),
                                 allow_slow_non_contiguous=True).then_inc(ld, 16)
                sp.dma_start(wab[:], w_in[:, 4096:4112].rearrange("(k p) n -> p k n", p=P)).then_inc(ld, 16)
                over(sp, 8, lambda b: ws.load(sp, b, column_block(w_in, 0, b * 512)))

            @block.tensor
            def _(pe):
                pe.wait_ge(ld, 16 * 5)
                for t in range(TT):
                    for k in range(KT):
                        for n, x in enumerate((g.xh, g.xl)):
                            mm = pe.matmul(small[:, 0, 16 * t:16 * t + 16],
                                           x[:, k, P * t:P * t + P].bitcast(F32), wab[:, k, :],
                                           start=(k == 0 and n == 0), stop=(k == KT - 1 and n == 1))
                mm.then_inc(ab_ready, 1)
                over(pe, 8, lambda b: ws.multiply(pe, b, g.xh, g.xl, True))

            @block.gpsimd
            def _(pool):
                for i in range(2):
                    pool.memset(padded[i][:, 0:3], 0.0).then_inc(zero, 1)
                over(pool, 8, lambda b: ws.split_lo(pool, b))

            @block.scalar
            def _(act):
                ws.split_hi(act, 0)

                def conv_block(b):
                    ws.split_hi(act, b + 1)
                    for s in range(4):
                        act.wait_ge(ws.acc_ready, b * 4 + (s + 1))
                        if not (isinstance(b, int) and b == 0 and s < 2):
                            act.wait_ge(conv_done, b * 4 + (s - 1))
                        act.activation(padded[s % 2][:, 3:3 + T], ws.acc[:, s, :],
                                       ACT.Copy).then_inc(ws.evicted, 1)
                        if s > 0:
                            act.wait_ge(conv_done, b * 4 + s)
                            act.activation(qkvz[:, bass.ds(b * 4 + (s - 1), 1), :].rearrange("p a n -> p (a n)"),
                                           mixed[(s - 1) % 2][:], ACT.Silu).then_inc(silu_done, 1)
                    act.wait_ge(conv_done, b * 4 + 4)
                    act.activation(qkvz[:, bass.ds(b * 4 + 3, 1), :].rearrange("p a n -> p (a n)"),
                                   mixed[1][:], ACT.Silu).then_inc(silu_done, 1)

                over(act, 6, conv_block)
                for b in (6, 7):
                    if b == 6:
                        ws.split_hi(act, 7)
                    for s in range(4):
                        act.wait_ge(ws.acc_ready, b * 4 + (s + 1))
                        act.activation(qkvz[:, b * 4 + s, :], ws.acc[:, s, :],
                                       ACT.Silu).then_inc(ws.evicted, 1)

            @block.vector
            def _(dve):
                dve.wait_ge(ab_ready, 1)
                dve.tensor_copy(ab[:].rearrange("p t n -> p (t n)"), small[:, 0, 0:64]).then_inc(ab_done, 1)
                dve.wait_ge(zero, 2)
                dve.wait_ge(ld, 16 * 5)

                def conv_block(b):
                    for s in range(4):
                        dve.wait_ge(ws.evicted, b * 4 + (s + 1))
                        if not (isinstance(b, int) and b == 0 and s < 2):
                            dve.wait_ge(silu_done, b * 4 + (s - 1))
                        x, y = padded[s % 2], mixed[s % 2]
                        w = convw[:, bass.ds(b * 4 + s, 1), :].rearrange("p a n -> p (a n)")
                        dve.tensor_scalar(y[:], x[:, 0:T], w[:, 0:1], None, ALU.mult).then_inc(step, 1)
                        for j in range(1, 4):
                            dve.wait_ge(step, b * 12 + (3 * s + j))
                            ins = dve.scalar_tensor_tensor(y[:], x[:, j:j + T], w[:, j:j + 1], y[:],
                                                           ALU.mult, ALU.add)
                            ins.then_inc(step if j < 3 else conv_done, 1)
                over(dve, 6, conv_block)


def stage_gdn_norm(g, a, qkvz):
    nc = g.nc
    n = 2 * GDN_H
    with Stage(nc, "gnorm") as st:
        sq = [st.sb(f"sq{i}", [P, T]) for i in range(2)]
        rows, spread = st.ps("rows", 1), st.ps("spread", 4)
        root, inv = st.sb("root", [n, T]), st.sb("inv", [n, T])
        squared, summed, rooted = st.sem("squared"), st.sem("summed"), st.sem("rooted")
        inverted, spread_done, used = st.sem("inverted"), st.sem("spread_done"), st.sem("spread_used")
        sel_loaded = st.sem("sel_loaded")
        with nc.Block() as block:
            @block.sync
            def _(sp):
                sp.dma_start(g.sel[:], a["c_sel"]).then_inc(sel_loaded, 16)

            @block.scalar
            def _(act):
                for r in range(n):
                    if r >= 2:
                        act.wait_ge(summed, r - 1)
                    act.activation(sq[r % 2][:], qkvz[:, r, :], ACT.Square).then_inc(squared, 1)
                act.wait_ge(summed, n)
                act.activation(root[:], rows[0:n, 0, :], ACT.Sqrt, bias=g.eps6[0:n, :]).then_inc(rooted, 1)

            @block.tensor
            def _(pe):
                for r in range(n):
                    pe.wait_ge(squared, r + 1)
                    pe.matmul(rows[0:n, 0, :], g.column(r, n), sq[r % 2][:],
                              start=(r == 0), stop=(r == n - 1)).then_inc(summed, 1)
                pe.wait_ge(inverted, 1)
                pe.wait_ge(sel_loaded, 16)
                for r in range(n):
                    if r >= 4:
                        pe.wait_ge(used, r - 3)
                    pe.matmul(spread[:, r % 4, :], g.row(r, n), inv[:],
                              start=True, stop=True).then_inc(spread_done, 1)

            @block.vector
            def _(dve):
                dve.wait_ge(rooted, 1)
                dve.reciprocal(inv[:], root[:]).then_inc(inverted, 1)
                for r in range(n):
                    dve.wait_ge(spread_done, r + 1)
                    dve.scalar_tensor_tensor(qkvz[:, r, :], qkvz[:, r, :],
                                             P ** -0.5 if r < GDN_H else 1.0, spread[:, r % 4, :],
                                             ALU.mult, ALU.mult).then_inc(used, 1)


def stage_gdn_gates(g, a, ab, gt):
    nc = g.nc
    n = TT * GDN_H
    with Stage(nc, "ggate") as st:
        bias, alog = st.sb("bias", [P, GDN_H]), st.sb("alog", [P, GDN_H])
        ea, a1, neg, ab_s, sp_ = (st.sb(x, [P, n]) for x in ("ea", "a1", "neg", "abs", "sp"))
        e1, e2 = st.sb("e1", [P, n]), st.sb("e2", [P, n])
        cum = st.ps("cum", 1)
        ld, link_a, link_v = st.sem("loaded"), st.sem("act_step"), st.sem("dve_step")
        v_abs, a_ln, a_ea, v_g = st.sem("v_abs"), st.sem("a_ln"), st.sem("a_ea"), st.sem("v_g")
        p_cum, v_cum, done = st.sem("p_cum"), st.sem("v_cum"), st.sem("done")
        a_in = ab[:, :, 0:GDN_H]
        b_in = ab[:, :, GDN_H:2 * GDN_H]
        def v3(t):
            return t[:].rearrange("p (t h) -> p t h", h=GDN_H)
        with nc.Block() as block:
            @block.sync
            def _(sp):
                sp.dma_start(bias[:], rows_of(a["gdn_dt_bias"], 0, GDN_H)).then_inc(ld, 16)
                sp.dma_start(alog[:], rows_of(a["gdn_a_log"], 0, GDN_H)).then_inc(ld, 16)

            @block.vector
            def _(dve):
                link = Link(dve, link_v)
                dve.wait_ge(ld, 32)
                link(dve.tensor_tensor(v3(a1), a_in, bias[:].unsqueeze(1).to_broadcast([P, TT, GDN_H]), ALU.add))
                link(dve.tensor_scalar(neg[:], a1[:], -1.0, None, ALU.mult))
                dve.tensor_tensor(ab_s[:], a1[:], neg[:], ALU.max).then_inc(v_abs, 1)
                dve.wait_ge(a_ln, 1)
                link(dve.scalar_tensor_tensor(sp_[:], a1[:], 0.0, e2[:], ALU.max, ALU.add))
                dve.wait_ge(a_ea, 2)
                dve.scalar_tensor_tensor(v3(gt["g"]), v3(sp_), -1.0,
                                         ea[:, 0:GDN_H].unsqueeze(1).to_broadcast([P, TT, GDN_H]),
                                         ALU.mult, ALU.mult).then_inc(v_g, 1)
                link(dve.tensor_scalar(e1[:], e1[:], 1.0, None, ALU.add))
                link(dve.reciprocal(gt["beta"][:], e1[:]))
                dve.wait_ge(p_cum, 1)
                link(dve.tensor_scalar(gt["neg_gc"][:], cum[:, 0, 0:n], -1.0, None, ALU.mult))
                dve.tensor_copy(gt["gl"][:], cum[:, 0, n:2 * n]).then_inc(v_cum, 1)
                dve.wait_ge(done, 2)
                link(dve.tensor_tensor(gt["beta_egc"][:], gt["beta"][:], gt["egc"][:], ALU.mult))
                dve.wait_ge(v_cum, 1)
                link(dve.tensor_tensor(gt["rest"][:], gt["gl"][:], gt["neg_gc"][:], ALU.add))
                dve.tensor_copy(gt["tmp"][:], gt["rest"][:]).then_inc(v_cum, 1)

            @block.scalar
            def _(act):
                act.wait_ge(ld, 32)
                act.activation(ea[:, 0:GDN_H], alog[:], ACT.Exp).then_inc(a_ea, 1)
                act.activation(v3(e1), b_in, ACT.Exp, scale=-1.0).then_inc(a_ea, 1)
                act.wait_ge(v_abs, 1)
                act.activation(e2[:], ab_s[:], ACT.Exp, scale=-1.0).then_inc(link_a, 1)
                act.wait_ge(link_a, 1)
                act.activation(e2[:], e2[:], ACT.Ln, bias=1.0).then_inc(a_ln, 1)
                act.wait_ge(v_cum, 1)
                act.activation(gt["egc"][:], gt["neg_gc"][:], ACT.Exp, scale=-1.0).then_inc(done, 1)
                act.activation(gt["dlast"][:], gt["gl"][:], ACT.Exp).then_inc(done, 1)
                act.wait_ge(v_cum, 2)
                act.activation(gt["krest"][:], gt["tmp"][:], ACT.Exp).then_inc(done, 1)

            @block.tensor
            def _(pe):
                pe.wait_ge(v_g, 1)
                pe.matmul(cum[:, 0, 0:n], g.triu[:], gt["g"][:], start=True, stop=True)
                pe.matmul(cum[:, 0, n:2 * n], g.ones[:], gt["g"][:], start=True, stop=True).then_inc(p_cum, 1)


def stage_gdn_chunks(g, a, qkvz, gt, qk_t, k_dec):
    nc = g.nc
    with Stage(nc, "gchunk") as st:
        levels = st.sb("levels", [P, LEVELS, P])
        NB = 2
        B = [{x: st.sb(f"{x}{i}", [P, TT, P]) for x in
              ("dec", "decb", "eg", "at", "m", "x", "tm", "um", "kbg", "vb")} for i in range(NB)]
        ps = [st.ps(f"ps{i}", 4) for i in range(NB)]
        ld = st.sem("loaded")
        pe_done = [st.sem(f"pe_done{i}") for i in range(NB)]
        act_done = [st.sem(f"act_done{i}") for i in range(NB)]
        dve_done = [st.sem(f"dve_done{i}") for i in range(NB)]
        L = LEVELS - 1
        N_PE, N_ACT, N_DVE = 6 + (3 * L - 1) + 1, 9 + L, 8 + (3 * L - 1) + 2
        def flat(ap):
            return ap.rearrange("p c n -> p (c n)")

        with nc.Block() as block:
            @block.sync
            def _(sp):
                sp.dma_start(levels[:], a["c_levels"].rearrange("l p n -> p l n")).then_inc(ld, 16)

            @block.tensor
            def _(pe):
                def bank(i, j, c):
                    return ps[i][:, j, P * c:P * c + P]

                def front(h, i, r):
                    q, k = qkvz[:, h, :], qkvz[:, GDN_H + h, :]
                    if r:
                        pe.wait_ge(dve_done[i], N_DVE * r)
                        pe.wait_ge(act_done[i], N_ACT * r)
                    for c in range(TT):
                        col = GDN_H * c + h
                        mm = pe.matmul(bank(i, 0, c), gt["g"][:, col:col + 1].to_broadcast([P, P]), g.triu[:],
                                       start=True, stop=True)
                    mm.then_inc(pe_done[i], 1)
                    for c in range(TT):
                        col = GDN_H * c + h
                        mm = pe.matmul(bank(i, 1, c), gt["beta"][:, col:col + 1].to_broadcast([P, P]), g.ident[:],
                                       start=True, stop=True)
                    mm.then_inc(pe_done[i], 1)
                    for c in range(TT):
                        kc = k[:, P * c:P * c + P]
                        mm = pe.matmul(bank(i, 2, c), kc, kc, start=True, stop=True)
                    mm.then_inc(pe_done[i], 1)
                    for c in range(TT):
                        mm = pe.matmul(bank(i, 3, c), k[:, P * c:P * c + P], q[:, P * c:P * c + P],
                                       start=True, stop=True)
                    mm.then_inc(pe_done[i], 1)

                def first_level(h, i, r):
                    b = B[i]
                    pe.wait_ge(dve_done[i], N_DVE * r + 7)
                    for c in range(TT):
                        mm = pe.matmul(bank(i, 0, c), b["m"][:, c, :], g.ident[:], start=True, stop=True)
                    mm.then_inc(pe_done[i], 1)
                    pe.wait_ge(act_done[i], N_ACT * r + 5)
                    for c in range(TT):
                        pe.transpose(bank(i, 1, c), qkvz[:, GDN_H + h, P * c:P * c + P], g.ident[:])
                    for c in range(TT):
                        mm = pe.transpose(bank(i, 2, c), qkvz[:, 2 * GDN_H + h, P * c:P * c + P], g.ident[:])
                    mm.then_inc(pe_done[i], 1)

                def level(h, i, r, lv):
                    b = B[i]
                    base_d = N_DVE * r + 8 + 3 * (lv - 1)
                    base_p = N_PE * r + 6
                    pe.wait_ge(dve_done[i], base_d + 1)
                    for c in range(TT):
                        mm = pe.matmul(bank(i, 3, c), b["m"][:, c, :], b["tm"][:, c, :], start=True, stop=True)
                    mm.then_inc(pe_done[i], 1)
                    pe.wait_ge(act_done[i], N_ACT * r + 9 + lv)
                    for c in range(TT):
                        mm = pe.matmul(bank(i, 0, c), b["x"][:, c, :], b["um"][:, c, :], start=True, stop=True)
                    mm.then_inc(pe_done[i], 1)
                    if lv < L:
                        for c in range(TT):
                            mm = pe.matmul(bank(i, 3, c), b["um"][:, c, :], b["x"][:, c, :], start=True, stop=True)
                        mm.then_inc(pe_done[i], 1)

                def back(h, i, r):
                    b = B[i]
                    pe.wait_ge(dve_done[i], N_DVE * r + 8 + 3 * L - 1)
                    for c in range(TT):
                        pe.matmul(bank(i, 1, c), b["um"][:, c, :], b["vb"][:, c, :], start=True, stop=True)
                    for c in range(TT):
                        mm = pe.matmul(bank(i, 2, c), b["kbg"][:, c, :], b["um"][:, c, :], start=True, stop=True)
                    mm.then_inc(pe_done[i], 1)

                for r in range(GDN_H // NB):
                    for i in range(NB):
                        front(NB * r + i, i, r)
                    for i in range(NB):
                        first_level(NB * r + i, i, r)
                    for lv in range(1, L + 1):
                        for i in range(NB):
                            level(NB * r + i, i, r, lv)
                    for i in range(NB):
                        back(NB * r + i, i, r)

            @block.scalar
            def _(act):
                def front(h, i, r):
                    b = B[i]
                    act.wait_ge(pe_done[i], N_PE * r + 1)
                    act.wait_ge(dve_done[i], N_DVE * r + 1)
                    act.activation(flat(b["eg"][:]), ps[i][:, 0, :], ACT.Exp).then_inc(act_done[i], 1)
                    for c in range(TT):
                        col = GDN_H * c + h
                        act.activation(b["dec"][:, c, :], b["dec"][:, c, :], ACT.Exp,
                                       bias=gt["neg_gc"][:, col:col + 1]).then_inc(act_done[i], 1)

                def turned(h, i, r):
                    b = B[i]
                    act.wait_ge(pe_done[i], N_PE * r + 6)
                    for c in range(TT):
                        col = GDN_H * c + h
                        act.activation(b["kbg"][:, c, :], ps[i][:, 1, P * c:P * c + P], ACT.Copy,
                                       scale=gt["beta_egc"][:, col:col + 1]).then_inc(act_done[i], 1)

                def level(h, i, r, lv):
                    b = B[i]
                    act.wait_ge(pe_done[i], N_PE * r + 7 + 3 * (lv - 1))
                    act.activation(flat(b["x"][:]), ps[i][:, 3, :], ACT.Copy).then_inc(act_done[i], 1)

                for r in range(GDN_H // NB):
                    for i in range(NB):
                        front(NB * r + i, i, r)
                    for i in range(NB):
                        turned(NB * r + i, i, r)
                    for lv in range(1, L + 1):
                        for i in range(NB):
                            level(NB * r + i, i, r, lv)

            @block.vector
            def _(dve):
                dve.wait_ge(ld, 16)

                def masked(t, lv):
                    return levels[:, lv:lv + 1, :].to_broadcast([P, TT, P])

                def wide(ap):
                    return ap.rearrange("p (c n) -> p c n", c=TT)

                def front(h, i, r):
                    b = B[i]
                    q = qkvz[:, h, :]
                    dve.wait_ge(pe_done[i], N_PE * r + 1)
                    dve.tensor_tensor(b["dec"][:], wide(ps[i][:, 0, :]),
                                      g.neg_below[:].unsqueeze(1).to_broadcast([P, TT, P]),
                                      ALU.add).then_inc(dve_done[i], 1)
                    dve.wait_ge(act_done[i], N_ACT * r + 5)
                    dve.wait_ge(pe_done[i], N_PE * r + 4)
                    dve.tensor_tensor(q, q, flat(b["eg"][:]), ALU.mult).then_inc(dve_done[i], 1)
                    dve.tensor_tensor(flat(b["decb"][:]), flat(b["dec"][:]), ps[i][:, 1, :],
                                      ALU.mult).then_inc(dve_done[i], 1)
                    dve.tensor_tensor(qk_t[:, h, :], flat(b["dec"][:]), ps[i][:, 3, :],
                                      ALU.mult).then_inc(dve_done[i], 1)
                    dve.wait_ge(dve_done[i], N_DVE * r + 3)
                    dve.tensor_tensor(flat(b["at"][:]), flat(b["decb"][:]), ps[i][:, 2, :],
                                      ALU.mult).then_inc(dve_done[i], 1)
                    dve.wait_ge(dve_done[i], N_DVE * r + 5)
                    dve.tensor_tensor(b["m"][:], b["at"][:], masked(b, 0), ALU.mult).then_inc(dve_done[i], 1)
                    dve.wait_ge(dve_done[i], N_DVE * r + 6)
                    dve.tensor_tensor(b["um"][:], g.ident[:].unsqueeze(1).to_broadcast([P, TT, P]), b["m"][:],
                                      ALU.subtract).then_inc(dve_done[i], 1)

                def first_level(h, i, r):
                    b = B[i]
                    dve.wait_ge(pe_done[i], N_PE * r + 5)
                    dve.tensor_tensor(b["tm"][:], g.ident[:].unsqueeze(1).to_broadcast([P, TT, P]),
                                      wide(ps[i][:, 0, :]), ALU.subtract).then_inc(dve_done[i], 1)

                def turned(h, i, r):
                    b = B[i]
                    dve.wait_ge(act_done[i], N_ACT * r + 9)
                    for c in range(TT):
                        col = GDN_H * c + h
                        dve.tensor_scalar(k_dec[:, h, P * c:P * c + P], ps[i][:, 1, P * c:P * c + P],
                                          gt["krest"][:, col:col + 1], None, ALU.mult)
                        dve.tensor_scalar(b["vb"][:, c, :], ps[i][:, 2, P * c:P * c + P],
                                          gt["beta"][:, col:col + 1], None, ALU.mult)

                def level(h, i, r, lv):
                    b = B[i]
                    base_d = N_DVE * r + 8 + 3 * (lv - 1)
                    base_p = N_PE * r + 6 + 3 * (lv - 1)
                    dve.tensor_tensor(b["m"][:], b["at"][:], masked(b, lv), ALU.mult).then_inc(dve_done[i], 1)
                    dve.wait_ge(pe_done[i], base_p + (3 if lv < L else 2))
                    dve.wait_ge(dve_done[i], base_d + 1)
                    dve.tensor_tensor(flat(b["um"][:]), flat(b["um"][:]), ps[i][:, 0, :],
                                      ALU.subtract).then_inc(dve_done[i], 1)
                    if lv < L:
                        dve.tensor_tensor(flat(b["tm"][:]), flat(b["tm"][:]), ps[i][:, 3, :],
                                          ALU.subtract).then_inc(dve_done[i], 1)

                def back(h, i, r):
                    dve.wait_ge(pe_done[i], N_PE * (r + 1))
                    dve.tensor_copy(qkvz[:, 2 * GDN_H + h, :], ps[i][:, 1, :]).then_inc(dve_done[i], 1)
                    dve.tensor_copy(qkvz[:, GDN_H + h, :], ps[i][:, 2, :]).then_inc(dve_done[i], 1)

                for r in range(GDN_H // NB):
                    for i in range(NB):
                        front(NB * r + i, i, r)
                    for i in range(NB):
                        first_level(NB * r + i, i, r)
                    for i in range(NB):
                        turned(NB * r + i, i, r)
                    for lv in range(1, L + 1):
                        for i in range(NB):
                            level(NB * r + i, i, r, lv)
                    for i in range(NB):
                        back(NB * r + i, i, r)


def stage_gdn_scan(g, a, qkvz, gt, qk_t, k_dec):
    nc = g.nc
    with Stage(nc, "gscan") as st:
        state = st.sb("state", [P, GDN_H, P])
        v_new = st.sb("v_new", [P, GDN_H, P])
        ps_p, ps_o, ps_s = st.ps("p", 2), st.ps("o", 2), st.ps("s", 2)
        zeroed, p_done, v_done = st.sem("zeroed"), st.sem("p_done"), st.sem("v_done")
        o_done, s_done, o_out, s_out = st.sem("o_done"), st.sem("s_done"), st.sem("o_out"), st.sem("s_out")

        def blk(t, h, c):
            return t[:, h, P * c:P * c + P]

        def bank(ps, h):
            return ps[:, h // 4, P * (h % 4):P * (h % 4) + P]

        with nc.Block() as block:
            @block.gpsimd
            def _(pool):
                pool.memset(state[:], 0.0).then_inc(zeroed, 1)

            @block.tensor
            def _(pe):
                pe.wait_ge(zeroed, 1)
                for c in range(TT):
                    for half in range(2):
                        hs = range(4 * half, 4 * half + 4)
                        if c:
                            pe.wait_ge(s_out, 8 * (c - 1) + 4 * half + 4)
                            pe.wait_ge(v_done, 2 * (c - 1) + half + 1)
                        for h in hs:
                            mm = pe.matmul(bank(ps_p, h), blk(qkvz, GDN_H + h, c), state[:, h, :],
                                           start=True, stop=True)
                        mm.then_inc(p_done, 1)
                    for half in range(2):
                        hs = range(4 * half, 4 * half + 4)
                        pe.wait_ge(v_done, 2 * c + half + 1)
                        for h in hs:
                            mm = pe.matmul(bank(ps_s, h), blk(k_dec, h, c), v_new[:, h, :],
                                           start=True, stop=True)
                        mm.then_inc(s_done, 1)
                        if c:
                            pe.wait_ge(o_out, 2 * (c - 1) + half + 1)
                        for h in hs:
                            pe.matmul(bank(ps_o, h), state[:, h, :], blk(qkvz, h, c), start=True, stop=False)
                            mm = pe.matmul(bank(ps_o, h), v_new[:, h, :], blk(qk_t, h, c),
                                           start=False, stop=True)
                        mm.then_inc(o_done, 1)

            @block.vector
            def _(dve):
                for c in range(TT):
                    for half in range(2):
                        h0 = 4 * half
                        dve.wait_ge(p_done, 2 * c + half + 1)
                        if c:
                            dve.wait_ge(o_done, 2 * (c - 1) + half + 1)
                        dve.tensor_tensor(v_new[:, h0:h0 + 4, :],
                                          qkvz[:, 2 * GDN_H + h0:2 * GDN_H + h0 + 4, P * c:P * c + P],
                                          ps_p[:, half, :].rearrange("p (h n) -> p h n", h=4),
                                          ALU.subtract).then_inc(v_done, 1)
                    for half in range(2):
                        dve.wait_ge(s_done, 2 * c + half + 1)
                        dve.wait_ge(o_done, 2 * c + half + 1)
                        for h in range(4 * half, 4 * half + 4):
                            col = GDN_H * c + h
                            dve.scalar_tensor_tensor(state[:, h, :], state[:, h, :], gt["dlast"][:, col:col + 1],
                                                     bank(ps_s, h), ALU.mult, ALU.add).then_inc(s_out, 1)

            @block.scalar
            def _(act):
                for c in range(TT):
                    for half in range(2):
                        h0 = 4 * half
                        act.wait_ge(o_done, 2 * c + half + 1)
                        act.activation(qkvz[:, h0:h0 + 4, P * c:P * c + P],
                                       ps_o[:, half, :].rearrange("p (h n) -> p h n", h=4),
                                       ACT.Copy).then_inc(o_out, 1)


def stage_gdn_out(g, a, qkvz):
    nc = g.nc
    n = GDN_H
    with Stage(nc, "gout") as st:
        sq = [st.sb(f"sq{i}", [P, T]) for i in range(2)]
        y = [st.sb(f"y{i}", [P, T]) for i in range(2)]
        nw = st.sb("nw", [P, 1])
        rows, spread = st.ps("rows", 1), st.ps("spread", 4)
        root, inv = st.sb("root", [n, T]), st.sb("inv", [n, T])
        ld, squared, summed, rooted = st.sem("loaded"), st.sem("squared"), st.sem("summed"), st.sem("rooted")
        inverted, spread_done, used = st.sem("inverted"), st.sem("spread_done"), st.sem("spread_used")
        y_done, hi_done, lo_done = st.sem("y_done"), st.sem("hi_done"), st.sem("lo_done")
        with nc.Block() as block:
            @block.sync
            def _(sp):
                sp.dma_start(nw[:], a["gdn_norm_w"].rearrange("a p -> p a"),
                             allow_slow_non_contiguous=True).then_inc(ld, 16)

            @block.scalar
            def _(act):
                for r in range(n):
                    if r >= 2:
                        act.wait_ge(summed, r - 1)
                    act.activation(sq[r % 2][:], qkvz[:, r, :], ACT.Square).then_inc(squared, 1)
                act.wait_ge(summed, n)
                act.activation(root[:], rows[0:n, 0, :], ACT.Sqrt, scale=1.0 / P,
                               bias=g.eps6[0:n, :]).then_inc(rooted, 1)
                for r in range(n):
                    act.wait_ge(y_done, r + 1)
                    act.activation(g.xh[:, r, :], y[r % 2][:], ACT.Copy).then_inc(hi_done, 1)

            @block.tensor
            def _(pe):
                for r in range(n):
                    pe.wait_ge(squared, r + 1)
                    pe.matmul(rows[0:n, 0, :], g.column(r, n), sq[r % 2][:],
                              start=(r == 0), stop=(r == n - 1)).then_inc(summed, 1)
                pe.wait_ge(inverted, 1)
                for r in range(n):
                    if r >= 4:
                        pe.wait_ge(used, r - 3)
                    pe.matmul(spread[:, r % 4, :], g.row(r, n), inv[:],
                              start=True, stop=True).then_inc(spread_done, 1)

            @block.vector
            def _(dve):
                dve.wait_ge(rooted, 1)
                dve.wait_ge(ld, 16)
                dve.reciprocal(inv[:], root[:]).then_inc(inverted, 1)
                for r in range(n):
                    dve.wait_ge(spread_done, r + 1)
                    if r >= 2:
                        dve.wait_ge(hi_done, r - 1)
                        dve.wait_ge(lo_done, r - 1)
                    dve.scalar_tensor_tensor(y[r % 2][:], qkvz[:, r, :], nw[:, 0:1], spread[:, r % 4, :],
                                             ALU.mult, ALU.mult).then_inc(used, 1)
                    dve.wait_ge(used, r + 1)
                    dve.tensor_tensor(y[r % 2][:], y[r % 2][:], qkvz[:, 3 * GDN_H + r, :],
                                      ALU.mult).then_inc(y_done, 1)

            @block.gpsimd
            def _(pool):
                for r in range(n):
                    pool.wait_ge(hi_done, r + 1)
                    pool.tensor_tensor(g.xl[:, r, :], y[r % 2][:], g.xh[:, r, :].bitcast(F32),
                                       ALU.subtract).then_inc(lo_done, 1)


def stage_out_proj(g, name, w, alpha):
    nc = g.nc
    with Stage(nc, name) as st:
        ws = WeightStream(st)
        with nc.Block() as block:
            @block.sync
            def _(sp):
                over(sp, 2, lambda b: ws.load(sp, b, column_block(w, 0, b * 512)))

            @block.tensor
            def _(pe):
                over(pe, 2, lambda b: ws.multiply(pe, b, g.xh, g.xl, False))

            @block.gpsimd
            def _(pool):
                over(pool, 2, lambda b: ws.split_lo(pool, b))

            @block.scalar
            def _(act):
                over(act, 2, lambda b: ws.split_hi(act, b))

            @block.vector
            def _(dve):
                def body(b):
                    for t in range(TT):
                        dve.wait_ge(ws.acc_ready, b * 4 + (t + 1))
                        h = g.h[:, t, bass.ds(b * 512, 512)]
                        dve.scalar_tensor_tensor(h, h, alpha, ws.acc[:, t, :],
                                                 ALU.mult, ALU.add).then_inc(ws.evicted, 1)
                over(dve, 2, body)


def stage_norm(g, name, src, dst, gain, shift, eps, center):
    nc = g.nc
    with Stage(nc, name) as st:
        gb = st.sb("gain", [P, D])
        bb = st.sb("shift", [P, D]) if shift else None
        stats, mv = st.sb("stats", [P, TT, 2, 6]), st.sb("mv", [P, TT, 2])
        sq = st.sb("sq", [P, D]) if not center else None
        root, inv = st.sb("root", [P, TT]), st.sb("inv", [P, TT])
        ld, stat, agg, rooted, inverted = (st.sem(x) for x in ("loaded", "stat", "agg", "rooted", "inverted"))
        scaled, gained, done = st.sem("scaled"), st.sem("gained"), st.sem("done")
        n_ld = 32 if shift else 16
        turn = to_feature_major(g, st, dst, lambda pe: pe.wait_ge(done, TT))
        with nc.Block() as block:
            @block.sync
            def _(sp):
                sp.dma_start(gb[:], rows_of(*gain, D)).then_inc(ld, 16)
                if shift:
                    sp.dma_start(bb[:], rows_of(*shift, D)).then_inc(ld, 16)

            @block.vector
            def _(dve):
                if center:
                    for t in range(TT):
                        for i in range(2):
                            dve.bn_stats(stats[:, t, i, :], src[:, t, 512 * i:512 * i + 512]).then_inc(stat, 1)
                        dve.wait_ge(stat, 2 * t + 2)
                        dve.bn_aggr(mv[:, t, :], stats[:, t, :, :].rearrange("p a b -> p (a b)")).then_inc(agg, 1)
                dve.wait_ge(rooted, 1)
                dve.reciprocal(inv[:], root[:]).then_inc(inverted, 1)
                dve.wait_ge(inverted, 1)
                dve.wait_ge(ld, n_ld)
                for t in range(TT):
                    if center:
                        dve.tensor_scalar(dst[:, t, :], src[:, t, :], mv[:, t, 0:1], inv[:, t:t + 1],
                                          ALU.subtract, ALU.mult).then_inc(scaled, 1)
                        dve.wait_ge(scaled, t + 1)
                        dve.tensor_tensor(dst[:, t, :], dst[:, t, :], gb[:], ALU.mult).then_inc(gained, 1)
                    else:
                        dve.scalar_tensor_tensor(dst[:, t, :], src[:, t, :], inv[:, t:t + 1], gb[:],
                                                 ALU.mult, ALU.mult).then_inc(done, 1)
                turn[2](dve)

            @block.scalar
            def _(act):
                if center:
                    act.wait_ge(agg, TT)
                    act.activation(root[:], mv[:, :, 1], ACT.Sqrt,
                                   bias=(g.eps5 if eps == LN_EPS else g.eps6)[:]).then_inc(rooted, 1)
                else:
                    for t in range(TT):
                        act.activation(sq[:], src[:, t, :], ACT.Square,
                                       accum_out=mv[:, t, 1:2]).then_inc(agg, 1)
                        act.wait_ge(agg, t + 1)
                    act.activation(root[:], mv[:, :, 1], ACT.Sqrt, scale=1.0 / D, bias=g.eps6[:]).then_inc(rooted, 1)
                turn[1](act)

            @block.gpsimd
            def _(pool):
                if center:
                    for t in range(TT):
                        pool.wait_ge(gained, t + 1)
                        pool.tensor_tensor(dst[:, t, :], dst[:, t, :], bb[:], ALU.add).then_inc(done, 1)

            @block.tensor
            def _(pe):
                turn[0](pe)


MAX_BLOCKS = 2 * T // P + N_EXP - 1


def stage_route(g, name, a, layer, rt):
    nc = g.nc
    G, E = 4, 4
    with Stage(nc, name) as st:
        wr = st.sb("wr", [P, KT, G + N_EXP])
        br = st.sb("br", [P, G + N_EXP])
        desc, iota_b = st.sb("desc", [P, G]), st.sb("iota_b", [1, MAX_BLOCKS, N_EXP])
        lg = st.sb("lg", [P, TT, G + N_EXP])
        def small(n, *shape):
            return st.sb(n, [P, TT, *shape])
        mx, nmx, s1, pr, eq, tie, tm = (small(x, k) for x, k in
                                        (("mx", 1), ("nmx", 1), ("s1", 1), ("pr", 4), ("eq", 4), ("tie", 4), ("tm", 1)))
        gp, ohg, el, t16 = small("gp", 1), small("ohg", 4), small("el", 4), small("t16", G, E)
        m1, m2, oh1, oh2, p2 = small("m1", 1), small("m2", 1), small("oh1", 4), small("oh2", 4), small("p2", 4)
        f1, f2, oh = small("f1", G, E), small("f2", G, E), small("oh", N_EXP)
        pre, tot, cnt, cmp = small("pre", N_EXP), small("tot", N_EXP), st.sb("cnt", [P, N_EXP]), st.sb("cmp", [P, N_EXP])
        blocks, incl, base = st.sb("blocks", [P, N_EXP]), st.sb("incl", [P, N_EXP]), st.sb("base", [P, N_EXP])
        one16 = st.sb("one16", [P, N_EXP])
        le, tabf = st.sb("le", [1, MAX_BLOCKS, N_EXP]), st.sb("tabf", [1, 24])
        ps = st.ps("ps", 3)
        ld, step, p_lg, v_max, a_exp, v_oh, p_cnt = (st.sem(x) for x in
            ("loaded", "step", "p_logits", "v_max", "a_exp", "v_onehot", "p_count"))
        h_split, x_free = st.sem("h_split"), st.sem("x_free")

        with nc.Block() as block:
            @block.sync
            def _(sp):
                sp.dma_start(wr[:, :, 0:G], a["moe_w_grp"][layer].rearrange("(k p) n -> p k n", p=P)).then_inc(ld, 16)
                sp.dma_start(wr[:, :, G:], a["moe_w_rt"][layer].rearrange("(k p) n -> p k n", p=P)).then_inc(ld, 16)
                sp.dma_start(br[:, 0:G], rows_of(a["moe_b_grp"], layer * G, G)).then_inc(ld, 16)
                sp.dma_start(br[:, G:], rows_of(a["moe_b_rt"], layer * N_EXP, N_EXP)).then_inc(ld, 16)
                sp.dma_start(desc[:], rows_of(a["c_desc"], 0, G)).then_inc(ld, 16)
                sp.dma_start(iota_b[:], a["c_iota_b"]).then_inc(ld, 16)

            @block.tensor
            def _(pe):
                pe.wait_ge(ld, 16 * 6)
                for t in range(TT):
                    for k in range(KT):
                        for n, x in enumerate((g.xh, g.xl)):
                            mm = pe.matmul(ps[:, 0, 20 * t:20 * t + 20], x[:, k, P * t:P * t + P].bitcast(F32),
                                           wr[:, k, :], start=(k == 0 and n == 0), stop=(k == KT - 1 and n == 1))
                mm.then_inc(p_lg, 1)
                pe.wait_ge(v_oh, 1)
                flat = oh[:].rearrange("p t e -> p (t e)")
                pe.matmul(ps[:, 1, 0:64], g.striu[:], flat, start=True, stop=True)
                pe.matmul(ps[:, 2, 0:64], g.ones[:], flat, start=True, stop=True).then_inc(p_cnt, 1)

            @block.scalar
            def _(act):
                act.wait_ge(v_max, 1)
                act.activation(pr[:], pr[:], ACT.Exp).then_inc(a_exp, 1)
                act.wait_ge(v_max, 2)
                act.activation(pr[:], pr[:], ACT.Exp).then_inc(a_exp, 1)
                act.wait_ge(p_lg, 1)
                for t in range(TT):
                    act.activation(rt.hh[:, t, :], g.h[:, t, :], ACT.Copy).then_inc(h_split, 1)

            @block.gpsimd
            def _(pool):
                for t in range(TT):
                    pool.wait_ge(h_split, t + 1)
                    pool.tensor_tensor(rt.hl[:, t, :], g.h[:, t, :], rt.hh[:, t, :].bitcast(F32),
                                       ALU.subtract).then_inc(x_free, 1)

            @block.vector
            def _(dve):
                link = Link(dve, step)
                b4 = lambda t: t[:].to_broadcast([P, TT, 4])

                def first_of(onehot, p, m):
                    link(dve.tensor_tensor(eq[:], p[:], b4(m), ALU.is_equal))
                    link(dve.tensor_tensor(tie[:], eq[:], desc[:].unsqueeze(1).to_broadcast([P, TT, 4]), ALU.mult))
                    link(dve.tensor_reduce(tm[:], tie[:], AX.X, ALU.max))
                    link(dve.tensor_tensor(onehot[:], tie[:], b4(tm), ALU.is_equal))

                def softmax(src, n):
                    link(dve.tensor_reduce(mx[:], src, AX.X, ALU.max))
                    dve.tensor_tensor(pr[:], src, b4(mx), ALU.subtract).then_inc(v_max, 1)
                    dve.wait_ge(a_exp, n)
                    link(dve.tensor_reduce(s1[:], pr[:], AX.X, ALU.add))
                    link(dve.reciprocal(s1[:], s1[:]))
                    link(dve.tensor_tensor(pr[:], pr[:], b4(s1), ALU.mult))

                dve.wait_ge(ld, 16 * 6)
                dve.wait_ge(p_lg, 1)
                link(dve.tensor_tensor(lg[:], ps[:, 0, 0:80].rearrange("p (t n) -> p t n", t=TT),
                                       br[:].unsqueeze(1).to_broadcast([P, TT, 20]), ALU.add))
                softmax(lg[:, :, 0:G], 1)
                link(dve.tensor_reduce(gp[:], pr[:], AX.X, ALU.max))
                first_of(ohg, pr, gp)
                link(dve.tensor_tensor(t16[:], lg[:, :, G:].rearrange("p t (g e) -> p t g e", g=G),
                                       ohg[:].unsqueeze(3).to_broadcast([P, TT, G, E]), ALU.mult))
                link(dve.tensor_reduce(el[:], t16[:].rearrange("p t g e -> p t e g"), AX.X, ALU.add))
                softmax(el[:], 2)
                link(dve.tensor_reduce(m1[:], pr[:], AX.X, ALU.max))
                first_of(oh1, pr, m1)
                link(dve.scalar_tensor_tensor(p2[:], oh1[:], -2.0, pr[:], ALU.mult, ALU.add))
                link(dve.tensor_reduce(m2[:], p2[:], AX.X, ALU.max))
                first_of(oh2, p2, m2)
                link(dve.tensor_tensor(s1[:], m1[:], m2[:], ALU.add))
                link(dve.reciprocal(s1[:], s1[:]))
                link(dve.tensor_tensor(s1[:], s1[:], gp[:], ALU.mult))
                link(dve.tensor_tensor(rt.weight[:, :, 0:1], m1[:], s1[:], ALU.mult))
                link(dve.tensor_tensor(rt.weight[:, :, 1:2], m2[:], s1[:], ALU.mult))
                for f, o in ((f1, oh1), (f2, oh2)):
                    for t in range(TT):
                        link(dve.tensor_tensor(f[:, t], ohg[:, t].unsqueeze(2).to_broadcast([P, G, E]),
                                               o[:, t].unsqueeze(1).to_broadcast([P, G, E]), ALU.mult))
                flat = lambda t: t[:].rearrange("p t g e -> p t (g e)")
                dve.tensor_tensor(oh[:], flat(f1), flat(f2), ALU.add).then_inc(v_oh, 1)
                dve.memset(one16[:], 1.0)
                dve.wait_ge(p_cnt, 1)
                link(dve.tensor_copy(pre[:], ps[:, 1, 0:64].rearrange("p (t e) -> p t e", t=TT)))
                link(dve.tensor_copy(tot[:], ps[:, 2, 0:64].rearrange("p (t e) -> p t e", t=TT)))
                link(dve.tensor_copy(cnt[:], tot[:, 0, :]))
                for t in range(1, TT):
                    link(dve.tensor_tensor(pre[:, t, :], pre[:, t, :], cnt[:], ALU.add))
                    link(dve.tensor_tensor(cnt[:], cnt[:], tot[:, t, :], ALU.add))
                link(dve.tensor_scalar(blocks[:], cnt[:], 0.5, None, ALU.is_gt))
                for j in range(1, TT):
                    link(dve.tensor_scalar(cmp[:], cnt[:], P * j + 0.5, None, ALU.is_gt))
                    link(dve.tensor_tensor(blocks[:], blocks[:], cmp[:], ALU.add))
                link(dve.tensor_tensor_scan(incl[:], one16[:], blocks[:], 0.0, ALU.mult, ALU.add))
                link(dve.tensor_tensor(base[:], incl[:], blocks[:], ALU.subtract))
                link(dve.tensor_scalar(base[:], base[:], float(P), None, ALU.mult))
                link(dve.tensor_tensor(pre[:], pre[:], base[:].unsqueeze(1).to_broadcast([P, TT, N_EXP]), ALU.add))
                for n, f in enumerate((f1, f2)):
                    link(dve.tensor_tensor(flat(f), flat(f), pre[:], ALU.mult))
                    link(dve.tensor_reduce(rt.slot[:, :, n:n + 1], flat(f), AX.X, ALU.add))
                link(dve.tensor_copy(rt.slot_i[:], rt.slot[:]))
                link(dve.tensor_tensor(le[:], incl[0:1, :].unsqueeze(1).to_broadcast([1, MAX_BLOCKS, N_EXP]),
                                       iota_b[:], ALU.is_le))
                link(dve.tensor_reduce(tabf[:, 0:MAX_BLOCKS], le[:], AX.X, ALU.add))
                link(dve.tensor_scalar(tabf[:, MAX_BLOCKS:24], incl[0:1, N_EXP - 1:N_EXP], -1.0, None, ALU.add))
                link(dve.tensor_copy(rt.table[:], tabf[:]))


def stage_experts(g, name, a, layer, rt):
    nc = g.nc
    wg, wu, wd = a["moe_w_gate"][layer], a["moe_w_up"][layer], a["moe_w_down"][layer]
    rows = g.moe_rows
    with Stage(nc, name) as st:
        wf = [st.sb(f"wf{u}", [P, HALF, 512]) for u in range(3)]
        wh = [st.sb(f"wh{u}", [P, HALF, 512], F32R) for u in range(3)]
        wl = [st.sb(f"wl{u}", [P, HALF, 512], F32R) for u in range(3)]
        pick, eq0 = st.sb("pick", [P, TT, P], F32R), st.sb("eq0", [P, TT, P])
        xh, xl = st.sb("xh", [P, KT, P], F32R), st.sb("xl", [P, KT, P], F32R)
        act_g, hid = st.sb("act_g", [P, HID]), st.sb("hid", [P, HID])
        hth, htl = st.sb("hth", [P, 2, P], F32R), st.sb("htl", [P, 2, P], F32R)
        y = st.sb("y", [P, D])
        slot = st.sb("slot", [P, TT, 2])
        iota = st.sb("iota", [P, P])
        ps_xh, ps_xl, ps_gu, ps_t, ps_y = st.ps("ps_xh", 2), st.ps("ps_xl", 2), st.ps("ps_gu", 1), st.ps("ps_t", 1), st.ps("ps_y", 2)
        ld = st.sem("loaded")
        w_loaded = [st.sem(f"w_loaded{u}") for u in range(3)]
        w_hi, w_lo = [st.sem(f"w_hi{u}") for u in range(3)], [st.sem(f"w_lo{u}") for u in range(3)]
        unit0_used, gu_done, xh_done, xl_done = st.sem("unit0_used"), st.sem("gu_done"), st.sem("xh_done"), st.sem("xl_done")
        picked, eq_done, slot_done = st.sem("picked"), st.sem("eq_done"), st.sem("slot_done")
        xh_out, xl_out, silu_done, hid_done = st.sem("xh_out"), st.sem("xl_out"), st.sem("silu_done"), st.sem("hid_done")
        t_done, th_out, tl_out, y_done, y_out, y_stored = (st.sem(x) for x in
            ("t_done", "th_out", "tl_out", "y_done", "y_out", "y_stored"))
        back, scaled, added = st.sem("back"), st.sem("scaled"), st.sem("added")
        yg = [wf[0], wf[1], wf[2], None]

        def last_block(eng):
            return eng.value_load(rt.table[0:1, MAX_BLOCKS:24], min_val=2 * T // P - 1, max_val=MAX_BLOCKS - 1)

        def first(i):
            return isinstance(i, int) and i == 0

        with nc.Block() as block:
            @block.sync
            def _(sp):
                sp.dma_start(iota[:], a["c_iota"]).then_inc(ld, 16)
                end = last_block(sp)

                def body(i):
                    e = sp.value_load(rt.table[0:1, bass.ds(i, 1)], min_val=0, max_val=N_EXP - 1)
                    for u in range(2):
                        if not first(i):
                            sp.wait_ge(w_lo[u], i)
                        for c, w in ((0, wg), (HID, wu)):
                            src = w[bass.ds(e, 1), HALF * P * u:HALF * P * (u + 1), :]
                            sp.dma_start(wf[u][:, :, c:c + HID],
                                         src.rearrange("a (k p) n -> p (a k) n", p=P)).then_inc(w_loaded[u], 16)
                    if not first(i):
                        sp.wait_ge(w_lo[2], i)
                    src = wd[bass.ds(e, 1), :, :].rearrange("a (k p) n -> p (a k) n", p=P)
                    sp.dma_start(wf[2][:].rearrange("p (k c) n -> p k (c n)", k=2), src).then_inc(w_loaded[2], 16)
                body(0)
                with sp.Fori(1, end + 1) as i:
                    body(i)

            @block.tensor
            def _(pe):
                end = last_block(pe)

                def gather(i, half):
                    src, dst, done, out = ((rt.hh, ps_xh, xh_done, xh_out), (rt.hl, ps_xl, xl_done, xl_out))[half]
                    pe.wait_ge(picked, i + 1)
                    if not first(i):
                        pe.wait_ge(out, i)
                    for k in range(KT):
                        for t in range(TT):
                            mm = pe.matmul(dst[:, k // 4, P * (k % 4):P * (k % 4) + P],
                                           src[:, t, P * k:P * k + P], pick[:, t, :],
                                           start=(t == 0), stop=(t == TT - 1))
                    mm.then_inc(done, 1)

                def body(i, last=False):
                    pe.wait_ge(xh_out, i + 1)
                    pe.wait_ge(xl_out, i + 1)
                    if not first(i):
                        pe.wait_ge(hid_done, i)
                    for u in range(2):
                        pe.wait_ge(w_lo[u], i + 1)
                        for k in range(HALF):
                            for m, (x, w) in enumerate(((xh, wh), (xh, wl), (xl, wh))):
                                mm = pe.matmul(ps_gu[:, 0, :], x[:, HALF * u + k, :], w[u][:, k, :],
                                               start=(u == 0 and k == 0 and m == 0),
                                               stop=(u == 1 and k == HALF - 1 and m == 2))
                        mm.then_inc(unit0_used if u == 0 else gu_done, 1)
                    if not last:
                        gather(i + 1, 0)
                    pe.wait_ge(hid_done, i + 1)
                    if not first(i):
                        pe.wait_ge(tl_out, i)
                    for k in range(2):
                        mm = pe.transpose(ps_t[:, 0, P * k:P * k + P], hid[:, P * k:P * k + P], g.ident[:])
                    mm.then_inc(t_done, 1)
                    if not last:
                        gather(i + 1, 1)
                    pe.wait_ge(tl_out, i + 1)
                    pe.wait_ge(w_lo[2], i + 1)
                    if not first(i):
                        pe.wait_ge(y_out, i)
                    down = [w[2][:].rearrange("p (k c) n -> p k c n", k=2) for w in (wh, wl)]
                    for c in range(2):
                        for k in range(2):
                            for m, (x, w) in enumerate(((hth, down[0]), (hth, down[1]), (htl, down[0]))):
                                mm = pe.matmul(ps_y[:, c, :], x[:, k, :], w[:, k, c, :],
                                               start=(k == 0 and m == 0), stop=(k == 1 and m == 2))
                    mm.then_inc(y_done, 1)
                gather(0, 0)
                gather(0, 1)
                body(0)
                with pe.Fori(1, end) as i:
                    body(i)
                body(end, last=True)

            @block.scalar
            def _(act):
                end = last_block(act)

                def hi(i, u):
                    act.wait_ge(w_loaded[u], (i + 1) * (32 if u < 2 else 16))
                    if not first(i):
                        act.wait_ge((unit0_used, gu_done, y_done)[u], i)
                    act.activation(wh[u][:], wf[u][:], ACT.Copy).then_inc(w_hi[u], 1)

                def x_hi(i):
                    act.wait_ge(xh_done, i + 1)
                    act.activation(xh[:].rearrange("p k n -> p (k n)"), ps_xh[:].rearrange("p b n -> p (b n)"),
                                   ACT.Copy).then_inc(xh_out, 1)

                def body(i, last=False):
                    if not last:
                        hi(i + 1, 0)
                    act.wait_ge(gu_done, i + 1)
                    if not first(i):
                        act.wait_ge(hid_done, i)
                    act.activation(act_g[:], ps_gu[:, 0, 0:HID], ACT.Silu).then_inc(silu_done, 1)
                    if not last:
                        x_hi(i + 1)
                    act.wait_ge(t_done, i + 1)
                    if not first(i):
                        act.wait_ge(y_done, i)
                    act.activation(hth[:].rearrange("p k n -> p (k n)"), ps_t[:, 0, 0:HID], ACT.Copy).then_inc(th_out, 1)
                    if not last:
                        hi(i + 1, 1)
                    act.wait_ge(y_done, i + 1)
                    if not first(i):
                        act.wait_ge(y_stored, i * 16)
                    act.activation(y[:], ps_y[:].rearrange("p b n -> p (b n)"), ACT.Copy).then_inc(y_out, 1)
                    act.wait_ge(y_out, i + 1)
                    act.dma_start(rows[bass.ds(i * P, P), :], y[:]).then_inc(y_stored, 16)
                    if not last:
                        hi(i + 1, 2)
                for u in range(3):
                    hi(0, u)
                x_hi(0)
                body(0)
                with act.Fori(1, end) as i:
                    body(i)
                body(end, last=True)

            @block.gpsimd
            def _(pool):
                end = last_block(pool)

                def lo(i):
                    pool.wait_ge(w_hi[2], i + 1)
                    pool.tensor_tensor(wl[2][:], wf[2][:], wh[2][:].bitcast(F32), ALU.subtract).then_inc(w_lo[2], 1)
                lo(0)
                with pool.Fori(1, end + 1) as i:
                    lo(i)
                pool.wait_ge(added, 1)
                for t in range(TT):
                    for k in range(2):
                        pool.indirect_dma_start(rt.rows_back[:, k, t, :], None, rows[:, :],
                                                bass.IndirectOffsetOnAxis(rt.slot_i[:, t, k:k + 1], 0)).then_inc(back, 16)

            @block.vector
            def _(dve):
                end = last_block(dve)
                dve.wait_ge(ld, 16)
                dve.tensor_copy(slot[:], rt.slot[:]).then_inc(slot_done, 1)

                def choose(i):
                    dve.wait_ge(slot_done, i + 1)
                    for t in range(TT):
                        ins = dve.tensor_scalar(eq0[:, t, :], iota[:], slot[:, t, 0:1], None, ALU.is_equal)
                    ins.then_inc(eq_done, 1)
                    dve.wait_ge(eq_done, i + 1)
                    if not first(i):
                        dve.wait_ge(xl_done, i)
                    for t in range(TT):
                        ins = dve.scalar_tensor_tensor(pick[:, t, :], iota[:], slot[:, t, 1:2], eq0[:, t, :],
                                                       ALU.is_equal, ALU.add)
                    ins.then_inc(picked, 1)
                    dve.wait_ge(picked, i + 1)
                    dve.tensor_scalar(slot[:], slot[:], -float(P), None, ALU.add).then_inc(slot_done, 1)

                def lo(i, u):
                    dve.wait_ge(w_hi[u], i + 1)
                    dve.tensor_tensor(wl[u][:], wf[u][:], wh[u][:].bitcast(F32), ALU.subtract).then_inc(w_lo[u], 1)

                def x_lo(i):
                    dve.wait_ge(xl_done, i + 1)
                    if not first(i):
                        dve.wait_ge(gu_done, i)
                    dve.tensor_copy(xl[:].rearrange("p k n -> p (k n)"),
                                    ps_xl[:].rearrange("p b n -> p (b n)")).then_inc(xl_out, 1)

                def body(i, last=False):
                    dve.wait_ge(silu_done, i + 1)
                    if not first(i):
                        dve.wait_ge(t_done, i)
                    dve.tensor_tensor(hid[:], act_g[:], ps_gu[:, 0, HID:512], ALU.mult).then_inc(hid_done, 1)
                    dve.wait_ge(th_out, i + 1)
                    dve.tensor_tensor(htl[:].rearrange("p k n -> p (k n)"), ps_t[:, 0, 0:HID],
                                      hth[:].rearrange("p k n -> p (k n)").bitcast(F32),
                                      ALU.subtract).then_inc(tl_out, 1)
                    if not last:
                        x_lo(i + 1)
                        lo(i + 1, 0)
                        choose(i + 2)
                        lo(i + 1, 1)
                choose(0)
                lo(0, 0)
                lo(0, 1)
                x_lo(0)
                choose(1)
                body(0)
                with dve.Fori(1, end) as i:
                    body(i)
                body(end, last=True)
                dve.wait_ge(y_stored, end * 16 + 16)
                dve.tensor_copy(slot[:, 0, 0:1], slot[:, 0, 1:2]).then_inc(added, 1)
                dve.wait_ge(back, 16 * 2 * TT)
                for t in range(TT):
                    dve.tensor_scalar(g.h[:, t, :], g.h[:, t, :], ALPHA, None, ALU.mult).then_inc(scaled, 1)
                    for k in range(2):
                        dve.wait_ge(scaled, 3 * t + k + 1)
                        dve.scalar_tensor_tensor(g.h[:, t, :], rt.rows_back[:, k, t, :], rt.weight[:, t, k:k + 1],
                                                 g.h[:, t, :], ALU.mult, ALU.add).then_inc(scaled, 1)


CA_ROW = T + P
NSA_ROW = 2 * T
NSA_BIAS = 896


def stage_tables(g, a):
    nc = g.nc
    with Stage(nc, "tables") as st:
        tbl, onehot = st.sb("tbl", [32, NSA_H]), st.sb("onehot", [32, NSA_ROW])
        mask = st.sb("mask", [NSA_H, NSA_ROW])
        row = st.sb("row", [NSA_H, NSA_ROW])
        ca = st.sb("ca", [16, CA_ROW])
        ca_neg = st.sb("ca_neg", [16, CA_ROW])
        ps = st.ps("ps", 2)
        ld, mm, done, step, stored = (st.sem(x) for x in ("loaded", "mm", "done", "step", "stored"))
        with nc.Block() as block:
            @block.sync
            def _(sp):
                sp.dma_start(tbl[:], a["rel_bias"]).then_inc(ld, 16)
                sp.dma_start(onehot[:], a["c_t5_onehot"]).then_inc(ld, 16)
                sp.dma_start(mask[:], rows_of(a["c_t5_mask"], 0, NSA_ROW, NSA_H)).then_inc(ld, 16)
                sp.dma_start(ca[:, 0:2 * P + 1], a["ca_rel_bias_2"].rearrange("l h n -> (l h) n")).then_inc(ld, 16)
                sp.wait_ge(done, 2)
                sp.dma_start(g.nsa_rows, row[:]).then_inc(stored, 16)
                sp.dma_start(g.ca_rows, ca_neg[:]).then_inc(stored, 16)
                sp.wait_ge(stored, 32)

            @block.tensor
            def _(pe):
                pe.wait_ge(ld, 64)
                for j in range(2):
                    mm_ = pe.matmul(ps[0:NSA_H, j, :], tbl[:], onehot[:, 512 * j:512 * j + 512], start=True, stop=True)
                mm_.then_inc(mm, 1)

            @block.vector
            def _(dve):
                dve.wait_ge(mm, 1)
                dve.wait_ge(ld, 64)
                dve.scalar_tensor_tensor(row[:], ps[0:NSA_H].rearrange("p b n -> p (b n)"), -1.0, mask[:],
                                         ALU.mult, ALU.add).then_inc(done, 1)
                dve.tensor_copy(ca[:, 2 * P + 1:], ca[:, 2 * P:2 * P + 1].to_broadcast([16, CA_ROW - 2 * P - 1])).then_inc(step, 1)
                dve.wait_ge(step, 1)
                dve.tensor_scalar(ca_neg[:], ca[:], -1.0, None, ALU.mult).then_inc(done, 1)


def toeplitz(rows, head, width):
    n = rows.shape[1]
    return bass.AP(rows.tensor, rows.offset + head * n + n - (width + P - 1), [[1, P], [1, width]])


def backwards(tile, start, count, step=1):
    part = tile[:, 0:1]
    last = tile.shape[1] - 1
    return bass.AP(part.tensor, part.offset + last - start, [list(part.ap[0]), [-step, count]])


def stage_nsa_project(g, a, n):
    nc = g.nc
    w_kv, w_in = a["nsa_w_kv"], a["nsa_w_in"][0]

    def columns(w, c0, c1):
        def src(u):
            rows = slice(HALF * P * u, HALF * P * (u + 1))
            return [(c, w[rows, x:x + 256].rearrange("(k p) n -> p k n", p=P)) for c, x in ((0, c0), (256, c1))]
        return src
    blocks = [(columns(w_kv, 0, 256), True), (columns(w_kv, 512, 1024), True), (columns(w_kv, 768, 1280), False),
              (columns(w_in, 0, 256), True), (columns(w_in, 512, 768), True)]
    with Stage(nc, "nproj") as st:
        ws = WeightStream(st)
        wg = st.sb("wg", [P, KT, 48])
        small = st.ps("small", 1)
        e = st.sb("e", [P, TT, 48])
        ld, g_mm, g_exp, step = st.sem("loaded"), st.sem("g_mm"), st.sem("g_exp"), st.sem("step")
        with nc.Block() as block:
            @block.sync
            def _(sp):
                sp.dma_start(wg[:], w_in[:, NSA_H * DH:].rearrange("(k p) n -> p k n", p=P)).then_inc(ld, 16)
                for b, (src, _) in enumerate(blocks):
                    ws.load(sp, b, src)

            @block.tensor
            def _(pe):
                pe.wait_ge(ld, 16)
                for t in range(TT):
                    for k in range(KT):
                        for m, x in enumerate((g.xh, g.xl)):
                            mm = pe.matmul(small[:, 0, 48 * t:48 * t + 48], x[:, k, P * t:P * t + P].bitcast(F32),
                                           wg[:, k, :], start=(k == 0 and m == 0), stop=(k == KT - 1 and m == 1))
                mm.then_inc(g_mm, 1)
                for b, (_, stationary) in enumerate(blocks):
                    ws.multiply(pe, b, g.xh, g.xl, stationary)

            @block.gpsimd
            def _(pool):
                for b in range(len(blocks)):
                    ws.split_lo(pool, b)

            @block.scalar
            def _(act):
                for b in range(len(blocks)):
                    ws.split_hi(act, b, parts=2)
                    if b == 0:
                        act.wait_ge(g_mm, 1)
                        act.activation(e[:].rearrange("p t n -> p (t n)"), small[:, 0, 0:192], ACT.Exp,
                                       scale=-1.0).then_inc(g_exp, 1)

            @block.vector
            def _(dve):
                link = Link(dve, step)
                dve.wait_ge(g_exp, 1)
                link(dve.tensor_scalar(e[:], e[:], 1.0, None, ALU.add))
                link(dve.reciprocal(n.gate[:], e[:]))
                for b in range(len(blocks)):
                    for s in range(4):
                        dve.wait_ge(ws.acc_ready, 4 * b + s + 1)
                        acc = ws.acc[:, s, :]
                        if b == 0:
                            ins = dve.tensor_copy(n.raw[:, s, :], acc)
                        elif b == 1:
                            for grp in range(2):
                                for half in range(2):
                                    ins = dve.tensor_copy(n.kt[64 * half:64 * half + 64, s // 2, 2 * (s % 2) + grp, :],
                                                          ws.acc[64 * grp:64 * grp + 64, s, :])
                        elif b == 2:
                            ins = dve.tensor_copy(n.v[:, s, :], acc)
                        else:
                            ins = dve.tensor_scalar(n.qt[:, 4 * (b - 3) + s, :], acc, -(DH ** -0.5), None, ALU.mult)
                        ins.then_inc(ws.evicted, 1)


def stage_nsa_compress(g, a, n):
    nc = g.nc
    with Stage(nc, "ncomp") as st:
        w1 = [st.sb(f"w1{x}", [P, 32, P]) for x in "kv"]
        pos = [st.sb(f"pos{x}", [DH, 32]) for x in "kv"]
        w2k, w2v = st.sb("w2k", [P, 2, DH]), st.sb("w2v", [P, DH])
        pb = st.sb("pb", [P, 2])
        hid = st.sb("hid", [P, 2, NSA_G, N_CMP])
        ps = st.ps("ps", 6)
        ld, mm_hid, pb_done, hid_done, mm_out, done = (st.sem(x) for x in
            ("loaded", "mm_hid", "pb_done", "hid_done", "mm_out", "done"))
        with nc.Block() as block:
            @block.sync
            def _(sp):
                for i, x in enumerate("kv"):
                    w = a[f"cmp_{x}_w1"].rearrange("(l d) n -> d l n", d=DH)
                    for half in range(2):
                        sp.dma_start(w1[i][64 * half:64 * half + 64], w).then_inc(ld, 16)
                    sp.dma_start(pos[i][:], a[f"cmp_{x}_pos"].rearrange("l d -> d l"),
                                 allow_slow_non_contiguous=True).then_inc(ld, 16)
                for half in range(2):
                    sp.dma_start(w2k[:, half, :], a["cmp_k_w2"]).then_inc(ld, 16)
                sp.dma_start(w2v[:], a["cmp_v_w2"]).then_inc(ld, 16)

            @block.tensor
            def _(pe):
                pe.wait_ge(ld, 16 * 9)
                for i in range(2):
                    for l in range(32):
                        mm = pe.matmul(ps[:, 4, i:i + 1], w1[i][0:DH, l, :], pos[i][:, l:l + 1],
                                       start=(l == 0), stop=(l == 31))
                for i in range(2):
                    for grp in range(NSA_G):
                        half = grp % 2
                        rows = slice(64 * half, 64 * half + 64)
                        col = 32 * (grp // 2)
                        for l in range(32):
                            mm = pe.matmul(ps[:, 2 * i + half, col:col + N_CMP], w1[i][rows, l, :],
                                           n.raw[rows, 2 * i + grp // 2, l:l + 16 * (N_CMP - 1) + 1:16],
                                           start=(l == 0), stop=(l == 31))
                mm.then_inc(mm_hid, 1)
                pe.wait_ge(hid_done, 4)
                pe.matmul(ps[:, 5, 0:NSA_G * N_CMP], w2k[:].rearrange("p a d -> p (a d)"),
                          hid[:, 0].rearrange("p g n -> p (g n)"), start=True, stop=True)
                for grp in range(NSA_G):
                    mm = pe.matmul(ps[0:N_CMP, 4, 64 + DH * grp:64 + DH * grp + DH], hid[:, 1, grp, :], w2v[:],
                                   start=True, stop=True)
                mm.then_inc(mm_out, 1)

            @block.scalar
            def _(act):
                act.wait_ge(pb_done, 1)
                for i in range(2):
                    for half in range(2):
                        act.activation(hid[:, i, half::2, :],
                                       ps[:, 2 * i + half, 0:64].rearrange("p (g n) -> p g n", g=2)[:, :, 0:N_CMP],
                                       ACT.Silu, bias=pb[:, i:i + 1]).then_inc(hid_done, 1)

            @block.vector
            def _(dve):
                dve.wait_ge(mm_hid, 1)
                dve.tensor_copy(pb[:], ps[:, 4, 0:2]).then_inc(pb_done, 1)
                dve.wait_ge(mm_out, 1)
                dve.tensor_copy(n.kct[:].rearrange("p g n -> p (g n)"), ps[:, 5, 0:NSA_G * N_CMP]).then_inc(done, 1)
                dve.tensor_copy(n.vc[:].rearrange("p g n -> p (g n)"), ps[0:N_CMP, 4, 64:320]).then_inc(done, 1)


def stage_nsa_cmp(g, a, n):
    nc = g.nc
    H4, W = 4, 16 * N_CMP
    with Stage(nc, "ncmp") as st:
        bias = [st.sb(f"bias{i}", [P, NSA_BIAS]) for i in range(4)]
        valid = st.sb("valid", [P, TT, N_CMP])
        s = [st.sb(f"s{i}", [P, H4, TT, N_CMP]) for i in range(2)]
        m, l, r = ([st.sb(f"{x}{i}", [P, H4, TT]) for i in range(2)] for x in "mlr")
        ps, pt = st.ps("ps", 2), st.ps("pt", 4)
        ld, b_loaded, b_used, s_ready, v1, a1, p_done, t_done, out, step = (st.sem(x) for x in
            ("loaded", "b_loaded", "b_used", "s_ready", "shifted", "exped", "p_done", "t_done", "out", "step"))
        with nc.Block() as block:
            @block.sync
            def _(sp):
                sp.dma_start(valid[:], a["c_cmp_valid"]).then_inc(ld, 16)
                for h in range(NSA_H):
                    if h >= 4:
                        sp.wait_ge(b_used, h - 3)
                    sp.dma_start(bias[h % 4][:], toeplitz(g.nsa_rows, h, NSA_BIAS)).then_inc(b_loaded, 16)
                    sp.wait_ge(b_loaded, 16 * (h + 1))

            @block.tensor
            def _(pe):
                def scores(grp):
                    if grp >= 2:
                        pe.wait_ge(b_used, 4 * (grp - 1))
                    for hh in range(H4):
                        h = 4 * grp + hh
                        rows = slice(64 * (h % 2), 64 * (h % 2) + 64)
                        for t in range(TT):
                            c = (hh // 2 * TT + t) * N_CMP
                            mm = pe.matmul(ps[:, h % 2, 256 * (grp % 2) + c:256 * (grp % 2) + c + N_CMP],
                                           n.qt[rows, h // 2, P * t:P * t + P],
                                           n.kct[rows, grp, :], start=True, stop=True)
                    mm.then_inc(s_ready, 1)
                for grp in range(NSA_G):
                    if grp >= 1:
                        pe.wait_ge(b_used, 4 * grp)
                    scores(grp)
                    pe.wait_ge(p_done, grp + 1)
                    for hh in range(H4):
                        if grp >= 1:
                            pe.wait_ge(out, 4 * (grp - 1) + hh + 1)
                        for t in range(TT):
                            mm = pe.transpose(pt[0:N_CMP, hh, P * t:P * t + P], s[grp % 2][:, hh, t, :], g.ident[:])
                        mm.then_inc(t_done, 1)

            @block.vector
            def _(dve):
                link = Link(dve, step)
                dve.wait_ge(ld, 16)
                for grp in range(NSA_G):
                    x, mm_, ll, rr = s[grp % 2], m[grp % 2], l[grp % 2], r[grp % 2]
                    dve.wait_ge(s_ready, grp + 1)
                    if grp >= 2:
                        dve.wait_ge(t_done, 4 * (grp - 1))
                    for hh in range(H4):
                        h = 4 * grp + hh
                        dve.wait_ge(b_loaded, 16 * (h + 1))
                        c = 256 * (grp % 2) + (hh // 2) * TT * N_CMP
                        for t in range(TT):
                            x0 = 384 - P * t + 31
                            ins = dve.tensor_tensor(x[:, hh, t, :], ps[:, h % 2, c + t * N_CMP:c + (t + 1) * N_CMP],
                                                    backwards(bias[h % 4], x0, N_CMP, 16), ALU.add)
                        ins.then_inc(b_used, 1)
                    dve.wait_ge(b_used, 4 * grp + 4)
                    link(dve.tensor_reduce(mm_[:], x[:], AX.X, ALU.min))
                    for hh in range(H4):
                        ins = dve.tensor_tensor(x[:, hh], x[:, hh], mm_[:, hh].unsqueeze(2).to_broadcast([P, TT, N_CMP]),
                                                ALU.subtract)
                    ins.then_inc(v1, 1)
                    dve.wait_ge(a1, grp + 1)
                    link(dve.tensor_reduce(ll[:], x[:], AX.X, ALU.add))
                    link(dve.reciprocal(rr[:], ll[:]))
                    gate = n.gate[:, :, 12 * grp:12 * grp + 12].rearrange("p t (h b) -> p h t b", b=3)[:, :, :, 0]
                    link(dve.tensor_tensor(rr[:], rr[:], gate, ALU.mult))
                    for hh in range(H4):
                        ins = dve.tensor_tensor(x[:, hh], x[:, hh], rr[:, hh].unsqueeze(2).to_broadcast([P, TT, N_CMP]),
                                                ALU.mult)
                    link(ins)
                    for hh in range(H4):
                        ins = dve.tensor_tensor(x[:, hh], x[:, hh], valid[:], ALU.mult)
                    ins.then_inc(p_done, 1)

            @block.scalar
            def _(act):
                for grp in range(NSA_G):
                    act.wait_ge(v1, grp + 1)
                    act.activation(s[grp % 2][:], s[grp % 2][:], ACT.Exp, scale=-1.0).then_inc(a1, 1)
                    for hh in range(H4):
                        act.wait_ge(t_done, 4 * grp + hh + 1)
                        act.activation(n.pct[:, 4 * grp + hh, :], pt[0:N_CMP, hh, :], ACT.Copy).then_inc(out, 1)


def attend(g, name, heads, branches, q, k, v, bias_rows, bias_width, bias, gate, extra, finish, mask=None):
    nc = g.nc
    nb = branches
    U = heads * TT
    with Stage(nc, name) as st:
        s = [st.sb(f"s{i}", [P, nb, T]) for i in range(3)]
        m, l, r = ([st.sb(f"{x}{i}", [P, nb]) for i in range(3)] for x in "mlr")
        ptb = [st.sb(f"pt{i}", [P, nb, T]) for i in range(2)]
        bt = [st.sb(f"bias{i}", [P, bias_width]) for i in range(2)]
        mt = st.sb("mask", [P, P]) if mask is not None else None
        fin = finish(st)
        ps_s, ps_t, ps_o = [st.ps(f"pss{i}", nb) for i in range(2)], st.ps("pst", nb), \
            [st.ps(f"pso{i}", 1) for i in range(2)]
        m_loaded, masked = st.sem("m_loaded"), st.sem("masked")
        b_loaded = [st.sem(f"b_loaded{i}") for i in range(2)]
        s_ready, reduced, exped, normed, turned, copied, o_done, o_read, r_step = (st.sem(x) for x in
            ("s_ready", "reduced", "exped", "normed", "turned", "copied", "o_done", "o_read", "r_step"))
        fin.o_done = o_done

        def unit(u):
            return u // TT, u % TT, P * (u % TT + 1)

        with nc.Block() as block:
            @block.sync
            def _(sp):
                if mask is not None:
                    sp.dma_start(mt[:], mask[:, 0:P]).then_inc(m_loaded, 16)
                for h in range(heads):
                    if h >= 2:
                        sp.wait_ge(reduced, TT * (h - 1))
                    sp.dma_start(bt[h % 2][:], bias_rows(h)).then_inc(b_loaded[h % 2], 16)

            @block.gpsimd
            def _(pool):
                if mask is not None:
                    pool.wait_ge(m_loaded, 16)
                    for h in range(heads):
                        pool.wait_ge(b_loaded[h % 2], 16 * (h // 2 + 1))
                        diag = bt[h % 2][:, 0:P]
                        pool.tensor_tensor(diag, diag, mt[:], ALU.add).then_inc(masked, 1)

            @block.tensor
            def _(pe):
                for n in range(U + 3):
                    if n < U:
                        h, i, width = unit(n)
                        if n >= 2:
                            pe.wait_ge(reduced, n - 1)
                        for b in range(nb):
                            mm = pe.matmul(ps_s[n % 2][:, b, 0:width], q(h, i), k(h, b, width), start=True, stop=True)
                        mm.then_inc(s_ready, 1)
                    if 0 <= n - 2 < U:
                        u = n - 2
                        h, i, width = unit(u)
                        pe.wait_ge(normed, u + 1)
                        if u >= 1:
                            pe.wait_ge(copied, u)
                        for b in range(nb):
                            for kt in range(i + 1):
                                mm = pe.transpose(ps_t[:, b, P * kt:P * kt + P], s[u % 3][:, b, P * kt:P * kt + P],
                                                  g.ident[:])
                        mm.then_inc(turned, 1)
                    if 0 <= n - 3:
                        u = n - 3
                        h, i, width = unit(u)
                        pe.wait_ge(copied, u + 1)
                        half = h % 2
                        if i == 0 and half == 0 and h >= 4:
                            pe.wait_ge(o_read, h // 2 - 1)
                        out = ps_o[(h // 2) % 2][64 * half:64 * half + 64, 0, P * i:P * i + P]
                        parts = [(v(h, b, kt), ptb[u % 2][:, b, P * kt:P * kt + P])
                                 for b in range(nb) for kt in range(i + 1)] + extra(h, i)
                        for j, (lhs, rhs) in enumerate(parts):
                            mm = pe.matmul(out, lhs, rhs, start=(j == 0), stop=(j == len(parts) - 1))
                        mm.then_inc(o_done, 1)

            @block.scalar
            def _(act):
                for n in range(U + 3):
                    if 0 <= n - 3 and (n - 3) % (2 * TT) == 2 * TT - 1:
                        fin.act(act, (n - 3) // (2 * TT), ps_o, o_done)
                    if 0 <= n - 2 < U:
                        u = n - 2
                        act.wait_ge(turned, u + 1)
                        if u >= 2:
                            act.wait_ge(o_done, u - 1)
                        width = unit(u)[2]
                        act.activation(ptb[u % 2][:, :, 0:width], ps_t[:, :, 0:width], ACT.Copy).then_inc(copied, 1)
                    if n < U:
                        act.wait_ge(reduced, n + 1)
                        width = unit(n)[2]
                        for b in range(nb):
                            ins = act.activation(s[n % 3][:, b, 0:width], s[n % 3][:, b, 0:width], ACT.Exp, scale=-1.0,
                                                 bias=m[n % 3][:, b:b + 1], accum_out=l[n % 3][:, b:b + 1])
                        ins.then_inc(exped, 1)

            @block.vector
            def _(dve):
                for n in range(U + 3):
                    if n < U:
                        h, i, width = unit(n)
                        if mask is None:
                            dve.wait_ge(b_loaded[h % 2], 16 * (h // 2 + 1))
                        else:
                            dve.wait_ge(masked, h + 1)
                        dve.wait_ge(s_ready, n + 1)
                        if n >= 3:
                            dve.wait_ge(turned, n - 2)
                        bias_ap = bias(bt[h % 2], h, i, width)
                        for b in range(nb):
                            ins = dve.tensor_tensor_reduce(s[n % 3][:, b, 0:width], ps_s[n % 2][:, b, 0:width], bias_ap,
                                                           1.0, 3e38, ALU.add, ALU.min, m[n % 3][:, b:b + 1])
                        ins.then_inc(reduced, 1)
                    if 0 <= n - 1 < U:
                        u = n - 1
                        h, i, width = unit(u)
                        dve.wait_ge(exped, u + 1)
                        dve.reciprocal(r[u % 3][:], l[u % 3][:]).then_inc(r_step, 1)
                        steps = 2 if gate else 1
                        dve.wait_ge(r_step, steps * u + 1)
                        if gate:
                            dve.tensor_tensor(r[u % 3][:], r[u % 3][:], gate(h, i), ALU.mult).then_inc(r_step, 1)
                            dve.wait_ge(r_step, steps * u + 2)
                        for b in range(nb):
                            ins = dve.tensor_scalar(s[u % 3][:, b, 0:width], s[u % 3][:, b, 0:width],
                                                    r[u % 3][:, b:b + 1], None, ALU.mult)
                        ins.then_inc(normed, 1)
                    if 0 <= n - 3 and (n - 3) % (2 * TT) == 2 * TT - 1:
                        fin.dve(dve, (n - 3) // (2 * TT), ps_o, o_read)


class SplitOutput:

    def __init__(self, st, heads, hi, lo, factor=None):
        self.hi, self.lo, self.factor, self.heads = hi, lo, factor, heads
        self.hi_done, self.y_done = st.sem("hi_done"), st.sem("y_done")
        self.y = [st.sb(f"y{i}", [P, T]) for i in range(2)] if factor is not None else None

    def act(self, act, j, ps_o, o_done):
        if self.factor is None:
            act.wait_ge(o_done, 2 * TT * (j + 1))
            act.activation(self.hi[:, j, :], ps_o[j % 2][:, 0, :], ACT.Copy).then_inc(self.hi_done, 1)
        else:
            act.wait_ge(self.y_done, j + 1)
            act.activation(self.hi[:, j, :], self.y[j % 2][:], ACT.Copy).then_inc(self.hi_done, 1)

    def dve(self, dve, j, ps_o, o_read):
        if self.factor is None:
            dve.wait_ge(self.hi_done, j + 1)
            dve.tensor_tensor(self.lo[:, j, :], ps_o[j % 2][:, 0, :], self.hi[:, j, :].bitcast(F32),
                              ALU.subtract).then_inc(o_read, 1)
        else:
            dve.wait_ge(self.o_done, 2 * TT * (j + 1))
            dve.tensor_tensor(self.y[j % 2][:], ps_o[j % 2][:, 0, :], self.factor[:, j, :],
                              ALU.mult).then_inc(self.y_done, 1)
            dve.wait_ge(self.hi_done, j + 1)
            dve.tensor_tensor(self.lo[:, j, :], self.y[j % 2][:], self.hi[:, j, :].bitcast(F32),
                              ALU.subtract).then_inc(o_read, 1)


def stage_nsa_attend(g, a, n):
    def half(h):
        return slice(64 * (h % 2), 64 * (h % 2) + 64)
    attend(g, "natt", NSA_H, 2,
           q=lambda h, i: n.qt[half(h), h // 2, P * i:P * i + P],
           k=lambda h, b, w: n.kt[half(h), b, h // 4, 0:w],
           v=lambda h, b, kt: n.v[:, kt, 256 * b + DH * (h // 4):256 * b + DH * (h // 4) + DH],
           bias_rows=lambda h: toeplitz(g.nsa_rows, h, NSA_BIAS), bias_width=NSA_BIAS,
           bias=lambda t, h, i, w: backwards(t, 384 - P * i, w),
           gate=lambda h, i: n.gate[:, i, 3 * h + 1:3 * h + 3],
           extra=lambda h, i: [(n.vc[:, h // 4, :], n.pct[:, h, P * i:P * i + P])],
           finish=lambda st: SplitOutput(st, NSA_H, g.xh, g.xl))


BW = 512
BF = BW // P
MH = 8
MLA_NOPE, MLA_ROPE, MLA_QK = 64, 32, 96
MLA_SCALE = MLA_QK ** -0.5
COL = {"u": 0, "va": 512, "za": 1024, "mla": 1536, "zb": 1952, "qc": 2464, "kc": 2976, "vc": 3488,
       "zc": 4000, "g": 4512}
MLA_COLS = 256 + 128 + 32


def stage_branch_project(g, a, layer, s, part, order):
    nc = g.nc
    w = a["w_in_2"][layer]

    def source(name):
        width = MLA_COLS if name == "mla" else BW

        def src(u):
            rows = slice(HALF * P * u, HALF * P * (u + 1))
            return [(0, w[rows, COL[name]:COL[name] + width].rearrange("(k p) n -> p k n", p=P))]
        return src

    with Stage(nc, f"bproj{part}{layer}") as st:
        ws = WeightStream(st)
        with nc.Block() as block:
            @block.sync
            def _(sp):
                for b, (name, _) in enumerate(order):
                    ws.load(sp, b, source(name))

            @block.tensor
            def _(pe):
                for b, (name, stationary) in enumerate(order):
                    ws.multiply(pe, b, g.xh, g.xl, stationary, MLA_COLS if name == "mla" else BW)

            @block.gpsimd
            def _(pool):
                for b, (name, _) in enumerate(order):
                    ws.split_lo(pool, b, MLA_COLS if name == "mla" else BW)

            @block.scalar
            def _(act):
                ws.split_hi(act, 0, cols=MLA_COLS if order[0][0] == "mla" else BW)
                for b, (name, _) in enumerate(order):
                    if b + 1 < len(order):
                        ws.split_hi(act, b + 1, cols=MLA_COLS if order[b + 1][0] == "mla" else BW)
                    for t in range(4):
                        if name in ("za", "zb", "zc"):
                            act.wait_ge(ws.acc_ready, 4 * b + t + 1)
                            act.wait_ge(ws.evicted, 4 * b + t)
                            act.activation(s.t[name][:, t, :], ws.acc[:, t, :], ACT.Silu).then_inc(ws.evicted, 1)

            @block.vector
            def _(dve):
                for b, (name, _) in enumerate(order):
                    for t in range(4):
                        if name in ("za", "zb", "zc"):
                            continue
                        dve.wait_ge(ws.acc_ready, 4 * b + t + 1)
                        dve.wait_ge(ws.evicted, 4 * b + t)
                        if name == "qc":
                            ins = dve.tensor_scalar(s.t[name][:, t, :], ws.acc[:, t, :], -(DH ** -0.5), None, ALU.mult)
                        elif name == "mla":
                            ins = dve.tensor_copy(s.t[name][:, t, :], ws.acc[:, t, 0:MLA_COLS])
                        else:
                            ins = dve.tensor_copy(s.t[name][:, t, :], ws.acc[:, t, :])
                        ins.then_inc(ws.evicted, 1)


def stage_spatial_gate(g, a, layer, s):
    nc = g.nc
    G = 8
    with Stage(nc, f"sgu{layer}") as st:
        wraw, wt = st.sb("wraw", [P, G, P]), st.sb("wt", [P, G, P])
        gain, shift = st.sb("gain", [P, BW]), st.sb("shift", [P, BW])
        bias = st.sb("bias", [P, BF, P])
        stats, mv = st.sb("stats", [P, TT, 6]), st.sb("mv", [P, TT, 2])
        root, inv = st.sb("root", [P, TT]), st.sb("inv", [P, TT])
        uz = st.sb("uz", [P, BF, T])
        y = st.sb("y", [P, BF, T])
        ps_w, ps_m = st.ps("w", 2), st.ps("m", 4)
        ld, step, agg, rooted, normed, shifted = (st.sem(x) for x in ("loaded", "step", "agg", "rooted", "normed", "shifted"))
        w_t, w_done, mixed, y_step, hi_done, lo_done, uz_done = (st.sem(x) for x in
            ("w_turned", "w_done", "mixed", "y_step", "hi_done", "lo_done", "uz_done"))
        va = s.t["va"]
        with nc.Block() as block:
            @block.sync
            def _(sp):
                sp.dma_start(wraw[:], a["sgu_w_2"][layer].rearrange("g t s -> t g s")).then_inc(ld, 16)
                sp.dma_start(gain[:], rows_of(a["sgu_ln_g_2"], layer * BW, BW)).then_inc(ld, 16)
                sp.dma_start(shift[:], rows_of(a["sgu_ln_b_2"], layer * BW, BW)).then_inc(ld, 16)
                b = a["sgu_b_2"]
                for half in range(2):
                    sp.dma_start(bias[64 * half:64 * half + 64],
                                 bass.AP(b.tensor, b.offset + (layer * G + half) * P, [[0, 64], [2 * P, BF], [1, P]])
                                 ).then_inc(ld, 16)

            @block.tensor
            def _(pe):
                pe.wait_ge(ld, 80)
                for j in range(G):
                    mm = pe.transpose(ps_w[:, j // 4, P * (j % 4):P * (j % 4) + P], wraw[:, j, :], g.ident[:])
                mm.then_inc(w_t, 1)
                pe.wait_ge(w_done, 2)
                pe.wait_ge(shifted, TT)
                for f in range(BF):
                    for t in range(TT):
                        for half in range(2):
                            j = 2 * f + half
                            mm = pe.matmul(ps_m[64 * half:64 * half + 64, f, P * t:P * t + P],
                                           va[:, t, 64 * j:64 * j + 64], wt[:, j, :], start=True, stop=True)
                    mm.then_inc(mixed, 1)

            @block.vector
            def _(dve):
                for t in range(TT):
                    dve.bn_stats(stats[:, t, :], va[:, t, :]).then_inc(step, 1)
                    dve.wait_ge(step, t + 1)
                    dve.bn_aggr(mv[:, t, :], stats[:, t, :]).then_inc(agg, 1)
                dve.wait_ge(rooted, 1)
                dve.reciprocal(inv[:], root[:]).then_inc(step, 1)
                dve.wait_ge(step, TT + 1)
                dve.wait_ge(ld, 80)
                for t in range(TT):
                    dve.tensor_scalar(va[:, t, :], va[:, t, :], mv[:, t, 0:1], inv[:, t:t + 1],
                                      ALU.subtract, ALU.mult).then_inc(step, 1)
                    dve.wait_ge(step, TT + 2 + t)
                    dve.tensor_tensor(va[:, t, :], va[:, t, :], gain[:], ALU.mult).then_inc(normed, 1)
                dve.wait_ge(w_t, 1)
                for j in range(2):
                    dve.tensor_tensor(wt[:, 4 * j:4 * j + 4, :], ps_w[:, j, :].rearrange("p (a n) -> p a n", a=4),
                                      g.triu[:].unsqueeze(1).to_broadcast([P, 4, P]), ALU.mult).then_inc(w_done, 1)
                for f in range(BF):
                    dve.wait_ge(mixed, f + 1)
                    dve.tensor_tensor(y[:, f, :].rearrange("p (t n) -> p t n", t=TT),
                                      ps_m[:, f, :].rearrange("p (t n) -> p t n", t=TT),
                                      bias[:, f:f + 1, :].to_broadcast([P, TT, P]), ALU.add).then_inc(y_step, 1)
                    dve.wait_ge(y_step, 2 * f + 1)
                    dve.wait_ge(uz_done, 1)
                    dve.tensor_tensor(y[:, f, :], y[:, f, :], uz[:, f, :], ALU.mult).then_inc(y_step, 1)
                    dve.wait_ge(hi_done, f + 1)
                    dve.tensor_tensor(s.yl[:, f, :], y[:, f, :], s.yh[:, f, :].bitcast(F32), ALU.subtract).then_inc(lo_done, 1)

            @block.gpsimd
            def _(pool):
                for t in range(TT):
                    pool.wait_ge(normed, t + 1)
                    pool.tensor_tensor(va[:, t, :], va[:, t, :], shift[:], ALU.add).then_inc(shifted, 1)
                pool.tensor_tensor(uz[:], s.t["u"][:], s.t["za"][:], ALU.mult).then_inc(uz_done, 1)

            @block.scalar
            def _(act):
                act.wait_ge(agg, TT)
                act.activation(root[:], mv[:, :, 1], ACT.Sqrt, bias=g.eps6[:]).then_inc(rooted, 1)
                for f in range(BF):
                    act.wait_ge(y_step, 2 * f + 2)
                    act.activation(s.yh[:, f, :], y[:, f, :], ACT.Copy).then_inc(hi_done, 1)


def stage_latent(g, a, layer, s):
    nc = g.nc
    x = s.t["mla"]
    with Stage(nc, f"mla{layer}") as st:
        uq, usw = st.sb("uq", [P, 2, MH * MLA_QK]), st.sb("usw", [P, 2, MH, MLA_ROPE])
        kn, kv = st.sb("kn", [P, MH, MLA_NOPE]), st.sb("kv", [P, MH, 64])
        gain = st.sb("gain", [P, 384])
        cq, sq_ = st.sb("ropec", [P, T]), st.sb("ropes", [P, T])
        kc, ks = st.sb("kcos", [P, TT, 16]), st.sb("ksin", [P, TT, 16])
        junk = st.sb("junk", [P, 256])
        ms, root, inv = st.sb("ms", [P, TT, 2]), st.sb("root", [P, TT, 2]), st.sb("inv", [P, TT, 2])
        kr, t1, t2 = st.sb("kr", [P, TT, MLA_QK]), st.sb("t1", [P, TT, 16]), st.sb("t2", [P, TT, 16])
        xt = st.sb("xt", [P, 3, T])
        r1, r2 = st.sb("r1", [P, T]), st.sb("r2", [P, T])
        ps_t, ps_q, ps_s, ps_k = st.ps("t", 2), st.ps("q", 2), st.ps("sw", 2), st.ps("k", 2)
        ld, step, sq_done, rooted, zeroed = (st.sem(z) for z in ("loaded", "step", "squared", "rooted", "zeroed"))
        ready, turned, taken, q_done, q_nope, q_rope = (st.sem(z) for z in
            ("ready", "turned", "taken", "q_done", "q_nope", "q_rope"))
        kv_taken = st.sem("kv_taken")
        k_done, k_out, sw_done, kr_out = st.sem("k_done"), st.sem("k_out"), st.sem("sw_done"), st.sem("kr_out")
        w_uq, w_kv = a["mla_w_uq_2"][layer], a["mla_w_ukv_2"][layer]
        with nc.Block() as block:
            @block.sync
            def _(sp):
                sp.dma_start(gain[:, 0:256], rows_of(a["mla_q_norm_g_2"], layer * 256, 256)).then_inc(ld, 16)
                sp.dma_start(gain[:, 256:], rows_of(a["mla_kv_norm_g_2"], layer * 128, 128)).then_inc(ld, 16)
                sp.dma_start(kc[:], a["c_rope_cos"]).then_inc(ld, 16)
                sp.dma_start(ks[:], a["c_rope_sin"]).then_inc(ld, 16)
                sp.dma_start(cq[:], a["c_ropeq_cos"]).then_inc(ld, 16)
                sp.dma_start(sq_[:], a["c_ropeq_sin"]).then_inc(ld, 16)
                sp.dma_start(uq[:], w_uq.rearrange("(k p) n -> p k n", p=P)).then_inc(ld, 16)
                v = w_uq.rearrange("(k p) (h n) -> k p h n", p=P, n=MLA_QK)
                for k in range(2):
                    sp.dma_start(usw[:, k, :, 0:16], v[k, :, :, 80:96]).then_inc(ld, 16)
                    sp.dma_start(usw[:, k, :, 16:32], v[k, :, :, 64:80]).then_inc(ld, 16)
                v = w_kv.rearrange("p (h n) -> p h n", n=128)
                sp.dma_start(kn[:], v[:, :, 0:64]).then_inc(ld, 16)
                sp.dma_start(kv[:], v[:, :, 64:128]).then_inc(ld, 16)

            @block.gpsimd
            def _(pool):
                pool.memset(kr[:, :, 0:64], 0.0).then_inc(zeroed, 1)

            @block.scalar
            def _(act):
                for t in range(TT):
                    act.activation(junk[:], x[:, t, 0:256], ACT.Square, scale=1.0 / 16,
                                   accum_out=ms[:, t, 0:1]).then_inc(sq_done, 1)
                    act.wait_ge(sq_done, 2 * t + 1)
                    act.activation(junk[:, 0:128], x[:, t, 256:384], ACT.Square, scale=128 ** -0.5,
                                   accum_out=ms[:, t, 1:2]).then_inc(sq_done, 1)
                    act.wait_ge(sq_done, 2 * t + 2)
                act.activation(root[:], ms[:], ACT.Sqrt, bias=g.eps6[:]).then_inc(rooted, 1)
                act.wait_ge(turned, 3)
                act.activation(xt[:, 2, :], ps_t[:, 0, :], ACT.Copy).then_inc(kv_taken, 1)
                for h in range(MH):
                    act.wait_ge(q_done, h + 1)
                    act.activation(s.mq[0:64, h, :], ps_q[0:64, h % 2, :], ACT.Copy, scale=-MLA_SCALE).then_inc(q_nope, 1)

            @block.tensor
            def _(pe):
                pe.wait_ge(ready, 1)
                for j in range(3):
                    if j == 2:
                        pe.wait_ge(taken, 1)
                    for t in range(TT):
                        mm = pe.transpose(ps_t[:, j % 2, P * t:P * t + P], x[:, t, P * j:P * j + P], g.ident[:])
                    mm.then_inc(turned, 1)
                pe.wait_ge(taken, 2)
                for t in range(TT):
                    mm = pe.transpose(ps_t[0:MLA_QK, 1, P * t:P * t + P], kr[:, t, :], g.ident[:])
                mm.then_inc(turned, 1)
                pe.wait_ge(kv_taken, 1)
                for j in range(2):
                    for k in range(2):
                        mm = pe.matmul(ps_s[:, j, :], usw[:, k, 4 * j:4 * j + 4, :].rearrange("p h n -> p (h n)"),
                                       xt[:, k, :], start=(k == 0), stop=(k == 1))
                mm.then_inc(sw_done, 1)
                for h in range(MH):
                    if h >= 2:
                        pe.wait_ge(q_nope, h - 1)
                        pe.wait_ge(q_rope, h - 1)
                    for k in range(2):
                        mm = pe.matmul(ps_q[0:MLA_QK, h % 2, :], uq[:, k, MLA_QK * h:MLA_QK * h + MLA_QK], xt[:, k, :],
                                       start=(k == 0), stop=(k == 1))
                    mm.then_inc(q_done, 1)
                    if h >= 2:
                        pe.wait_ge(k_out, h - 1)
                    if h < 4:
                        mm = pe.matmul(ps_k[:, h % 2, :], kn[:, 2 * h:2 * h + 2, :].rearrange("p h n -> p (h n)"),
                                       xt[:, 2, :], start=True, stop=True)
                    else:
                        t = h - 4
                        mm = pe.matmul(ps_k[:, h % 2, :], xt[:, 2, P * t:P * t + P], kv[:].rearrange("p h n -> p (h n)"),
                                       start=True, stop=True)
                    mm.then_inc(k_done, 1)

            @block.vector
            def _(dve):
                link = Link(dve, step)
                dve.wait_ge(rooted, 1)
                dve.wait_ge(ld, 16 * 13)
                dve.wait_ge(zeroed, 1)
                link(dve.reciprocal(inv[:], root[:]))
                for t in range(TT):
                    dve.scalar_tensor_tensor(x[:, t, 0:256], x[:, t, 0:256], inv[:, t, 0:1], gain[:, 0:256],
                                             ALU.mult, ALU.mult)
                    dve.scalar_tensor_tensor(x[:, t, 256:384], x[:, t, 256:384], inv[:, t, 1:2], gain[:, 256:],
                                             ALU.mult, ALU.mult)
                x1, x2 = x[:, :, 384:400], x[:, :, 400:416]
                dve.tensor_tensor(t1[:], x1, kc[:], ALU.mult)
                link(dve.tensor_tensor(t2[:], x2, ks[:], ALU.mult))
                link(dve.tensor_tensor(kr[:, :, 64:80], t1[:], t2[:], ALU.subtract))
                dve.tensor_tensor(t1[:], x1, ks[:], ALU.mult)
                link(dve.tensor_tensor(t2[:], x2, kc[:], ALU.mult))
                dve.tensor_tensor(kr[:, :, 80:96], t1[:], t2[:], ALU.add).then_inc(ready, 1)
                for j in range(2):
                    dve.wait_ge(turned, j + 1)
                    dve.tensor_copy(xt[:, j, :], ps_t[:, j, :]).then_inc(taken, 1)
                dve.wait_ge(turned, 4)
                for h in range(MH):
                    ins = dve.tensor_copy(s.mk[64:96, h, :], ps_t[64:96, 1, :])
                ins.then_inc(kr_out, 1)
                dve.wait_ge(sw_done, 1)
                n_step = link.n
                for h in range(MH):
                    if h < 4:
                        dve.wait_ge(k_done, h + 1)
                        dve.tensor_copy(s.mk[0:64, 2 * h, :], ps_k[0:64, h % 2, :])
                        dve.tensor_copy(s.mk[0:64, 2 * h + 1, :], ps_k[64:128, h % 2, :]).then_inc(k_out, 1)
                    else:
                        dve.wait_ge(k_done, h + 1)
                        dve.tensor_copy(s.mv[:, h - 4, :], ps_k[:, h % 2, :]).then_inc(k_out, 1)
                    dve.wait_ge(q_nope, h + 1)
                    j = 32 * (h % 4)
                    dve.tensor_tensor(r1[64:96, :], ps_q[64:96, h % 2, :], cq[64:96, :], ALU.mult)
                    link(dve.tensor_tensor(r2[64:96, :], ps_s[j:j + 32, h // 4, :], sq_[j:j + 32, :], ALU.mult))
                    dve.tensor_tensor(s.mq[64:96, h, :], r1[64:96, :], r2[64:96, :], ALU.add).then_inc(q_rope, 1)
                    dve.wait_ge(q_rope, h + 1)


def stage_latent_attend(g, a, layer, s):
    attend(g, f"matt{layer}", MH, 1,
           q=lambda h, i: s.mq[:, h, P * i:P * i + P],
           k=lambda h, b, w: s.mk[:, h, 0:w],
           v=lambda h, b, kt: s.mv[:, kt, 64 * h:64 * h + 64],
           bias_rows=lambda h: a["c_block_bias"], bias_width=T,
           bias=lambda t, h, i, w: backwards(t, 384 - P * i, w),
           gate=None, extra=lambda h, i: [],
           finish=lambda st: SplitOutput(st, MH, s.yh[:, BF:2 * BF, :], s.yl[:, BF:2 * BF, :], s.t["zb"]))


def stage_band_attend(g, a, layer, s):
    def half(h):
        return slice(64 * (h % 2), 64 * (h % 2) + 64)
    attend(g, f"batt{layer}", MH, 1,
           q=lambda h, i: s.t["qc"][half(h), h // 2, P * i:P * i + P],
           k=lambda h, b, w: s.t["kc"][half(h), h // 2, 0:w],
           v=lambda h, b, kt: s.t["vc"][:, kt, 64 * h:64 * h + 64],
           bias_rows=lambda h: toeplitz(g.ca_rows, MH * layer + h, T), bias_width=T,
           bias=lambda t, h, i, w: backwards(t, 384 - P * i, w),
           gate=None, extra=lambda h, i: [], mask=a["c_block_bias"],
           finish=lambda st: SplitOutput(st, MH, s.yh[:, 2 * BF:, :], s.yl[:, 2 * BF:, :], s.t["zc"]))


def stage_merge(g, a, layer, s):
    nc = g.nc
    w, wb = a["w_in_2"][layer], a["w_branch_2"][layer]
    with Stage(nc, f"merge{layer}") as st:
        wf = [st.sb(f"wf{u}", [P, HALF, 512]) for u in range(3)]
        wh = [st.sb(f"wh{u}", [P, HALF, 512], F32R) for u in range(3)]
        wl = [st.sb(f"wl{u}", [P, HALF, 512], F32R) for u in range(3)]
        merged = st.sb("merged", [P, KT, T])
        gate, prod = st.sb("gate", [P, 2, T]), st.sb("prod", [P, 2, T])
        gb = st.sb("gb", [P, 3, KT])
        ps_g, ps_b = st.ps("g", 4), st.ps("b", 4)
        ld = st.sem("loaded")
        loaded = [st.sem(f"w_loaded{u}") for u in range(3)]
        hi_ready, lo_ready = [st.sem(f"w_hi{u}") for u in range(3)], [st.sem(f"w_lo{u}") for u in range(3)]
        unit0_used, g_ready, b_ready = st.sem("unit0_used"), st.sem("gate_acc"), st.sem("branch_acc")
        g_out, b_out, added, hi_done, lo_done = (st.sem(x) for x in ("gate_out", "branch_out", "added", "hi_done", "lo_done"))

        def at(n, j, per, k=0):
            return n * (2 * per) + (j * per + k)

        def start(n, j):
            return isinstance(n, int) and n == 0 and j == 0

        with nc.Block() as block:
            @block.sync
            def _(sp):
                for n in range(3):
                    sp.dma_start(gb[:, n, :], a["gate_b_2"][layer][n].rearrange("(k p) -> p k", p=P),
                                 allow_slow_non_contiguous=True).then_inc(ld, 16)

                def body(n):
                    for j in range(2):
                        for u in range(3):
                            if not start(n, j):
                                sp.wait_ge(lo_ready[u], at(n, j, 1))
                            if u < 2:
                                src = w[HALF * P * u:HALF * P * (u + 1), bass.ds(n * D + (COL["g"] + 512 * j), 512)] \
                                    .rearrange("(k p) n -> p k n", p=P)
                            else:
                                src = wb[bass.ds(n, 1), :, 512 * j:512 * j + 512].rearrange("a (k p) n -> p (a k) n", p=P)
                            sp.dma_start(wf[u][:], src).then_inc(loaded[u], 16)
                over(sp, 3, body)

            @block.tensor
            def _(pe):
                def product(ps, u, x, k0, f, first, last):
                    for k in range(HALF):
                        for m, (wm, xm) in enumerate(((wh, x[0]), (wh, x[1]), (wl, x[0]))):
                            rhs = xm[:, bass.ds(k0 + k, 1), :].rearrange("p a n -> p (a n)")
                            mm = pe.matmul(ps[:, f, :], wm[u][:, k, P * f:P * f + P], rhs,
                                           start=(first and k == 0 and m == 0), stop=(last and k == HALF - 1 and m == 2))
                    return mm

                def body(n):
                    for j in range(2):
                        for u in range(2):
                            pe.wait_ge(lo_ready[u], at(n, j, 1, 1))
                            for f in range(4):
                                if u == 0 and not start(n, j):
                                    pe.wait_ge(g_out, at(n, j, 4, f - 3))
                                mm = product(ps_g, u, (g.xh, g.xl), HALF * u, f, u == 0, u == 1)
                                if u == 1:
                                    mm.then_inc(g_ready, 1)
                            if u == 0:
                                mm.then_inc(unit0_used, 1)
                        pe.wait_ge(lo_ready[2], at(n, j, 1, 1))
                        for f in range(4):
                            if not start(n, j):
                                pe.wait_ge(b_out, at(n, j, 4, f - 3))
                            product(ps_b, 2, (s.yh, s.yl), n * HALF, f, True, True).then_inc(b_ready, 1)
                over(pe, 3, body)

            @block.gpsimd
            def _(pool):
                def body(n):
                    for j in range(2):
                        for u in range(3):
                            pool.wait_ge(hi_ready[u], at(n, j, 1, 1))
                            pool.tensor_tensor(wl[u][:], wf[u][:], wh[u][:].bitcast(F32), ALU.subtract).then_inc(lo_ready[u], 1)
                over(pool, 3, body)

            @block.scalar
            def _(act):
                act.wait_ge(ld, 48)

                def hi(n, j, u):
                    act.wait_ge(loaded[u], at(n, j, 16, 16))
                    if not start(n, j):
                        act.wait_ge((unit0_used, g_ready, b_ready)[u], at(n, j, 1 if u == 0 else 4))
                    act.activation(wh[u][:], wf[u][:], ACT.Copy).then_inc(hi_ready[u], 1)

                def body(n):
                    for j in range(2):
                        for u in range(3):
                            hi(n, j, u)
                        for f in range(4):
                            act.wait_ge(g_ready, at(n, j, 4, f + 1))
                            if not (start(n, j) and f < 2):
                                act.wait_ge(b_out, at(n, j, 4, f - 1))
                            act.activation(gate[:, f % 2, :], ps_g[:, f, :], ACT.Sigmoid,
                                           bias=gb[:, bass.ds(n, 1), 4 * j + f:4 * j + f + 1]
                                           .rearrange("p a n -> p (a n)")).then_inc(g_out, 1)
                over(act, 3, body)
                act.wait_ge(b_ready, 24)
                for k in range(KT):
                    act.wait_ge(added, KT + k + 1)
                    act.activation(g.xh[:, k, :], merged[:, k, :], ACT.Copy).then_inc(hi_done, 1)

            @block.vector
            def _(dve):
                def body(n):
                    for j in range(2):
                        for f in range(4):
                            dve.wait_ge(b_ready, at(n, j, 4, f + 1))
                            dve.wait_ge(g_out, at(n, j, 4, f + 1))
                            out = merged[:, 4 * j + f, :]
                            if isinstance(n, int) and n == 0:
                                dve.tensor_tensor(out, gate[:, f % 2, :], ps_b[:, f, :], ALU.mult).then_inc(b_out, 1)
                            else:
                                dve.tensor_tensor(prod[:, f % 2, :], gate[:, f % 2, :], ps_b[:, f, :],
                                                  ALU.mult).then_inc(b_out, 1)
                                dve.wait_ge(b_out, at(n, j, 4, f + 1))
                                dve.tensor_tensor(out, out, prod[:, f % 2, :], ALU.add).then_inc(added, 1)
                over(dve, 3, body)
                for k in range(KT):
                    dve.wait_ge(hi_done, k + 1)
                    dve.tensor_tensor(g.xl[:, k, :], merged[:, k, :], g.xh[:, k, :].bitcast(F32),
                                      ALU.subtract).then_inc(lo_done, 1)


def stage_branch_out(g, a, layer, store):
    nc = g.nc
    w = a["w_out_2"][layer]
    with Stage(nc, f"bout{layer}") as st:
        ws = WeightStream(st)
        y, gain = st.sb("y", [P, TT, D]), st.sb("gain", [P, D])
        junk = st.sb("junk", [P, D])
        ms, root, inv = st.sb("ms", [P, TT]), st.sb("root", [P, TT]), st.sb("inv", [P, TT])
        ld, squared, rooted, inverted, scaled, added, stored = (st.sem(x) for x in
            ("loaded", "squared", "rooted", "inverted", "scaled", "added", "stored"))
        with nc.Block() as block:
            @block.sync
            def _(sp):
                sp.dma_start(gain[:], rows_of(a["post_g_2"], layer * D, D)).then_inc(ld, 16)
                over(sp, 2, lambda b: ws.load(sp, b, column_block(w, 0, b * 512)))
                if store is not None:
                    for t in range(TT):
                        sp.wait_ge(added, t + 1)
                        sp.dma_start(store[P * t:P * t + P, :], g.h[:, t, :]).then_inc(stored, 16)
                    sp.wait_ge(stored, 16 * TT)

            @block.tensor
            def _(pe):
                over(pe, 2, lambda b: ws.multiply(pe, b, g.xh, g.xl, False))

            @block.gpsimd
            def _(pool):
                over(pool, 2, lambda b: ws.split_lo(pool, b))

            @block.scalar
            def _(act):
                over(act, 2, lambda b: ws.split_hi(act, b))
                for t in range(TT):
                    act.wait_ge(ws.evicted, 4 + t + 1)
                    act.activation(junk[:], y[:, t, :], ACT.Square, accum_out=ms[:, t:t + 1]).then_inc(squared, 1)
                    act.wait_ge(squared, t + 1)
                act.activation(root[:], ms[:], ACT.Sqrt, scale=1.0 / D, bias=g.eps6[:]).then_inc(rooted, 1)

            @block.vector
            def _(dve):
                def body(b):
                    for t in range(TT):
                        dve.wait_ge(ws.acc_ready, b * 4 + (t + 1))
                        dve.tensor_copy(y[:, t, bass.ds(b * 512, 512)], ws.acc[:, t, :]).then_inc(ws.evicted, 1)
                over(dve, 2, body)
                dve.wait_ge(rooted, 1)
                dve.reciprocal(inv[:], root[:]).then_inc(inverted, 1)
                dve.wait_ge(inverted, 1)
                dve.wait_ge(ld, 16)
                for t in range(TT):
                    dve.scalar_tensor_tensor(y[:, t, :], y[:, t, :], inv[:, t:t + 1], gain[:],
                                             ALU.mult, ALU.mult).then_inc(scaled, 1)
                    dve.wait_ge(scaled, t + 1)
                    dve.tensor_tensor(g.h[:, t, :], g.h[:, t, :], y[:, t, :], ALU.add).then_inc(added, 1)


def branch_layer(g, a, layer, store, dumped):
    nc = g.nc
    with ExitStack() as part:
        def psb(name, shape, dt=F32, ctx=part):
            return ctx.enter_context(nc.sbuf_tensor(f"br{layer}_{name}", shape, dt))
        s = Globals()
        s.yh, s.yl = psb("yh", [P, 3 * BF, T], F32R), psb("yl", [P, 3 * BF, T], F32R)
        with ExitStack() as inner:
            xn = psb("xn", [P, TT, D], ctx=inner)
            stage_norm(g, f"pre{layer}", g.h, xn, (a["pre_g_2"], layer * D), None, GDN_EPS, False)
        s.t = {}
        with ExitStack() as inner:
            for x in ("u", "va", "za"):
                s.t[x] = psb(x, [P, BF, T], ctx=inner)
            stage_branch_project(g, a, layer, s, "a", [("va", False), ("u", True), ("za", True)])
            stage_spatial_gate(g, a, layer, s)
        with ExitStack() as inner:
            for x in ("qc", "kc", "vc", "zc"):
                s.t[x] = psb(x, [P, BF, T], ctx=inner)
            stage_branch_project(g, a, layer, s, "b", [("qc", True), ("kc", True), ("vc", False), ("zc", True)])
            stage_band_attend(g, a, layer, s)
        with ExitStack() as inner:
            s.t["zb"], s.t["mla"] = psb("zb", [P, BF, T], ctx=inner), psb("mla", [P, TT, MLA_COLS], ctx=inner)
            stage_branch_project(g, a, layer, s, "c", [("mla", False), ("zb", True)])
            s.mq, s.mk = psb("mq", [MLA_QK, MH, T], ctx=inner), psb("mk", [MLA_QK, MH, T], ctx=inner)
            s.mv = psb("mv", [P, TT, MH * 64], ctx=inner)
            stage_latent(g, a, layer, s)
            stage_latent_attend(g, a, layer, s)
        dumped(f"yh{layer}", s.yh[:].bitcast(F32))
        stage_merge(g, a, layer, s)
    stage_branch_out(g, a, layer, store)


class Globals:
    pass


def consts():
    i = np.arange(P)
    c = {}
    c["c_ident"] = np.eye(P, dtype=np.float32)
    c["c_ones"] = np.ones((P, P), np.float32)
    c["c_triu"] = (i[:, None] <= i[None, :]).astype(np.float32)
    c["c_neg_below"] = np.where(i[:, None] > i[None, :], np.float32(NEG), np.float32(0))
    sel = np.zeros((16, 16, P), np.float32)
    for r in range(16):
        sel[r, r, :] = 1
    c["c_sel"] = sel
    lev = np.zeros((LEVELS, P, P), np.float32)
    for l in range(LEVELS):
        s = 1 << l
        same = (i[:, None] // (2 * s)) == (i[None, :] // (2 * s))
        lev[l] = same & ((i[:, None] // s) % 2 == 0) & ((i[None, :] // s) % 2 == 1)
    c["c_levels"] = lev
    c["c_striu"] = (i[:, None] < i[None, :]).astype(np.float32)
    c["c_desc"] = np.arange(4, 0, -1, dtype=np.float32)[None]
    c["c_iota"] = np.tile(i.astype(np.float32), (P, 1))
    c["c_iota_b"] = np.tile(np.arange(MAX_BLOCKS, dtype=np.float32)[None, :, None], (1, 1, N_EXP))
    dist = np.arange(NSA_ROW) - T
    near = np.maximum(dist, 0)
    far = np.maximum(near, 1).astype(np.float32)
    large = 16 + (np.log(far / np.float32(16)) / np.float32(math.log(128 / 16)) * np.float32(16)).astype(np.int32)
    bucket = np.where(near < 16, near, np.minimum(large, 31))
    c["c_t5_onehot"] = (bucket[None, :] == np.arange(32)[:, None]).astype(np.float32) * (dist >= 0)
    c["c_t5_onehot"] = c["c_t5_onehot"].astype(np.float32)
    c["c_t5_mask"] = np.where(dist < 0, np.float32(-NEG), np.float32(0))[None].astype(np.float32)
    tq = np.arange(TT)[None, :, None] * P + i[:, None, None]
    c["c_cmp_valid"] = (np.arange(N_CMP)[None, None, :] * 16 + 31 <= tq).astype(np.float32)
    bb = np.zeros((P, T), np.float32)
    bb[:64, :64] = -NEG
    c["c_block_bias"] = bb
    half = MLA_ROPE // 2
    inv = np.float32(10000.0) ** (-np.arange(half, dtype=np.float32) / np.float32(half))
    ang = (np.arange(T, dtype=np.float32)[:, None] * inv[None, :]).astype(np.float32)
    cos, sin = np.cos(ang).astype(np.float32), np.sin(ang).astype(np.float32)
    c["c_rope_cos"] = np.ascontiguousarray(cos.reshape(TT, P, half).transpose(1, 0, 2))
    c["c_rope_sin"] = np.ascontiguousarray(sin.reshape(TT, P, half).transpose(1, 0, 2))
    scale = np.float32(-MLA_SCALE)
    c["c_ropeq_cos"] = np.tile(np.concatenate([cos.T, cos.T]) * scale, (4, 1))
    c["c_ropeq_sin"] = np.tile(np.concatenate([-sin.T, sin.T]) * scale, (4, 1))
    return c


def nsa_layer(g, a):
    nc = g.nc
    stage_tables(g, a)
    with ExitStack() as part:
        n = Globals()

        def psb(name, shape):
            return part.enter_context(nc.sbuf_tensor("nsa_" + name, shape, F32))
        n.qt, n.kt = psb("qt", [P, NSA_H // 2, T]), psb("kt", [P, 2, NSA_G, T])
        n.v, n.gate = psb("v", [P, TT, 2 * NSA_G * DH]), psb("gate", [P, TT, 3 * NSA_H])
        n.kct, n.vc = psb("kct", [P, NSA_G, N_CMP]), psb("vc", [N_CMP, NSA_G, DH])
        with ExitStack() as inner:
            n.raw = inner.enter_context(nc.sbuf_tensor("nsa_raw", [P, 4, T], F32))
            stage_nsa_project(g, a, n)
            stage_nsa_compress(g, a, n)
        n.pct = psb("pct", [N_CMP, NSA_H, T])
        stage_nsa_cmp(g, a, n)
        stage_nsa_attend(g, a, n)
    stage_out_proj(g, "nwo", a["nsa_w_o"][0], ALPHA)
    stage_norm(g, "ln1", g.h, g.h, (a["ln_mix_g"], D), (a["ln_mix_b"], D), LN_EPS, True)


def moe_layer(g, a, layer):
    nc = g.nc
    with ExitStack() as part:
        rt = Globals()

        def psb(name, shape, dt=F32):
            return part.enter_context(nc.sbuf_tensor(f"rt{layer}_{name}", shape, dt))
        rt.slot, rt.slot_i, rt.weight = psb("slot", [P, TT, 2]), psb("slot_i", [P, TT, 2], I32), psb("weight", [P, TT, 2])
        rt.table = psb("table", [1, 24], I32)
        rt.hh, rt.hl = g.xh[:].rearrange("p (t a) n -> p t (a n)", t=TT), g.xl[:].rearrange("p (t a) n -> p t (a n)", t=TT)
        rt.rows_back = psb("rows_back", [P, 2, TT, D])
        stage_route(g, f"route{layer}", a, layer, rt)
        stage_experts(g, f"exp{layer}", a, layer, rt)
    stage_norm(g, f"ffn_ln{layer}", g.h, g.h, (a["ln_ffn_g"], layer * D), (a["ln_ffn_b"], layer * D), LN_EPS, True)


def program(nc, a, dump=None, stop=None):
    with ExitStack() as ctx:
        g = Globals()
        g.nc = nc

        def sb(name, shape, dt=F32):
            return ctx.enter_context(nc.sbuf_tensor(name, shape, dt))
        g.h = sb("h", [P, TT, D])
        g.xh, g.xl = sb("xh", [P, KT, T], F32R), sb("xl", [P, KT, T], F32R)
        g.ident, g.ones, g.triu, g.neg_below, g.striu = (sb(n, [P, P]) for n in
                                                        ("ident", "ones", "triu", "neg_below", "striu"))
        g.moe_rows = nc.dram_tensor("moe_rows", (MAX_BLOCKS * P, D), F32, kind="Internal").ap()
        g.nsa_rows = nc.dram_tensor("nsa_rows", (NSA_H, NSA_ROW), F32, kind="Internal").ap()
        g.ca_rows = nc.dram_tensor("ca_rows", (16, CA_ROW), F32, kind="Internal").ap()
        g.eps5, g.eps6 = sb("eps5", [P, 1]), sb("eps6", [P, 1])
        g.row = lambda r, n: g.sel[0:n, r, :]
        g.colsel = sb("colsel", [P, 31])
        g.column = lambda r, n: g.colsel[:, 15 - r:15 - r + n]

        with Stage(nc, "eps") as st:
            s, s2 = st.sem("set"), st.sem("cleared")
            with nc.Block() as block:
                @block.gpsimd
                def _(pool):
                    pool.memset(g.eps5[:], LN_EPS).then_inc(s, 1)
                    pool.memset(g.eps6[:], GDN_EPS).then_inc(s, 1)
                    pool.memset(g.colsel[:], 0.0).then_inc(s2, 1)
                    pool.wait_ge(s2, 1)
                    pool.memset(g.colsel[:, 15:16], 1.0).then_inc(s, 1)

        def dumped(name, ap):
            if dump and name in dump:
                with Stage(nc, "dump_" + name) as st:
                    s = st.sem("s")
                    with nc.Block() as block:
                        @block.sync
                        def _(sp):
                            sp.dma_start(a["dump_" + name], ap).then_inc(s, 16)
                            sp.wait_ge(s, 16)

        stage_load(g, a)
        with ExitStack() as part:
            def psb(name, shape, dt=F32):
                return part.enter_context(nc.sbuf_tensor(name, shape, dt))
            qkvz = psb("qkvz", [P, 4 * GDN_H, T])
            ab = psb("ab", [P, TT, 16])
            gt = {x: psb("gt_" + x, [P, TT * GDN_H]) for x in
                  ("g", "beta", "neg_gc", "gl", "egc", "beta_egc", "rest", "tmp", "dlast", "krest")}
            g.sel = psb("sel", [16, 16, P])
            stage_gdn_project(g, a, qkvz, ab)
            dumped("qkvz", qkvz[:])
            stage_gdn_norm(g, a, qkvz)
            dumped("qkn", qkvz[:])
            stage_gdn_gates(g, a, ab, gt)
            with ExitStack() as inner:
                qk_t = inner.enter_context(nc.sbuf_tensor("qk_t", [P, GDN_H, T], F32))
                k_dec = inner.enter_context(nc.sbuf_tensor("k_dec", [P, GDN_H, T], F32))
                stage_gdn_chunks(g, a, qkvz, gt, qk_t, k_dec)
                dumped("chunk", qkvz[:])
                stage_gdn_scan(g, a, qkvz, gt, qk_t, k_dec)
                dumped("scan", qkvz[:])
            stage_gdn_out(g, a, qkvz)
        stage_out_proj(g, "gwo", a["gdn_w_o"][0], ALPHA)
        stage_norm(g, "ln0", g.h, g.h, (a["ln_mix_g"], 0), (a["ln_mix_b"], 0), LN_EPS, True)
        dumped("h0", g.h[:])
        moe_layer(g, a, 0)
        dumped("h1", g.h[:])
        nsa_layer(g, a)
        dumped("h2", g.h[:])
        moe_layer(g, a, 1)
        dumped("h3", g.h[:])
        for layer in range(2):
            branch_layer(g, a, layer, a["out"][0] if layer == 1 else None, dumped)
            dumped(f"x{layer}", g.h[:])


IN_NAMES = [
    "x", "gdn_w_in", "gdn_conv_w", "gdn_a_log", "gdn_dt_bias", "gdn_norm_w", "gdn_w_o", "nsa_w_kv", "cmp_k_pos",
    "cmp_k_w1", "cmp_k_w2", "cmp_v_pos", "cmp_v_w1", "cmp_v_w2", "nsa_w_in", "nsa_w_o", "rel_bias", "ln_mix_g",
    "ln_mix_b", "ln_ffn_g", "ln_ffn_b", "moe_w_grp", "moe_b_grp", "moe_w_rt", "moe_b_rt", "moe_w_gate",
    "moe_w_up", "moe_w_down", "w_in_2", "pre_g_2", "post_g_2", "sgu_ln_g_2", "sgu_ln_b_2", "sgu_w_2", "sgu_b_2",
    "mla_q_norm_g_2", "mla_kv_norm_g_2", "mla_w_uq_2", "mla_w_ukv_2", "ca_rel_bias_2", "w_branch_2",
    "gate_b_2", "w_out_2",
]


def kernel(**inputs):
    import concourse.bacc as bacc
    from concourse.bass_utils import run_bass_kernel_spmd

    nc = bacc.Bacc("TRN2", target_bir_lowering=False, num_devices=1)
    arrays = {name: np.ascontiguousarray(inputs[name]) for name in IN_NAMES}
    arrays.update(consts())
    a = {name: nc.dram_tensor(name, x.shape, mybir.dt.from_np(x.dtype), kind="ExternalInput").ap()
         for name, x in arrays.items()}
    a["out"] = nc.dram_tensor("out", (1, T, D), F32, kind="ExternalOutput").ap()
    program(nc, a)
    result = run_bass_kernel_spmd(nc, [arrays], core_ids=[0])
    return result.results[0]["out"]
```

```python
import math
from contextlib import ExitStack

import concourse.bass as bass
import numpy as np
from concourse import mybir

F32 = mybir.dt.float32
F32R = mybir.dt.float32r
I32 = mybir.dt.int32
U32 = mybir.dt.uint32
ALU = mybir.AluOpType
ACT = mybir.ActivationFunctionType
AX = mybir.AxisListType

P = 128
T = 512
TT = T // P
D = 1024
KT = D // P
HALF = KT // 2
NEG = -1e30

GDN_H = 8
GDN_EPS = 1e-6
LN_EPS = 1e-5
ALPHA = 4 ** 0.25
LEVELS = 7

NSA_H = 16
NSA_G = 4
DH = 64
N_CMP = (T - 32) // 16 + 1

N_EXP = 16
HID = 256


class Stage:

    def __init__(self, nc, name):
        self.nc, self.name, self.sems, self.ctx = nc, name, [], ExitStack()

    def sem(self, name):
        s = self.nc.alloc_semaphore(f"{self.name}_{name}")
        self.sems.append(s)
        return s

    def sb(self, name, shape, dt=F32):
        return self.ctx.enter_context(self.nc.sbuf_tensor(f"{self.name}_{name}", shape, dt))

    def ps(self, name, banks):
        return self.ctx.enter_context(self.nc.psum_tensor(f"{self.name}_{name}", [P, banks, 512], F32))

    def __enter__(self):
        return self

    def __exit__(self, *e):
        if e[0] is None:
            self.nc.clear_and_free_semaphores(self.sems)
            self.nc.all_engine_barrier()
        self.ctx.close()
        return False


class Link:

    def __init__(self, eng, sem):
        self.eng, self.sem, self.n = eng, sem, 0

    def __call__(self, *instructions):
        for ins in instructions:
            ins.then_inc(self.sem, 1)
            self.n += 1
        self.eng.wait_ge(self.sem, self.n)


def rows_of(ap, start, n, repeat=P):
    return bass.AP(ap.tensor, ap.offset + start, [[0, repeat], [1, n]])


def over(eng, n, body):
    body(0)
    if n > 1:
        with eng.Fori(1, n) as i:
            body(i)


class WeightSlots:

    def __init__(self, st):
        self.f = [st.sb(f"wf{u}", [P, HALF, 512]) for u in range(2)]
        self.h = [st.sb(f"wh{u}", [P, HALF, 512], F32R) for u in range(2)]
        self.l = [st.sb(f"wl{u}", [P, HALF, 512], F32R) for u in range(2)]
        self.loaded = [st.sem(f"w_loaded{u}") for u in range(2)]
        self.hi_ready = st.sem("w_hi_ready")
        self.lo_ready = st.sem("w_lo_ready")
        self.blocks, self.loads = 0, 0


class WeightRun:

    def __init__(self, slots, n, src, parts=1, cols=lambda b: 512):
        self.s, self.n, self.src, self.parts, self.cols = slots, n, src, parts, cols
        self.h, self.l = slots.h, slots.l
        self.base, self.load_base = slots.blocks, slots.loads
        slots.blocks += n
        slots.loads += 16 * parts * n

    def attach(self, st, banks=4):
        self.acc = st.ps("acc", banks) if banks else None
        self.unit0_used, self.acc_ready, self.evicted = st.sem("w_unit0_used"), st.sem("acc_ready"), st.sem("acc_evicted")
        return self

    def load(self, sp, b):
        for u in range(2):
            if not (isinstance(b, int) and self.base + b == 0):
                sp.wait_ge(self.s.lo_ready, (b - 1) * 2 + (2 * self.base + u + 1))
            for col, ap in self.src(b)(u):
                sp.dma_start(self.s.f[u][:, :, col:col + ap.shape[2]], ap).then_inc(self.s.loaded[u], 16)

    def hi(self, act, b, u, before=None):
        act.wait_ge(self.s.loaded[u], b * (16 * self.parts) + (self.load_base + 16 * self.parts))
        if before is not None:
            act.wait_ge(before.unit0_used if u == 0 else before.acc_ready, before.n * (1 if u == 0 else 4))
        elif not (isinstance(b, int) and b == 0):
            if u == 0:
                act.wait_ge(self.unit0_used, b)
            else:
                act.wait_ge(self.acc_ready, b * 4)
        act.activation(self.h[u][:, :, 0:self.cols(b)], self.s.f[u][:, :, 0:self.cols(b)],
                       ACT.Copy).then_inc(self.s.hi_ready, 1)

    def lo(self, pool, b, units=(0, 1)):
        for u in units:
            pool.wait_ge(self.s.hi_ready, b * 2 + (2 * self.base + u + 1))
            pool.tensor_tensor(self.l[u][:, :, 0:self.cols(b)], self.s.f[u][:, :, 0:self.cols(b)],
                               self.h[u][:, :, 0:self.cols(b)].bitcast(F32),
                               ALU.subtract).then_inc(self.s.lo_ready, 1)

    def unit_ready(self, pe, b, u):
        pe.wait_ge(self.s.lo_ready, b * 2 + (2 * self.base + u + 1))

    def load_first(self, sp):
        self.load(sp, 0)

    def hi_first(self, act, before=None):
        self.hi(act, 0, 0, before)

    def lo_first(self, pool):
        self.lo(pool, 0, (0,))

    def load_rest(self, sp):
        with sp.Fori(1, self.n) as b:
            self.load(sp, b)

    def hi_rest(self, act):
        self.hi(act, 0, 1)
        with act.Fori(1, self.n) as b:
            for u in range(2):
                self.hi(act, b, u)

    def lo_rest(self, pool):
        self.lo(pool, 0, (1,))
        with pool.Fori(1, self.n) as b:
            self.lo(pool, b)

    def multiply(self, pe, b, xh, xl, weights_stationary, cols=512):
        for u in range(2):
            self.unit_ready(pe, b, u)
            for s in range(4):
                if u == 0 and not (isinstance(b, int) and b == 0):
                    pe.wait_ge(self.evicted, (b - 1) * 4 + (s + 1))
                for k in range(HALF):
                    for n, (w, x) in enumerate(((self.h, xh), (self.h, xl), (self.l, xh))):
                        wk, xk = w[u][:, k, :], x[:, HALF * u + k, :]
                        lhs, rhs = (wk, xk) if weights_stationary else (xk, wk[:, 0:cols])
                        mm = pe.matmul(self.acc[:, s, 0:cols], lhs[:, P * s:P * s + P], rhs,
                                       start=(u == 0 and k == 0 and n == 0),
                                       stop=(u == 1 and k == HALF - 1 and n == 2))
                if u == 1:
                    mm.then_inc(self.acc_ready, 1)
            if u == 0:
                mm.then_inc(self.unit0_used, 1)


class NarrowProduct:

    def __init__(self, g, st, n):
        self.g, self.n = g, n
        self.w, self.wh, self.wl = st.sb("nw", [P, KT, n]), st.sb("nwh", [P, KT, n], F32R), st.sb("nwl", [P, KT, n], F32R)
        self.y = st.sb("ny", [n, T])
        self.banks = st.ps("narrow", 2)
        self.out = self.banks[:, 1, 0:TT * n]
        self.loaded, self.hi, self.lo = st.sem("nw_loaded"), st.sem("nw_hi"), st.sem("nw_lo")
        self.acc_done, self.y_done, self.turned = st.sem("n_acc"), st.sem("n_copied"), st.sem("n_turned")

    def split(self, dve, count):
        dve.wait_ge(self.loaded, count)
        dve.tensor_copy(self.wh[:], self.w[:]).then_inc(self.hi, 1)
        dve.wait_ge(self.hi, 1)
        dve.tensor_tensor(self.wl[:], self.w[:], self.wh[:].bitcast(F32), ALU.subtract).then_inc(self.lo, 1)

    def multiply(self, pe):
        pe.wait_ge(self.lo, 1)
        for k in range(KT):
            for m, (w, x) in enumerate(((self.wh, self.g.xh), (self.wh, self.g.xl), (self.wl, self.g.xh))):
                mm = pe.matmul(self.banks[0:self.n, 0, :], w[:, k, :], x[:, k, :],
                               start=(k == 0 and m == 0), stop=(k == KT - 1 and m == 2))
        mm.then_inc(self.acc_done, 1)

    def copy(self, dve):
        dve.wait_ge(self.acc_done, 1)
        dve.tensor_copy(self.y[:], self.banks[0:self.n, 0, :]).then_inc(self.y_done, 1)

    def turn(self, pe):
        pe.wait_ge(self.y_done, 1)
        for t in range(TT):
            mm = pe.transpose(self.banks[:, 1, self.n * t:self.n * t + self.n], self.y[:, P * t:P * t + P],
                              self.g.ident[0:self.n, 0:self.n])
        mm.then_inc(self.turned, 1)


def column_block(w, row0, col):
    def src(u):
        part = w[row0 + HALF * P * u:row0 + HALF * P * (u + 1), bass.ds(col, 512)]
        return [(0, part.rearrange("(k p) n -> p k n", p=P))]
    return src


def to_feature_major(g, st, src, pe_after, act_after=None):
    banks = st.ps("turn", 8)
    turned, hi_done, lo_done = st.sem("turned"), st.sem("turn_hi"), st.sem("turn_lo")

    def pe_part(pe):
        pe_after(pe)
        for k in range(KT):
            for t in range(TT):
                mm = pe.transpose(banks[:, k, P * t:P * t + P], src[:, t, P * k:P * k + P], g.ident[:])
            mm.then_inc(turned, 1)

    def act_part(act):
        for k in range(KT):
            act.wait_ge(turned, k + 1)
            act.activation(g.xh[:, k, :], banks[:, k, :], ACT.Copy).then_inc(hi_done, 1)

    def dve_part(dve):
        for k in range(KT):
            dve.wait_ge(hi_done, k + 1)
            dve.tensor_tensor(g.xl[:, k, :], banks[:, k, :], g.xh[:, k, :].bitcast(F32),
                              ALU.subtract).then_inc(lo_done, 1)
    return pe_part, act_part, dve_part


def stage_load(g, a, nxt):
    nc = g.nc
    with Stage(nc, "load") as st:
        ld = st.sem("loaded")
        turn = to_feature_major(g, st, g.h, lambda pe: pe.wait_ge(ld, 16 * 6))
        with nc.Block() as block:
            @block.sync
            def _(sp):
                sp.dma_start(g.h[:], a["x"][0].rearrange("(t p) d -> p t d", p=P)).then_inc(ld, 16)
                sp.dma_start(g.ident[:], a["c_ident"]).then_inc(ld, 16)
                sp.dma_start(g.ones[:], a["c_ones"]).then_inc(ld, 16)
                sp.dma_start(g.triu[:], a["c_triu"]).then_inc(ld, 16)
                sp.dma_start(g.neg_below[:], a["c_neg_below"]).then_inc(ld, 16)
                sp.dma_start(g.striu[:], a["c_striu"]).then_inc(ld, 16)
                nxt.load_first(sp)

            @block.gpsimd
            def _(pool):
                nxt.lo_first(pool)

            @block.tensor
            def _(pe):
                turn[0](pe)

            @block.scalar
            def _(act):
                turn[1](act)
                nxt.hi_first(act)

            @block.vector
            def _(dve):
                turn[2](dve)


def stage_gdn_project(g, a, run, qkvz, ab):
    nc = g.nc
    w_in = a["gdn_w_in"][0]
    with Stage(nc, "gproj") as st:
        ws = run.attach(st)
        narrow = NarrowProduct(g, st, 16)
        convw = st.sb("convw", [P, 24, 4])
        padded = [st.sb(f"padded{i}", [P, 3 + T]) for i in range(2)]
        mixed = [st.sb(f"mixed{i}", [P, T]) for i in range(2)]
        zeros, zero_stored = st.sb("zeros", [P, D]), st.sem("zero_stored")
        ld, zero = st.sem("small_loaded"), st.sem("zeroed")
        conv_done, silu_done, step = st.sem("conv_done"), st.sem("silu_done"), st.sem("conv_step")
        ab_done = st.sem("ab_done")
        with nc.Block() as block:
            @block.sync
            def _(sp):
                sp.dma_start(narrow.w[:], w_in[:, 4096:4112].rearrange("(k p) n -> p k n", p=P)).then_inc(narrow.loaded, 16)
                for j in range(4):
                    sp.dma_start(convw[:, :, j], a["gdn_conv_w"][0][j].rearrange("(f p) -> p f", p=P),
                                 allow_slow_non_contiguous=True).then_inc(ld, 16)
                ws.load_rest(sp)
                sp.wait_ge(zero, 3)
                sp.dma_start(g.moe_rows.rearrange("(b p) d -> p b d", p=P),
                             zeros[:].unsqueeze(1).to_broadcast([P, MAX_BLOCKS, D])).then_inc(zero_stored, 16)
                sp.wait_ge(zero_stored, 16)

            @block.tensor
            def _(pe):
                narrow.multiply(pe)
                narrow.turn(pe)
                over(pe, 8, lambda b: ws.multiply(pe, b, g.xh, g.xl, True))

            @block.gpsimd
            def _(pool):
                for i in range(2):
                    pool.memset(padded[i][:, 0:3], 0.0).then_inc(zero, 1)
                pool.memset(zeros[:], 0.0).then_inc(zero, 1)
                ws.lo_rest(pool)

            @block.scalar
            def _(act):
                def conv_block(b):
                    ws.hi(act, b + 1, 0)
                    for s in range(4):
                        act.wait_ge(ws.acc_ready, b * 4 + (s + 1))
                        if not (isinstance(b, int) and b == 0 and s < 2):
                            act.wait_ge(conv_done, b * 4 + (s - 1))
                        act.activation(padded[s % 2][:, 3:3 + T], ws.acc[:, s, :],
                                       ACT.Copy).then_inc(ws.evicted, 1)
                        if s > 0:
                            act.wait_ge(conv_done, b * 4 + s)
                            act.activation(qkvz[:, bass.ds(b * 4 + (s - 1), 1), :].rearrange("p a n -> p (a n)"),
                                           mixed[(s - 1) % 2][:], ACT.Silu).then_inc(silu_done, 1)
                    ws.hi(act, b + 1, 1)
                    act.wait_ge(conv_done, b * 4 + 4)
                    act.activation(qkvz[:, bass.ds(b * 4 + 3, 1), :].rearrange("p a n -> p (a n)"),
                                   mixed[1][:], ACT.Silu).then_inc(silu_done, 1)

                ws.hi(act, 0, 1)
                over(act, 6, conv_block)
                for b in (6, 7):
                    if b == 6:
                        ws.hi(act, 7, 0)
                    for s in range(4):
                        act.wait_ge(ws.acc_ready, b * 4 + (s + 1))
                        act.activation(qkvz[:, b * 4 + s, :], ws.acc[:, s, :],
                                       ACT.Silu).then_inc(ws.evicted, 1)
                    if b == 6:
                        ws.hi(act, 7, 1)

            @block.vector
            def _(dve):
                narrow.split(dve, 16)
                narrow.copy(dve)
                dve.wait_ge(narrow.turned, 1)
                dve.tensor_copy(ab[:].rearrange("p t n -> p (t n)"), narrow.out).then_inc(ab_done, 1)
                dve.wait_ge(zero, 3)
                dve.wait_ge(ld, 16 * 4)

                def conv_block(b):
                    for s in range(4):
                        dve.wait_ge(ws.evicted, b * 4 + (s + 1))
                        if not (isinstance(b, int) and b == 0 and s < 2):
                            dve.wait_ge(silu_done, b * 4 + (s - 1))
                        x, y = padded[s % 2], mixed[s % 2]
                        w = convw[:, bass.ds(b * 4 + s, 1), :].rearrange("p a n -> p (a n)")
                        dve.tensor_scalar(y[:], x[:, 0:T], w[:, 0:1], None, ALU.mult).then_inc(step, 1)
                        for j in range(1, 4):
                            dve.wait_ge(step, b * 12 + (3 * s + j))
                            ins = dve.scalar_tensor_tensor(y[:], x[:, j:j + T], w[:, j:j + 1], y[:],
                                                           ALU.mult, ALU.add)
                            ins.then_inc(step if j < 3 else conv_done, 1)
                over(dve, 6, conv_block)


def stage_gdn_norm(g, a, qkvz):
    nc = g.nc
    n = 2 * GDN_H
    with Stage(nc, "gnorm") as st:
        sq = [st.sb(f"sq{i}", [P, T]) for i in range(2)]
        rows, spread = st.ps("rows", 1), st.ps("spread", 4)
        root, inv = st.sb("root", [n, T]), st.sb("inv", [n, T])
        squared, summed, rooted = st.sem("squared"), st.sem("summed"), st.sem("rooted")
        inverted, spread_done, used = st.sem("inverted"), st.sem("spread_done"), st.sem("spread_used")
        sel_loaded, sel_ready, inv_step = st.sem("sel_loaded"), st.sem("sel_ready"), st.sem("inv_step")
        sel = st.sb("sel", [16, 16, P])
        invh, invl = st.sb("invh", [n, T], F32R), st.sb("invl", [n, T], F32R)
        with nc.Block() as block:
            @block.sync
            def _(sp):
                sp.dma_start(sel[:], a["c_sel"]).then_inc(sel_loaded, 16)

            @block.scalar
            def _(act):
                for r in range(n):
                    if r >= 2:
                        act.wait_ge(summed, r - 1)
                    act.activation(sq[r % 2][:], qkvz[:, r, :], ACT.Square).then_inc(squared, 1)
                act.wait_ge(summed, n)
                act.activation(root[:], rows[0:n, 0, :], ACT.Sqrt, bias=g.eps6[0:n, :]).then_inc(rooted, 1)

            @block.tensor
            def _(pe):
                for r in range(n):
                    pe.wait_ge(squared, r + 1)
                    pe.matmul(rows[0:n, 0, :], g.column(r, n), sq[r % 2][:],
                              start=(r == 0), stop=(r == n - 1)).then_inc(summed, 1)
                pe.wait_ge(inverted, 1)
                pe.wait_ge(sel_ready, 1)
                for r in range(n):
                    if r >= 4:
                        pe.wait_ge(used, r - 3)
                    pe.matmul(spread[:, r % 4, :], g.row(r, n), invh[:], start=True, stop=False)
                    pe.matmul(spread[:, r % 4, :], g.row(r, n), invl[:],
                              start=False, stop=True).then_inc(spread_done, 1)

            @block.vector
            def _(dve):
                dve.wait_ge(sel_loaded, 16)
                dve.tensor_copy(g.sel[:], sel[:]).then_inc(sel_ready, 1)
                dve.wait_ge(rooted, 1)
                link = Link(dve, inv_step)
                link(dve.reciprocal(inv[:], root[:]))
                link(dve.tensor_copy(invh[:], inv[:]))
                dve.tensor_tensor(invl[:], inv[:], invh[:].bitcast(F32), ALU.subtract).then_inc(inverted, 1)
                for r in range(n):
                    dve.wait_ge(spread_done, r + 1)
                    dve.scalar_tensor_tensor(qkvz[:, r, :], qkvz[:, r, :],
                                             P ** -0.5 if r < GDN_H else 1.0, spread[:, r % 4, :],
                                             ALU.mult, ALU.mult).then_inc(used, 1)


def stage_gdn_gates(g, a, ab, gt):
    nc = g.nc
    n = TT * GDN_H
    with Stage(nc, "ggate") as st:
        bias, alog = st.sb("bias", [P, GDN_H]), st.sb("alog", [P, GDN_H])
        ea, a1, neg, ab_s, sp_ = (st.sb(x, [P, n]) for x in ("ea", "a1", "neg", "abs", "sp"))
        e1, e2 = st.sb("e1", [P, n]), st.sb("e2", [P, n])
        cum = st.ps("cum", 1)
        ld, link_a, link_v = st.sem("loaded"), st.sem("act_step"), st.sem("dve_step")
        v_abs, a_ln, a_ea, v_g = st.sem("v_abs"), st.sem("a_ln"), st.sem("a_ea"), st.sem("v_g")
        p_cum, v_cum, done = st.sem("p_cum"), st.sem("v_cum"), st.sem("done")
        a_in = ab[:, :, 0:GDN_H]
        b_in = ab[:, :, GDN_H:2 * GDN_H]
        def v3(t):
            return t[:].rearrange("p (t h) -> p t h", h=GDN_H)
        with nc.Block() as block:
            @block.sync
            def _(sp):
                sp.dma_start(bias[:], rows_of(a["gdn_dt_bias"], 0, GDN_H)).then_inc(ld, 16)
                sp.dma_start(alog[:], rows_of(a["gdn_a_log"], 0, GDN_H)).then_inc(ld, 16)

            @block.vector
            def _(dve):
                link = Link(dve, link_v)
                dve.wait_ge(ld, 32)
                link(dve.tensor_tensor(v3(a1), a_in, bias[:].unsqueeze(1).to_broadcast([P, TT, GDN_H]), ALU.add))
                link(dve.tensor_scalar(neg[:], a1[:], -1.0, None, ALU.mult))
                dve.tensor_tensor(ab_s[:], a1[:], neg[:], ALU.max).then_inc(v_abs, 1)
                dve.wait_ge(a_ln, 1)
                link(dve.scalar_tensor_tensor(sp_[:], a1[:], 0.0, e2[:], ALU.max, ALU.add))
                dve.wait_ge(a_ea, 2)
                dve.scalar_tensor_tensor(v3(gt["g"]), v3(sp_), -1.0,
                                         ea[:, 0:GDN_H].unsqueeze(1).to_broadcast([P, TT, GDN_H]),
                                         ALU.mult, ALU.mult).then_inc(v_g, 1)
                link(dve.tensor_scalar(e1[:], e1[:], 1.0, None, ALU.add))
                link(dve.reciprocal(gt["beta"][:], e1[:]))
                dve.wait_ge(p_cum, 1)
                link(dve.tensor_scalar(gt["neg_gc"][:], cum[:, 0, 0:n], -1.0, None, ALU.mult))
                dve.tensor_copy(gt["gl"][:], cum[:, 0, n:2 * n]).then_inc(v_cum, 1)
                dve.wait_ge(done, 2)
                link(dve.tensor_tensor(gt["beta_egc"][:], gt["beta"][:], gt["egc"][:], ALU.mult))
                dve.wait_ge(v_cum, 1)
                link(dve.tensor_tensor(gt["rest"][:], gt["gl"][:], gt["neg_gc"][:], ALU.add))
                dve.tensor_copy(gt["tmp"][:], gt["rest"][:]).then_inc(v_cum, 1)

            @block.scalar
            def _(act):
                act.wait_ge(ld, 32)
                act.activation(ea[:, 0:GDN_H], alog[:], ACT.Exp).then_inc(a_ea, 1)
                act.activation(v3(e1), b_in, ACT.Exp, scale=-1.0).then_inc(a_ea, 1)
                act.wait_ge(v_abs, 1)
                act.activation(e2[:], ab_s[:], ACT.Exp, scale=-1.0).then_inc(link_a, 1)
                act.wait_ge(link_a, 1)
                act.activation(e2[:], e2[:], ACT.Ln, bias=1.0).then_inc(a_ln, 1)
                act.wait_ge(v_cum, 1)
                act.activation(gt["egc"][:], gt["neg_gc"][:], ACT.Exp, scale=-1.0).then_inc(done, 1)
                act.activation(gt["dlast"][:], gt["gl"][:], ACT.Exp).then_inc(done, 1)
                act.wait_ge(v_cum, 2)
                act.activation(gt["krest"][:], gt["tmp"][:], ACT.Exp).then_inc(done, 1)

            @block.tensor
            def _(pe):
                pe.wait_ge(v_g, 1)
                pe.matmul(cum[:, 0, 0:n], g.triu[:], gt["g"][:], start=True, stop=True)
                pe.matmul(cum[:, 0, n:2 * n], g.ones[:], gt["g"][:], start=True, stop=True).then_inc(p_cum, 1)


def stage_gdn_chunks(g, a, qkvz, gt, qk_t, k_dec):
    nc = g.nc
    with Stage(nc, "gchunk") as st:
        levels = st.sb("levels", [P, LEVELS, P])
        NB = 2
        B = [{x: st.sb(f"{x}{i}", [P, TT, P]) for x in
              ("dec", "decb", "eg", "at", "m", "x", "tm", "um", "kbg", "vb")} for i in range(NB)]
        ps = [st.ps(f"ps{i}", 4) for i in range(NB)]
        ld = st.sem("loaded")
        pe_done = [st.sem(f"pe_done{i}") for i in range(NB)]
        act_done = [st.sem(f"act_done{i}") for i in range(NB)]
        dve_done = [st.sem(f"dve_done{i}") for i in range(NB)]
        L = LEVELS - 1
        N_PE, N_ACT, N_DVE = 6 + (3 * L - 1) + 1, 9 + L, 8 + (3 * L - 1) + 2
        def flat(ap):
            return ap.rearrange("p c n -> p (c n)")

        with nc.Block() as block:
            @block.sync
            def _(sp):
                sp.dma_start(levels[:], a["c_levels"].rearrange("l p n -> p l n")).then_inc(ld, 16)

            @block.tensor
            def _(pe):
                def bank(i, j, c):
                    return ps[i][:, j, P * c:P * c + P]

                def front(h, i, r):
                    q, k = qkvz[:, h, :], qkvz[:, GDN_H + h, :]
                    if r:
                        pe.wait_ge(dve_done[i], N_DVE * r)
                        pe.wait_ge(act_done[i], N_ACT * r)
                    for c in range(TT):
                        col = GDN_H * c + h
                        mm = pe.matmul(bank(i, 0, c), gt["g"][:, col:col + 1].to_broadcast([P, P]), g.triu[:],
                                       start=True, stop=True)
                    mm.then_inc(pe_done[i], 1)
                    for c in range(TT):
                        col = GDN_H * c + h
                        mm = pe.matmul(bank(i, 1, c), gt["beta"][:, col:col + 1].to_broadcast([P, P]), g.ident[:],
                                       start=True, stop=True)
                    mm.then_inc(pe_done[i], 1)
                    for c in range(TT):
                        kc = k[:, P * c:P * c + P]
                        mm = pe.matmul(bank(i, 2, c), kc, kc, start=True, stop=True)
                    mm.then_inc(pe_done[i], 1)
                    for c in range(TT):
                        mm = pe.matmul(bank(i, 3, c), k[:, P * c:P * c + P], q[:, P * c:P * c + P],
                                       start=True, stop=True)
                    mm.then_inc(pe_done[i], 1)

                def first_level(h, i, r):
                    b = B[i]
                    pe.wait_ge(dve_done[i], N_DVE * r + 7)
                    for c in range(TT):
                        mm = pe.matmul(bank(i, 0, c), b["m"][:, c, :], g.ident[:], start=True, stop=True)
                    mm.then_inc(pe_done[i], 1)
                    pe.wait_ge(act_done[i], N_ACT * r + 5)
                    for c in range(TT):
                        pe.transpose(bank(i, 1, c), qkvz[:, GDN_H + h, P * c:P * c + P], g.ident[:])
                    for c in range(TT):
                        mm = pe.transpose(bank(i, 2, c), qkvz[:, 2 * GDN_H + h, P * c:P * c + P], g.ident[:])
                    mm.then_inc(pe_done[i], 1)

                def level_x(i, r, lv):
                    b = B[i]
                    base_d = N_DVE * r + 8 + 3 * (lv - 1)
                    pe.wait_ge(dve_done[i], base_d + 1)
                    for c in range(TT):
                        mm = pe.matmul(bank(i, 3, c), b["m"][:, c, :], b["tm"][:, c, :], start=True, stop=True)
                    mm.then_inc(pe_done[i], 1)

                def level_d(i, r, lv):
                    b = B[i]
                    pe.wait_ge(act_done[i], N_ACT * r + 9 + lv)
                    for c in range(TT):
                        mm = pe.matmul(bank(i, 0, c), b["x"][:, c, :], b["um"][:, c, :], start=True, stop=True)
                    mm.then_inc(pe_done[i], 1)
                    if lv < L:
                        for c in range(TT):
                            mm = pe.matmul(bank(i, 3, c), b["um"][:, c, :], b["x"][:, c, :], start=True, stop=True)
                        mm.then_inc(pe_done[i], 1)

                def back(h, i, r):
                    b = B[i]
                    pe.wait_ge(dve_done[i], N_DVE * r + 8 + 3 * L - 1)
                    for c in range(TT):
                        pe.matmul(bank(i, 1, c), b["um"][:, c, :], b["vb"][:, c, :], start=True, stop=True)
                    for c in range(TT):
                        mm = pe.matmul(bank(i, 2, c), b["kbg"][:, c, :], b["um"][:, c, :], start=True, stop=True)
                    mm.then_inc(pe_done[i], 1)

                for r in range(GDN_H // NB):
                    for i in range(NB):
                        front(NB * r + i, i, r)
                    for i in range(NB):
                        first_level(NB * r + i, i, r)
                    for lv in range(1, L + 1):
                        for i in range(NB):
                            level_x(i, r, lv)
                        for i in range(NB):
                            level_d(i, r, lv)
                    for i in range(NB):
                        back(NB * r + i, i, r)

            @block.scalar
            def _(act):
                def front(h, i, r):
                    b = B[i]
                    act.wait_ge(pe_done[i], N_PE * r + 1)
                    act.wait_ge(dve_done[i], N_DVE * r + 1)
                    act.activation(flat(b["eg"][:]), ps[i][:, 0, :], ACT.Exp).then_inc(act_done[i], 1)
                    for c in range(TT):
                        col = GDN_H * c + h
                        act.activation(b["dec"][:, c, :], b["dec"][:, c, :], ACT.Exp,
                                       bias=gt["neg_gc"][:, col:col + 1]).then_inc(act_done[i], 1)

                def turned(h, i, r):
                    b = B[i]
                    act.wait_ge(pe_done[i], N_PE * r + 6)
                    for c in range(TT):
                        col = GDN_H * c + h
                        act.activation(b["kbg"][:, c, :], ps[i][:, 1, P * c:P * c + P], ACT.Copy,
                                       scale=gt["beta_egc"][:, col:col + 1]).then_inc(act_done[i], 1)

                def level(h, i, r, lv):
                    b = B[i]
                    act.wait_ge(pe_done[i], N_PE * r + 7 + 3 * (lv - 1))
                    act.activation(flat(b["x"][:]), ps[i][:, 3, :], ACT.Copy).then_inc(act_done[i], 1)

                for r in range(GDN_H // NB):
                    for i in range(NB):
                        front(NB * r + i, i, r)
                    for i in range(NB):
                        turned(NB * r + i, i, r)
                    for lv in range(1, L + 1):
                        for i in range(NB):
                            level(NB * r + i, i, r, lv)

            @block.vector
            def _(dve):
                dve.wait_ge(ld, 16)

                def masked(t, lv):
                    return levels[:, lv:lv + 1, :].to_broadcast([P, TT, P])

                def wide(ap):
                    return ap.rearrange("p (c n) -> p c n", c=TT)

                def front(h, i, r):
                    b = B[i]
                    q = qkvz[:, h, :]
                    dve.wait_ge(pe_done[i], N_PE * r + 1)
                    dve.tensor_tensor(b["dec"][:], wide(ps[i][:, 0, :]),
                                      g.neg_below[:].unsqueeze(1).to_broadcast([P, TT, P]),
                                      ALU.add).then_inc(dve_done[i], 1)
                    dve.wait_ge(act_done[i], N_ACT * r + 5)
                    dve.wait_ge(pe_done[i], N_PE * r + 4)
                    dve.tensor_tensor(q, q, flat(b["eg"][:]), ALU.mult).then_inc(dve_done[i], 1)
                    dve.tensor_tensor(flat(b["decb"][:]), flat(b["dec"][:]), ps[i][:, 1, :],
                                      ALU.mult).then_inc(dve_done[i], 1)
                    dve.tensor_tensor(qk_t[:, h, :], flat(b["dec"][:]), ps[i][:, 3, :],
                                      ALU.mult).then_inc(dve_done[i], 1)
                    dve.wait_ge(dve_done[i], N_DVE * r + 3)
                    dve.tensor_tensor(flat(b["at"][:]), flat(b["decb"][:]), ps[i][:, 2, :],
                                      ALU.mult).then_inc(dve_done[i], 1)
                    dve.wait_ge(dve_done[i], N_DVE * r + 5)
                    dve.tensor_tensor(b["m"][:], b["at"][:], masked(b, 0), ALU.mult).then_inc(dve_done[i], 1)
                    dve.wait_ge(dve_done[i], N_DVE * r + 6)
                    dve.tensor_tensor(b["um"][:], g.ident[:].unsqueeze(1).to_broadcast([P, TT, P]), b["m"][:],
                                      ALU.subtract).then_inc(dve_done[i], 1)

                def first_level(h, i, r):
                    b = B[i]
                    dve.wait_ge(pe_done[i], N_PE * r + 5)
                    dve.tensor_tensor(b["tm"][:], g.ident[:].unsqueeze(1).to_broadcast([P, TT, P]),
                                      wide(ps[i][:, 0, :]), ALU.subtract).then_inc(dve_done[i], 1)

                def turned(h, i, r):
                    b = B[i]
                    dve.wait_ge(act_done[i], N_ACT * r + 9)
                    for c in range(TT):
                        col = GDN_H * c + h
                        dve.tensor_scalar(k_dec[:, h, P * c:P * c + P], ps[i][:, 1, P * c:P * c + P],
                                          gt["krest"][:, col:col + 1], None, ALU.mult)
                        dve.tensor_scalar(b["vb"][:, c, :], ps[i][:, 2, P * c:P * c + P],
                                          gt["beta"][:, col:col + 1], None, ALU.mult)

                def level_m(i, lv):
                    b = B[i]
                    dve.tensor_tensor(b["m"][:], b["at"][:], masked(b, lv), ALU.mult).then_inc(dve_done[i], 1)

                def level(h, i, r, lv):
                    b = B[i]
                    base_d = N_DVE * r + 8 + 3 * (lv - 1)
                    base_p = N_PE * r + 6 + 3 * (lv - 1)
                    dve.wait_ge(pe_done[i], base_p + (3 if lv < L else 2))
                    dve.wait_ge(dve_done[i], base_d + 1)
                    dve.tensor_tensor(flat(b["um"][:]), flat(b["um"][:]), ps[i][:, 0, :],
                                      ALU.subtract).then_inc(dve_done[i], 1)
                    if lv < L:
                        dve.tensor_tensor(flat(b["tm"][:]), flat(b["tm"][:]), ps[i][:, 3, :],
                                          ALU.subtract).then_inc(dve_done[i], 1)

                def back(h, i, r):
                    dve.wait_ge(pe_done[i], N_PE * (r + 1))
                    dve.tensor_copy(qkvz[:, 2 * GDN_H + h, :], ps[i][:, 1, :]).then_inc(dve_done[i], 1)
                    dve.tensor_copy(qkvz[:, GDN_H + h, :], ps[i][:, 2, :]).then_inc(dve_done[i], 1)

                for r in range(GDN_H // NB):
                    for i in range(NB):
                        front(NB * r + i, i, r)
                    for i in range(NB):
                        first_level(NB * r + i, i, r)
                    for i in range(NB):
                        turned(NB * r + i, i, r)
                    for i in range(NB):
                        level_m(i, 1)
                    for lv in range(1, L + 1):
                        for i in range(NB):
                            level(NB * r + i, i, r, lv)
                            if lv < L:
                                level_m(i, lv + 1)
                    for i in range(NB):
                        back(NB * r + i, i, r)


def stage_gdn_scan(g, a, qkvz, gt, qk_t, k_dec):
    nc = g.nc
    with Stage(nc, "gscan") as st:
        state = st.sb("state", [P, GDN_H, P])
        v_new = st.sb("v_new", [P, GDN_H, P])
        ps_p, ps_o, ps_s = st.ps("p", 2), st.ps("o", 2), st.ps("s", 2)
        zeroed, p_done, v_done = st.sem("zeroed"), st.sem("p_done"), st.sem("v_done")
        o_done, s_done, o_out, s_out = st.sem("o_done"), st.sem("s_done"), st.sem("o_out"), st.sem("s_out")

        def blk(t, h, c):
            return t[:, h, P * c:P * c + P]

        def bank(ps, h):
            return ps[:, h // 4, P * (h % 4):P * (h % 4) + P]

        with nc.Block() as block:
            @block.gpsimd
            def _(pool):
                pool.memset(state[:], 0.0).then_inc(zeroed, 1)

            @block.tensor
            def _(pe):
                pe.wait_ge(zeroed, 1)
                for c in range(TT):
                    for half in range(2):
                        hs = range(4 * half, 4 * half + 4)
                        if c:
                            pe.wait_ge(s_out, 8 * (c - 1) + 4 * half + 4)
                            pe.wait_ge(v_done, 2 * (c - 1) + half + 1)
                        for h in hs:
                            mm = pe.matmul(bank(ps_p, h), blk(qkvz, GDN_H + h, c), state[:, h, :],
                                           start=True, stop=True)
                        mm.then_inc(p_done, 1)
                    for half in range(2):
                        hs = range(4 * half, 4 * half + 4)
                        pe.wait_ge(v_done, 2 * c + half + 1)
                        for h in hs:
                            mm = pe.matmul(bank(ps_s, h), blk(k_dec, h, c), v_new[:, h, :],
                                           start=True, stop=True)
                        mm.then_inc(s_done, 1)
                        if c:
                            pe.wait_ge(o_out, 2 * (c - 1) + half + 1)
                        for h in hs:
                            pe.matmul(bank(ps_o, h), state[:, h, :], blk(qkvz, h, c), start=True, stop=False)
                            mm = pe.matmul(bank(ps_o, h), v_new[:, h, :], blk(qk_t, h, c),
                                           start=False, stop=True)
                        mm.then_inc(o_done, 1)

            @block.vector
            def _(dve):
                for c in range(TT):
                    for half in range(2):
                        h0 = 4 * half
                        dve.wait_ge(p_done, 2 * c + half + 1)
                        if c:
                            dve.wait_ge(o_done, 2 * (c - 1) + half + 1)
                        dve.tensor_tensor(v_new[:, h0:h0 + 4, :],
                                          qkvz[:, 2 * GDN_H + h0:2 * GDN_H + h0 + 4, P * c:P * c + P],
                                          ps_p[:, half, :].rearrange("p (h n) -> p h n", h=4),
                                          ALU.subtract).then_inc(v_done, 1)
                    for half in range(2):
                        dve.wait_ge(s_done, 2 * c + half + 1)
                        dve.wait_ge(o_done, 2 * c + half + 1)
                        for h in range(4 * half, 4 * half + 4):
                            col = GDN_H * c + h
                            dve.scalar_tensor_tensor(state[:, h, :], state[:, h, :], gt["dlast"][:, col:col + 1],
                                                     bank(ps_s, h), ALU.mult, ALU.add).then_inc(s_out, 1)

            @block.scalar
            def _(act):
                for c in range(TT):
                    for half in range(2):
                        h0 = 4 * half
                        act.wait_ge(o_done, 2 * c + half + 1)
                        act.activation(qkvz[:, h0:h0 + 4, P * c:P * c + P],
                                       ps_o[:, half, :].rearrange("p (h n) -> p h n", h=4),
                                       ACT.Copy).then_inc(o_out, 1)


def stage_gdn_out(g, a, nxt, qkvz):
    nc = g.nc
    n = GDN_H
    with Stage(nc, "gout") as st:
        sq = [st.sb(f"sq{i}", [P, T]) for i in range(2)]
        y = [st.sb(f"y{i}", [P, T]) for i in range(2)]
        nw = st.sb("nw", [P, 1])
        rows, spread = st.ps("rows", 1), st.ps("spread", 4)
        root, inv = st.sb("root", [n, T]), st.sb("inv", [n, T])
        invh, invl = st.sb("invh", [n, T], F32R), st.sb("invl", [n, T], F32R)
        inv_step = st.sem("inv_step")
        ld, squared, summed, rooted = st.sem("loaded"), st.sem("squared"), st.sem("summed"), st.sem("rooted")
        inverted, spread_done, used = st.sem("inverted"), st.sem("spread_done"), st.sem("spread_used")
        y_done, hi_done, lo_done = st.sem("y_done"), st.sem("hi_done"), st.sem("lo_done")
        with nc.Block() as block:
            @block.sync
            def _(sp):
                sp.dma_start(nw[:], a["gdn_norm_w"].rearrange("a p -> p a"),
                             allow_slow_non_contiguous=True).then_inc(ld, 16)
                nxt.load_first(sp)

            @block.scalar
            def _(act):
                for r in range(n):
                    if r >= 2:
                        act.wait_ge(summed, r - 1)
                    act.activation(sq[r % 2][:], qkvz[:, r, :], ACT.Square).then_inc(squared, 1)
                nxt.hi_first(act)
                act.wait_ge(summed, n)
                act.activation(root[:], rows[0:n, 0, :], ACT.Sqrt, scale=1.0 / P,
                               bias=g.eps6[0:n, :]).then_inc(rooted, 1)
                for r in range(n):
                    act.wait_ge(y_done, r + 1)
                    act.activation(g.xh[:, r, :], y[r % 2][:], ACT.Copy).then_inc(hi_done, 1)

            @block.tensor
            def _(pe):
                for r in range(n):
                    pe.wait_ge(squared, r + 1)
                    pe.matmul(rows[0:n, 0, :], g.column(r, n), sq[r % 2][:],
                              start=(r == 0), stop=(r == n - 1)).then_inc(summed, 1)
                pe.wait_ge(inverted, 1)
                for r in range(n):
                    if r >= 4:
                        pe.wait_ge(used, r - 3)
                    pe.matmul(spread[:, r % 4, :], g.row(r, n), invh[:], start=True, stop=False)
                    pe.matmul(spread[:, r % 4, :], g.row(r, n), invl[:],
                              start=False, stop=True).then_inc(spread_done, 1)

            @block.vector
            def _(dve):
                dve.wait_ge(rooted, 1)
                dve.wait_ge(ld, 16)
                link = Link(dve, inv_step)
                link(dve.reciprocal(inv[:], root[:]))
                link(dve.tensor_copy(invh[:], inv[:]))
                dve.tensor_tensor(invl[:], inv[:], invh[:].bitcast(F32), ALU.subtract).then_inc(inverted, 1)
                for r in range(n):
                    dve.wait_ge(spread_done, r + 1)
                    if r >= 2:
                        dve.wait_ge(hi_done, r - 1)
                        dve.wait_ge(lo_done, r - 1)
                    dve.scalar_tensor_tensor(y[r % 2][:], qkvz[:, r, :], nw[:, 0:1], spread[:, r % 4, :],
                                             ALU.mult, ALU.mult).then_inc(used, 1)
                    dve.wait_ge(used, r + 1)
                    dve.tensor_tensor(y[r % 2][:], y[r % 2][:], qkvz[:, 3 * GDN_H + r, :],
                                      ALU.mult).then_inc(y_done, 1)

            @block.gpsimd
            def _(pool):
                nxt.lo_first(pool)
                for r in range(n):
                    pool.wait_ge(hi_done, r + 1)
                    pool.tensor_tensor(g.xl[:, r, :], y[r % 2][:], g.xh[:, r, :].bitcast(F32),
                                       ALU.subtract).then_inc(lo_done, 1)


def stage_out_proj(g, name, run, alpha):
    nc = g.nc
    with Stage(nc, name) as st:
        ws = run.attach(st)
        with nc.Block() as block:
            @block.sync
            def _(sp):
                ws.load_rest(sp)

            @block.tensor
            def _(pe):
                over(pe, 2, lambda b: ws.multiply(pe, b, g.xh, g.xl, False))

            @block.gpsimd
            def _(pool):
                ws.lo_rest(pool)

            @block.scalar
            def _(act):
                ws.hi_rest(act)

            @block.vector
            def _(dve):
                def body(b):
                    for t in range(TT):
                        dve.wait_ge(ws.acc_ready, b * 4 + (t + 1))
                        h = g.h[:, t, bass.ds(b * 512, 512)]
                        dve.scalar_tensor_tensor(h, h, alpha, ws.acc[:, t, :],
                                                 ALU.mult, ALU.add).then_inc(ws.evicted, 1)
                over(dve, 2, body)


def stage_norm(g, name, src, dst, gain, shift, eps, center, nxt=None):
    nc = g.nc
    with Stage(nc, name) as st:
        gb = st.sb("gain", [P, D])
        bb = st.sb("shift", [P, D]) if shift else None
        stats, mv = st.sb("stats", [P, TT, 2, 6]), st.sb("mv", [P, TT, 2])
        sq = st.sb("sq", [P, D]) if not center else None
        root, inv = st.sb("root", [P, TT]), st.sb("inv", [P, TT])
        ld, stat, agg, rooted, inverted = (st.sem(x) for x in ("loaded", "stat", "agg", "rooted", "inverted"))
        scaled, gained, done = st.sem("scaled"), st.sem("gained"), st.sem("done")
        n_ld = 32 if shift else 16
        n_pool = TT // 2 if center else 0
        pool_done = st.sem("pool_done")

        def normalised(pe):
            pe.wait_ge(done, TT - n_pool)
            if n_pool:
                pe.wait_ge(pool_done, n_pool)
        turn = to_feature_major(g, st, dst, normalised)
        with nc.Block() as block:
            @block.sync
            def _(sp):
                sp.dma_start(gb[:], rows_of(*gain, D)).then_inc(ld, 16)
                if shift:
                    sp.dma_start(bb[:], rows_of(*shift, D)).then_inc(ld, 16)
                if nxt is not None:
                    nxt.load_first(sp)

            @block.vector
            def _(dve):
                if center:
                    for t in range(TT):
                        for i in range(2):
                            dve.bn_stats(stats[:, t, i, :], src[:, t, 512 * i:512 * i + 512]).then_inc(stat, 1)
                        dve.wait_ge(stat, 2 * t + 2)
                        dve.bn_aggr(mv[:, t, :], stats[:, t, :, :].rearrange("p a b -> p (a b)")).then_inc(agg, 1)
                dve.wait_ge(rooted, 1)
                dve.reciprocal(inv[:], root[:]).then_inc(inverted, 1)
                dve.wait_ge(inverted, 1)
                dve.wait_ge(ld, n_ld)
                for t in range(TT):
                    if center:
                        dve.tensor_scalar(dst[:, t, :], src[:, t, :], mv[:, t, 0:1], inv[:, t:t + 1],
                                          ALU.subtract, ALU.mult).then_inc(scaled, 1)
                        dve.wait_ge(scaled, t + 1)
                        dve.tensor_tensor(dst[:, t, :], dst[:, t, :], gb[:], ALU.mult).then_inc(gained, 1)
                    else:
                        dve.scalar_tensor_tensor(dst[:, t, :], src[:, t, :], inv[:, t:t + 1], gb[:],
                                                 ALU.mult, ALU.mult).then_inc(done, 1)
                if center:
                    for t in range(n_pool, TT):
                        dve.wait_ge(gained, t + 1)
                        dve.tensor_tensor(dst[:, t, :], dst[:, t, :], bb[:], ALU.add).then_inc(done, 1)
                turn[2](dve)

            @block.scalar
            def _(act):
                if center:
                    act.wait_ge(agg, TT)
                    act.activation(root[:], mv[:, :, 1], ACT.Sqrt,
                                   bias=(g.eps5 if eps == LN_EPS else g.eps6)[:]).then_inc(rooted, 1)
                else:
                    for t in range(TT):
                        act.activation(sq[:], src[:, t, :], ACT.Square,
                                       accum_out=mv[:, t, 1:2]).then_inc(agg, 1)
                        act.wait_ge(agg, t + 1)
                    act.activation(root[:], mv[:, :, 1], ACT.Sqrt, scale=1.0 / D, bias=g.eps6[:]).then_inc(rooted, 1)
                if nxt is not None:
                    nxt.hi_first(act)
                turn[1](act)

            @block.gpsimd
            def _(pool):
                for t in range(n_pool):
                    pool.wait_ge(gained, t + 1)
                    pool.tensor_tensor(dst[:, t, :], dst[:, t, :], bb[:], ALU.add).then_inc(pool_done, 1)
                if nxt is not None:
                    nxt.lo_first(pool)

            @block.tensor
            def _(pe):
                turn[0](pe)


MAX_BLOCKS = 2 * T // P + N_EXP


def stage_route(g, name, a, layer, rt):
    nc = g.nc
    G, E = 4, 4
    with Stage(nc, name) as st:
        narrow = NarrowProduct(g, st, G + N_EXP)
        wr = narrow.w
        br = st.sb("br", [P, G + N_EXP])
        desc, iota_b = st.sb("desc", [P, G]), st.sb("iota_b", [1, MAX_BLOCKS, N_EXP])
        lg = st.sb("lg", [P, TT, G + N_EXP])
        def small(n, *shape):
            return st.sb(n, [P, TT, *shape])
        mx, nmx, s1, pr, eq, tie, tm = (small(x, k) for x, k in
                                        (("mx", 1), ("nmx", 1), ("s1", 1), ("pr", 4), ("eq", 4), ("tie", 4), ("tm", 1)))
        gp, ohg, el, t16 = small("gp", 1), small("ohg", 4), small("el", 4), small("t16", G, E)
        m1, m2, oh1, oh2, p2 = small("m1", 1), small("m2", 1), small("oh1", 4), small("oh2", 4), small("p2", 4)
        f1, f2, oh = small("f1", G, E), small("f2", G, E), small("oh", N_EXP)
        pre, tot, cnt, cmp = small("pre", N_EXP), small("tot", N_EXP), st.sb("cnt", [P, N_EXP]), st.sb("cmp", [P, N_EXP])
        blocks, incl, base = st.sb("blocks", [P, N_EXP]), st.sb("incl", [P, N_EXP]), st.sb("base", [P, N_EXP])
        one16 = st.sb("one16", [P, N_EXP])
        le, tabf = st.sb("le", [1, MAX_BLOCKS, N_EXP]), st.sb("tabf", [1, MAX_BLOCKS + 1])
        more = st.sb("more", [1, MAX_BLOCKS // 2 - 1])
        ps = st.ps("ps", 3)
        ld, step, v_max, a_exp, v_oh, p_cnt = (st.sem(x) for x in
            ("loaded", "step", "v_max", "a_exp", "v_onehot", "p_count"))
        h_split, x_free = st.sem("h_split"), st.sem("x_free")

        with nc.Block() as block:
            @block.sync
            def _(sp):
                sp.dma_start(wr[:, :, 0:G], a["moe_w_grp"][layer].rearrange("(k p) n -> p k n", p=P)).then_inc(narrow.loaded, 16)
                sp.dma_start(wr[:, :, G:], a["moe_w_rt"][layer].rearrange("(k p) n -> p k n", p=P)).then_inc(narrow.loaded, 16)
                sp.dma_start(br[:, 0:G], rows_of(a["moe_b_grp"], layer * G, G)).then_inc(ld, 16)
                sp.dma_start(br[:, G:], rows_of(a["moe_b_rt"], layer * N_EXP, N_EXP)).then_inc(ld, 16)
                sp.dma_start(desc[:], rows_of(a["c_desc"], 0, G)).then_inc(ld, 16)
                sp.dma_start(iota_b[:], a["c_iota_b"]).then_inc(ld, 16)

            @block.tensor
            def _(pe):
                narrow.multiply(pe)
                narrow.turn(pe)
                pe.wait_ge(v_oh, 1)
                flat = oh[:].rearrange("p t e -> p (t e)")
                pe.matmul(ps[:, 1, 0:64], g.striu[:], flat, start=True, stop=True)
                pe.matmul(ps[:, 2, 0:64], g.ones[:], flat, start=True, stop=True).then_inc(p_cnt, 1)

            @block.scalar
            def _(act):
                act.wait_ge(v_max, 1)
                act.activation(pr[:], pr[:], ACT.Exp).then_inc(a_exp, 1)
                act.wait_ge(v_max, 2)
                act.activation(pr[:], pr[:], ACT.Exp).then_inc(a_exp, 1)
                act.wait_ge(narrow.acc_done, 1)
                for t in range(TT):
                    act.activation(rt.hh[:, t, :], g.h[:, t, :], ACT.Copy).then_inc(h_split, 1)

            @block.gpsimd
            def _(pool):
                for t in range(TT):
                    pool.wait_ge(h_split, t + 1)
                    pool.tensor_tensor(rt.hl[:, t, :], g.h[:, t, :], rt.hh[:, t, :].bitcast(F32),
                                       ALU.subtract).then_inc(x_free, 1)

            @block.vector
            def _(dve):
                link = Link(dve, step)
                b4 = lambda t: t[:].to_broadcast([P, TT, 4])

                def first_of(onehot, p, m):
                    link(dve.tensor_tensor(eq[:], p[:], b4(m), ALU.is_equal))
                    link(dve.tensor_tensor(tie[:], eq[:], desc[:].unsqueeze(1).to_broadcast([P, TT, 4]), ALU.mult))
                    link(dve.tensor_reduce(tm[:], tie[:], AX.X, ALU.max))
                    link(dve.tensor_tensor(onehot[:], tie[:], b4(tm), ALU.is_equal))

                def softmax(src, n):
                    link(dve.tensor_reduce(mx[:], src, AX.X, ALU.max))
                    dve.tensor_tensor(pr[:], src, b4(mx), ALU.subtract).then_inc(v_max, 1)
                    dve.wait_ge(a_exp, n)
                    link(dve.tensor_reduce(s1[:], pr[:], AX.X, ALU.add))
                    link(dve.reciprocal(s1[:], s1[:]))
                    link(dve.tensor_tensor(pr[:], pr[:], b4(s1), ALU.mult))

                narrow.split(dve, 32)
                narrow.copy(dve)
                dve.wait_ge(ld, 16 * 4)
                dve.wait_ge(narrow.turned, 1)
                link(dve.tensor_tensor(lg[:], narrow.out.rearrange("p (t n) -> p t n", t=TT),
                                       br[:].unsqueeze(1).to_broadcast([P, TT, 20]), ALU.add))
                softmax(lg[:, :, 0:G], 1)
                link(dve.tensor_reduce(gp[:], pr[:], AX.X, ALU.max))
                first_of(ohg, pr, gp)
                link(dve.tensor_tensor(t16[:], lg[:, :, G:].rearrange("p t (g e) -> p t g e", g=G),
                                       ohg[:].unsqueeze(3).to_broadcast([P, TT, G, E]), ALU.mult))
                link(dve.tensor_reduce(el[:], t16[:].rearrange("p t g e -> p t e g"), AX.X, ALU.add))
                softmax(el[:], 2)
                link(dve.tensor_reduce(m1[:], pr[:], AX.X, ALU.max))
                first_of(oh1, pr, m1)
                link(dve.scalar_tensor_tensor(p2[:], oh1[:], -2.0, pr[:], ALU.mult, ALU.add))
                link(dve.tensor_reduce(m2[:], p2[:], AX.X, ALU.max))
                first_of(oh2, p2, m2)
                link(dve.tensor_tensor(s1[:], m1[:], m2[:], ALU.add))
                link(dve.reciprocal(s1[:], s1[:]))
                link(dve.tensor_tensor(s1[:], s1[:], gp[:], ALU.mult))
                link(dve.tensor_tensor(rt.weight[:, :, 0:1], m1[:], s1[:], ALU.mult))
                link(dve.tensor_tensor(rt.weight[:, :, 1:2], m2[:], s1[:], ALU.mult))
                for f, o in ((f1, oh1), (f2, oh2)):
                    for t in range(TT):
                        link(dve.tensor_tensor(f[:, t], ohg[:, t].unsqueeze(2).to_broadcast([P, G, E]),
                                               o[:, t].unsqueeze(1).to_broadcast([P, G, E]), ALU.mult))
                flat = lambda t: t[:].rearrange("p t g e -> p t (g e)")
                dve.tensor_tensor(oh[:], flat(f1), flat(f2), ALU.add).then_inc(v_oh, 1)
                dve.memset(one16[:], 1.0)
                dve.wait_ge(p_cnt, 1)
                link(dve.tensor_copy(pre[:], ps[:, 1, 0:64].rearrange("p (t e) -> p t e", t=TT)))
                link(dve.tensor_copy(tot[:], ps[:, 2, 0:64].rearrange("p (t e) -> p t e", t=TT)))
                link(dve.tensor_copy(cnt[:], tot[:, 0, :]))
                for t in range(1, TT):
                    link(dve.tensor_tensor(pre[:, t, :], pre[:, t, :], cnt[:], ALU.add))
                    link(dve.tensor_tensor(cnt[:], cnt[:], tot[:, t, :], ALU.add))
                link(dve.tensor_scalar(blocks[:], cnt[:], 0.5, None, ALU.is_gt))
                for j in range(1, TT):
                    link(dve.tensor_scalar(cmp[:], cnt[:], P * j + 0.5, None, ALU.is_gt))
                    link(dve.tensor_tensor(blocks[:], blocks[:], cmp[:], ALU.add))
                link(dve.tensor_tensor_scan(incl[:], one16[:], blocks[:], 0.0, ALU.mult, ALU.add))
                link(dve.tensor_tensor(base[:], incl[:], blocks[:], ALU.subtract))
                link(dve.tensor_scalar(base[:], base[:], float(P), None, ALU.mult))
                link(dve.tensor_tensor(pre[:], pre[:], base[:].unsqueeze(1).to_broadcast([P, TT, N_EXP]), ALU.add))
                for n, f in enumerate((f1, f2)):
                    link(dve.tensor_tensor(flat(f), flat(f), pre[:], ALU.mult))
                    link(dve.tensor_reduce(rt.slot[:, :, n:n + 1], flat(f), AX.X, ALU.add))
                link(dve.tensor_copy(rt.slot_i[:], rt.slot[:]))
                link(dve.tensor_tensor(le[:], incl[0:1, :].unsqueeze(1).to_broadcast([1, MAX_BLOCKS, N_EXP]),
                                       iota_b[:], ALU.is_le))
                link(dve.tensor_reduce(tabf[:, 0:MAX_BLOCKS], le[:], AX.X, ALU.add))
                link(dve.tensor_scalar(tabf[:, 0:MAX_BLOCKS], tabf[:, 0:MAX_BLOCKS], N_EXP - 1.0, None, ALU.min))
                link(dve.tensor_scalar(more[:], iota_b[0:1, 2::2, 0], incl[0:1, N_EXP - 1:N_EXP], None, ALU.is_lt))
                link(dve.tensor_reduce(tabf[:, MAX_BLOCKS:MAX_BLOCKS + 1], more[:], AX.X, ALU.add))
                link(dve.tensor_copy(rt.table[:], tabf[:]))


def stage_experts(g, name, a, layer, rt):
    nc = g.nc
    wg, wu, wd = a["moe_w_gate"][layer], a["moe_w_up"][layer], a["moe_w_down"][layer]
    rows = g.moe_rows
    with Stage(nc, name) as st:
        wf = [[st.sb(f"wf{b}_{u}", [P, HALF, 512]) for u in range(3)] for b in range(2)]
        wh = [st.sb(f"wh{u}", [P, HALF, 512], F32R) for u in range(3)]
        wl = [st.sb(f"wl{u}", [P, HALF, 512], F32R) for u in range(3)]
        pick, eq0 = st.sb("pick", [P, TT, 2 * P], F32R), st.sb("eq0", [P, TT, 2 * P])
        xh, xl = st.sb("xh", [P, KT, 2 * P], F32R), st.sb("xl", [P, KT, 2 * P], F32R)
        act_g, hid = st.sb("act_g", [P, HID]), st.sb("hid", [P, HID])
        hth, htl = st.sb("hth", [P, 2, P], F32R), st.sb("htl", [P, 2, P], F32R)
        y = st.sb("y", [P, D])
        slot = st.sb("slot", [P, TT, 2])
        iota = st.sb("iota", [P, 2 * P])
        ps_xh, ps_xl, ps_gu, ps_t, ps_y = st.ps("ps_xh", 2), st.ps("ps_xl", 2), st.ps("ps_gu", 1), st.ps("ps_t", 1), st.ps("ps_y", 2)
        ld = st.sem("loaded")
        w_loaded = [[st.sem(f"w_loaded{b}_{u}") for u in range(3)] for b in range(2)]
        w_hi, w_lo = [st.sem(f"w_hi{u}") for u in range(3)], [st.sem(f"w_lo{u}") for u in range(3)]
        unit0_used, gu_done, x_done = st.sem("unit0_used"), st.sem("gu_done"), st.sem("x_done")
        picked, eq_done, slot_done = st.sem("picked"), st.sem("eq_done"), st.sem("slot_done")
        xh_out, xl_out, silu_done, hid_done = st.sem("xh_out"), st.sem("xl_out"), st.sem("silu_done"), st.sem("hid_done")
        t_done, th_out, tl_out, y_done, y_out, y_stored = (st.sem(x) for x in
            ("t_done", "th_out", "tl_out", "y_done", "y_out", "y_stored"))
        back = [st.sem(f"back{t}") for t in range(TT)]
        scaled, added = st.sem("scaled"), st.sem("added")

        def last_pair(eng):
            return eng.value_load(rt.table[0:1, MAX_BLOCKS:MAX_BLOCKS + 1], min_val=T // P - 1,
                                  max_val=MAX_BLOCKS // 2 - 1)

        def pairs(eng, end, body):
            body(0, 0, 0, False)
            body(0, 1, 1, False)
            with eng.Fori(1, end) as j:
                for b in range(2):
                    body(j, b, j * 2 + b, False)
            body(end, 0, end * 2, True)
            body(end, 1, end * 2 + 1, True)

        rows_back = [x[:].rearrange("p (k a) n -> p k (a n)", k=2) for x in (*wf[0], wf[1][0])]

        def first(i):
            return isinstance(i, int) and i == 0

        with nc.Block() as block:
            @block.sync
            def _(sp):
                sp.dma_start(iota[:], a["c_iota"]).then_inc(ld, 16)
                end = last_pair(sp)

                def store(i):
                    sp.wait_ge(y_out, i + 1)
                    sp.dma_start(rows[bass.ds(i * P, P), :], y[:]).then_inc(y_stored, 16)

                def body(j, b):
                    i = j * 2 + b
                    e = sp.value_load(rt.table[0:1, bass.ds(i, 1)], min_val=0, max_val=N_EXP - 1)
                    for u in range(2):
                        if not first(j):
                            sp.wait_ge(w_lo[u], i - 1)
                        for c, w in ((0, wg), (HID, wu)):
                            src = w[bass.ds(e, 1), HALF * P * u:HALF * P * (u + 1), :]
                            sp.dma_start(wf[b][u][:, :, c:c + HID],
                                         src.rearrange("a (k p) n -> p (a k) n", p=P)).then_inc(w_loaded[b][u], 16)
                    if not first(j):
                        sp.wait_ge(w_lo[2], i - 1)
                    if not first(j):
                        store(i - 2)
                    src = wd[bass.ds(e, 1), :, :].rearrange("a (k p) n -> p (a k) n", p=P)
                    sp.dma_start(wf[b][2][:].rearrange("p (k c) n -> p k (c n)", k=2), src).then_inc(w_loaded[b][2], 16)
                for b in range(2):
                    body(0, b)
                with sp.Fori(1, end + 1) as j:
                    for b in range(2):
                        body(j, b)
                for b in range(2):
                    store(end * 2 + b)

            @block.tensor
            def _(pe):
                end = last_pair(pe)

                def gather(j, v, part):
                    if part == 0:
                        pe.wait_ge(picked, j + 1)
                        if not (first(j) and v == 0):
                            pe.wait_ge(xh_out, j * 2 + v)
                            pe.wait_ge(xl_out, j * 2 + v)
                    for kk in (2 * part, 2 * part + 1):
                        k = HALF * v + kk
                        for src, dst in ((rt.hh, ps_xh), (rt.hl, ps_xl)):
                            for t in range(TT):
                                mm = pe.matmul(dst[:, kk // 2, 2 * P * (kk % 2):2 * P * (kk % 2) + 2 * P],
                                               src[:, t, P * k:P * k + P], pick[:, t, :],
                                               start=(t == 0), stop=(t == TT - 1))
                    if part == 1:
                        mm.then_inc(x_done, 1)

                def body(j, b, i, last_pair):
                    if not first(i):
                        pe.wait_ge(hid_done, i)
                    for u in range(2):
                        pe.wait_ge(w_lo[u], i + 1)
                        if b == 0:
                            pe.wait_ge(xh_out, j * 2 + (u + 1))
                            pe.wait_ge(xl_out, j * 2 + (u + 1))
                        for k in range(HALF):
                            for m, (x, w) in enumerate(((xh, wh), (xh, wl), (xl, wh))):
                                mm = pe.matmul(ps_gu[:, 0, :], x[:, HALF * u + k, P * b:P * b + P], w[u][:, k, :],
                                               start=(u == 0 and k == 0 and m == 0),
                                               stop=(u == 1 and k == HALF - 1 and m == 2))
                        mm.then_inc(unit0_used if u == 0 else gu_done, 1)
                    if not last_pair:
                        gather(j + 1, b, 0)
                    pe.wait_ge(hid_done, i + 1)
                    if not first(i):
                        pe.wait_ge(tl_out, i)
                    for k in range(2):
                        mm = pe.transpose(ps_t[:, 0, P * k:P * k + P], hid[:, P * k:P * k + P], g.ident[:])
                    mm.then_inc(t_done, 1)
                    if not last_pair:
                        gather(j + 1, b, 1)
                    pe.wait_ge(tl_out, i + 1)
                    pe.wait_ge(w_lo[2], i + 1)
                    if not first(i):
                        pe.wait_ge(y_out, i)
                    down = [w[2][:].rearrange("p (k c) n -> p k c n", k=2) for w in (wh, wl)]
                    for c in range(2):
                        for k in range(2):
                            for m, (x, w) in enumerate(((hth, down[0]), (hth, down[1]), (htl, down[0]))):
                                mm = pe.matmul(ps_y[:, c, :], x[:, k, :], w[:, k, c, :],
                                               start=(k == 0 and m == 0), stop=(k == 1 and m == 2))
                    mm.then_inc(y_done, 1)
                for v in range(2):
                    for part in range(2):
                        gather(0, v, part)
                pairs(pe, end, body)

            @block.scalar
            def _(act):
                end = last_pair(act)

                def hi(j, b, u):
                    i = j * 2 + b
                    act.wait_ge(w_loaded[b][u], (j + 1) * (32 if u < 2 else 16))
                    if not first(i):
                        act.wait_ge((unit0_used, gu_done, y_done)[u], i)
                    act.activation(wh[u][:], wf[b][u][:], ACT.Copy).then_inc(w_hi[u], 1)

                def hi_next(j, b, u):
                    hi(j + b, 1 - b, u)

                def x_hi(j, v):
                    act.wait_ge(x_done, j * 2 + (v + 1))
                    if not first(j):
                        act.wait_ge((unit0_used, gu_done)[v], j * 2)
                    act.activation(xh[:, HALF * v:HALF * v + HALF, :].rearrange("p k n -> p (k n)"),
                                   ps_xh[:].rearrange("p b n -> p (b n)"), ACT.Copy).then_inc(xh_out, 1)

                def body(j, b, i, last_pair):
                    last = last_pair and b == 1
                    if not last:
                        hi_next(j, b, 0)
                    if b == 1 and not last:
                        x_hi(j + 1, 0)
                    act.wait_ge(gu_done, i + 1)
                    if not first(i):
                        act.wait_ge(hid_done, i)
                    act.activation(act_g[:], ps_gu[:, 0, 0:HID], ACT.Silu).then_inc(silu_done, 1)
                    if not last:
                        hi_next(j, b, 1)
                    act.wait_ge(t_done, i + 1)
                    if not first(i):
                        act.wait_ge(y_done, i)
                    act.activation(hth[:].rearrange("p k n -> p (k n)"), ps_t[:, 0, 0:HID], ACT.Copy).then_inc(th_out, 1)
                    if b == 1 and not last:
                        x_hi(j + 1, 1)
                    act.wait_ge(y_done, i + 1)
                    if not first(i):
                        act.wait_ge(y_stored, i * 16)
                    act.activation(y[:], ps_y[:].rearrange("p b n -> p (b n)"), ACT.Copy).then_inc(y_out, 1)
                    if not last:
                        hi_next(j, b, 2)
                for u in range(3):
                    hi(0, 0, u)
                x_hi(0, 0)
                x_hi(0, 1)
                pairs(act, end, body)

            @block.gpsimd
            def _(pool):
                end = last_pair(pool)

                def lo(j, b):
                    for u in (1, 2):
                        pool.wait_ge(w_hi[u], j * 2 + (b + 1))
                        pool.tensor_tensor(wl[u][:], wf[b][u][:], wh[u][:].bitcast(F32),
                                           ALU.subtract).then_inc(w_lo[u], 1)
                for b in range(2):
                    lo(0, b)
                with pool.Fori(1, end + 1) as j:
                    for b in range(2):
                        lo(j, b)
                pool.wait_ge(added, 1)
                for t in range(TT):
                    for k in range(2):
                        pool.indirect_dma_start(rows_back[t][:, k, :], None, rows[:, :],
                                                bass.IndirectOffsetOnAxis(rt.slot_i[:, t, k:k + 1], 0)).then_inc(back[t], 16)

            @block.vector
            def _(dve):
                end = last_pair(dve)
                dve.wait_ge(ld, 16)
                dve.tensor_copy(slot[:], rt.slot[:]).then_inc(slot_done, 1)

                def choose(j):
                    dve.wait_ge(slot_done, j + 1)
                    for t in range(TT):
                        ins = dve.tensor_scalar(eq0[:, t, :], iota[:], slot[:, t, 0:1], None, ALU.is_equal)
                    ins.then_inc(eq_done, 1)
                    dve.wait_ge(eq_done, j + 1)
                    if not first(j):
                        dve.wait_ge(x_done, j * 2)
                    for t in range(TT):
                        ins = dve.scalar_tensor_tensor(pick[:, t, :], iota[:], slot[:, t, 1:2], eq0[:, t, :],
                                                       ALU.is_equal, ALU.add)
                    ins.then_inc(picked, 1)
                    dve.wait_ge(picked, j + 1)
                    dve.tensor_scalar(slot[:], slot[:], -2.0 * P, None, ALU.add).then_inc(slot_done, 1)

                def lo(j, b):
                    dve.wait_ge(w_hi[0], j * 2 + (b + 1))
                    dve.tensor_tensor(wl[0][:], wf[b][0][:], wh[0][:].bitcast(F32), ALU.subtract).then_inc(w_lo[0], 1)

                def x_lo(j, v):
                    dve.wait_ge(x_done, j * 2 + (v + 1))
                    if not first(j):
                        dve.wait_ge((unit0_used, gu_done)[v], j * 2)
                    dve.tensor_copy(xl[:, HALF * v:HALF * v + HALF, :].rearrange("p k n -> p (k n)"),
                                    ps_xl[:].rearrange("p b n -> p (b n)")).then_inc(xl_out, 1)

                def body(j, b, i, last_pair):
                    last = last_pair and b == 1
                    if b == 1 and not last:
                        x_lo(j + 1, 0)
                    if not last:
                        lo(j + b, 1 - b)
                    dve.wait_ge(silu_done, i + 1)
                    if not first(i):
                        dve.wait_ge(t_done, i)
                    dve.tensor_tensor(hid[:], act_g[:], ps_gu[:, 0, HID:512], ALU.mult).then_inc(hid_done, 1)
                    dve.wait_ge(th_out, i + 1)
                    dve.tensor_tensor(htl[:].rearrange("p k n -> p (k n)"), ps_t[:, 0, 0:HID],
                                      hth[:].rearrange("p k n -> p (k n)").bitcast(F32),
                                      ALU.subtract).then_inc(tl_out, 1)
                    if b == 1 and not last:
                        x_lo(j + 1, 1)
                        choose(j + 2)
                choose(0)
                lo(0, 0)
                x_lo(0, 0)
                x_lo(0, 1)
                choose(1)
                pairs(dve, end, body)
                dve.wait_ge(y_stored, end * 32 + 32)
                dve.tensor_copy(slot[:, 0, 0:1], slot[:, 0, 1:2]).then_inc(added, 1)
                for t in range(TT):
                    dve.tensor_scalar(g.h[:, t, :], g.h[:, t, :], ALPHA, None, ALU.mult).then_inc(scaled, 1)
                    dve.wait_ge(back[t], 32)
                    for k in range(2):
                        dve.wait_ge(scaled, 3 * t + k + 1)
                        dve.scalar_tensor_tensor(g.h[:, t, :], rows_back[t][:, k, :], rt.weight[:, t, k:k + 1],
                                                 g.h[:, t, :], ALU.mult, ALU.add).then_inc(scaled, 1)


CA_ROW = T + P
NSA_ROW = 2 * T
NSA_BIAS = 896


def stage_tables(g, a):
    nc = g.nc
    with Stage(nc, "tables") as st:
        tbl, onehot = st.sb("tbl", [32, NSA_H]), st.sb("onehot", [32, NSA_ROW])
        mask = st.sb("mask", [NSA_H, NSA_ROW])
        row = st.sb("row", [NSA_H, NSA_ROW])
        ca = st.sb("ca", [16, CA_ROW])
        ca_neg = st.sb("ca_neg", [16, CA_ROW])
        ps = st.ps("ps", 2)
        ld, mm, done, step, stored = (st.sem(x) for x in ("loaded", "mm", "done", "step", "stored"))
        with nc.Block() as block:
            @block.sync
            def _(sp):
                sp.dma_start(tbl[:], a["rel_bias"]).then_inc(ld, 16)
                sp.dma_start(onehot[:], a["c_t5_onehot"]).then_inc(ld, 16)
                sp.dma_start(mask[:], rows_of(a["c_t5_mask"], 0, NSA_ROW, NSA_H)).then_inc(ld, 16)
                sp.dma_start(ca[:, 0:2 * P + 1], a["ca_rel_bias_2"].rearrange("l h n -> (l h) n")).then_inc(ld, 16)
                sp.wait_ge(done, 2)
                sp.dma_start(g.nsa_rows, row[:]).then_inc(stored, 16)
                sp.dma_start(g.ca_rows, ca_neg[:]).then_inc(stored, 16)
                sp.wait_ge(stored, 32)

            @block.tensor
            def _(pe):
                pe.wait_ge(ld, 64)
                for j in range(2):
                    mm_ = pe.matmul(ps[0:NSA_H, j, :], tbl[:], onehot[:, 512 * j:512 * j + 512], start=True, stop=True)
                mm_.then_inc(mm, 1)

            @block.vector
            def _(dve):
                dve.wait_ge(mm, 1)
                dve.wait_ge(ld, 64)
                dve.scalar_tensor_tensor(row[:], ps[0:NSA_H].rearrange("p b n -> p (b n)"), -1.0, mask[:],
                                         ALU.mult, ALU.add).then_inc(done, 1)
                dve.tensor_copy(ca[:, 2 * P + 1:], ca[:, 2 * P:2 * P + 1].to_broadcast([16, CA_ROW - 2 * P - 1])).then_inc(step, 1)
                dve.wait_ge(step, 1)
                dve.tensor_scalar(ca_neg[:], ca[:], -1.0, None, ALU.mult).then_inc(done, 1)


def toeplitz(rows, head, width):
    n = rows.shape[1]
    return bass.AP(rows.tensor, rows.offset + head * n + n - (width + P - 1), [[1, P], [1, width]])


def backwards(tile, start, count, step=1):
    part = tile[:, 0:1]
    last = tile.shape[1] - 1
    return bass.AP(part.tensor, part.offset + last - start, [list(part.ap[0]), [-step, count]])


def nsa_blocks(a):
    w_kv, w_in = a["nsa_w_kv"], a["nsa_w_in"][0]

    def columns(w, c0, c1):
        def src(u):
            rows = slice(HALF * P * u, HALF * P * (u + 1))
            return [(c, w[rows, x:x + 256].rearrange("(k p) n -> p k n", p=P)) for c, x in ((0, c0), (256, c1))]
        return src
    return [(columns(w_kv, 0, 256), True), (columns(w_kv, 512, 1024), True), (columns(w_kv, 768, 1280), False),
            (columns(w_in, 0, 256), True), (columns(w_in, 512, 768), True)]


def stage_nsa_project(g, a, run, nxt, n):
    nc = g.nc
    w_in, blocks = a["nsa_w_in"][0], nsa_blocks(a)
    with Stage(nc, "nproj") as st:
        ws = run.attach(st)
        narrow = NarrowProduct(g, st, 3 * NSA_H)
        pos_t, pos_loaded = st.sb("pos", [P, 2, 16]), st.sem("pos_loaded")
        e = st.sb("e", [P, TT, 48])
        c_loaded, g_exp, step, zeroed = st.sem("cmp_loaded"), st.sem("g_exp"), st.sem("step"), st.sem("zeroed")
        with nc.Block() as block:
            @block.sync
            def _(sp):
                sp.dma_start(narrow.w[:], w_in[:, NSA_H * DH:].rearrange("(k p) n -> p k n", p=P)).then_inc(narrow.loaded, 16)
                for b in range(1, len(blocks)):
                    ws.load(sp, b)
                nxt.load_first(sp)
                for i, x in enumerate("kv"):
                    pos = a[f"cmp_{x}_pos"].rearrange("l d -> (l d)").rearrange("(c p) -> p c", p=P)
                    sp.dma_start(pos_t[:, i, :], pos, allow_slow_non_contiguous=True).then_inc(pos_loaded, 16)
                    for c in range(16):
                        sp.dma_start(n.w1[:, i, c], a[f"cmp_{x}_w1"][P * c:P * c + P, :]).then_inc(c_loaded, 16)
                for half in range(2):
                    sp.dma_start(n.w2k[:, half, :], a["cmp_k_w2"]).then_inc(c_loaded, 16)
                sp.dma_start(n.w2v[:], a["cmp_v_w2"]).then_inc(c_loaded, 16)
                sp.wait_ge(c_loaded, 16 * 35)

            @block.tensor
            def _(pe):
                narrow.multiply(pe)
                narrow.turn(pe)
                for b, (_, stationary) in enumerate(blocks):
                    ws.multiply(pe, b, g.xh, g.xl, stationary)

            @block.gpsimd
            def _(pool):
                pool.memset(n.raw[:, :, NSA_G, :], 0.0).then_inc(zeroed, 1)
                ws.lo(pool, 0, (1,))
                for b in range(1, len(blocks)):
                    ws.lo(pool, b)
                pool.wait_ge(zeroed, 1)
                pool.wait_ge(pos_loaded, 32)
                pool.tensor_copy(n.raw[:, :, NSA_G, 0:32:2], pos_t[:]).then_inc(zeroed, 1)
                nxt.lo_first(pool)

            @block.scalar
            def _(act):
                for b in range(len(blocks)):
                    for u in range(2):
                        if (b, u) != (0, 0):
                            ws.hi(act, b, u)
                    if b == 0:
                        act.wait_ge(narrow.turned, 1)
                        act.activation(e[:].rearrange("p t n -> p (t n)"), narrow.out, ACT.Exp,
                                       scale=-1.0).then_inc(g_exp, 1)

                nxt.hi_first(act, before=ws)

            @block.vector
            def _(dve):
                link = Link(dve, step)
                narrow.split(dve, 16)
                narrow.copy(dve)
                dve.wait_ge(g_exp, 1)
                link(dve.tensor_scalar(e[:], e[:], 1.0, None, ALU.add))
                link(dve.reciprocal(n.gate[:], e[:]))
                for b in range(len(blocks)):
                    for s in range(4):
                        dve.wait_ge(ws.acc_ready, 4 * b + s + 1)
                        acc = ws.acc[:, s, :]
                        if b == 0:
                            for grp in range(2):
                                for half in range(2):
                                    ins = dve.tensor_copy(n.raw[64 * half:64 * half + 64, s // 2, 2 * (s % 2) + grp, 0:T - half],
                                                          ws.acc[64 * grp:64 * grp + 64, s, half:])
                        elif b == 1:
                            for grp in range(2):
                                for half in range(2):
                                    ins = dve.tensor_copy(n.kt[64 * half:64 * half + 64, s // 2, 2 * (s % 2) + grp, :],
                                                          ws.acc[64 * grp:64 * grp + 64, s, :])
                        elif b == 2:
                            ins = dve.tensor_copy(n.v[:, s, :], acc)
                        else:
                            ins = dve.tensor_scalar(n.qt[:, 4 * (b - 3) + s, :], acc, -(DH ** -0.5), None, ALU.mult)
                        ins.then_inc(ws.evicted, 1)


def stage_nsa_compress(g, a, n):
    nc = g.nc
    with Stage(nc, "ncomp") as st:
        pb = st.sb("pb", [P, 2])
        hid = st.sb("hid", [P, 2, NSA_G, N_CMP])
        ps = st.ps("ps", 4)
        mm_hid, pb_done, hid_done, mm_out, done = (st.sem(x) for x in
            ("mm_hid", "pb_done", "hid_done", "mm_out", "done"))
        with nc.Block() as block:
            @block.tensor
            def _(pe):
                for i in range(2):
                    out = ps[:, i, 0:(NSA_G + 1) * N_CMP].rearrange("p (g n) -> p g n", n=N_CMP)
                    for c in range(16):
                        mm = pe.matmul(out, n.w1[:, i, c, :], n.raw[:, i, :, 2 * c:2 * c + 16 * (N_CMP - 1) + 1:16],
                                       start=(c == 0), stop=(c == 15))
                mm.then_inc(mm_hid, 1)
                pe.wait_ge(hid_done, 2)
                pe.matmul(ps[:, 2, 0:NSA_G * N_CMP], n.w2k[:].rearrange("p a d -> p (a d)"),
                          hid[:, 0].rearrange("p g n -> p (g n)"), start=True, stop=True)
                for grp in range(NSA_G):
                    mm = pe.matmul(ps[0:N_CMP, 3, DH * grp:DH * grp + DH], hid[:, 1, grp, :], n.w2v[:],
                                   start=True, stop=True)
                mm.then_inc(mm_out, 1)

            @block.scalar
            def _(act):
                act.wait_ge(pb_done, 1)
                for i in range(2):
                    act.activation(hid[:, i].rearrange("p g n -> p (g n)"), ps[:, i, 0:NSA_G * N_CMP],
                                   ACT.Silu, bias=pb[:, i:i + 1]).then_inc(hid_done, 1)

            @block.vector
            def _(dve):
                dve.wait_ge(mm_hid, 1)
                dve.tensor_copy(pb[:], ps[:, 0:2, NSA_G * N_CMP]).then_inc(pb_done, 1)
                dve.wait_ge(mm_out, 1)
                dve.tensor_copy(n.kct[:].rearrange("p g n -> p (g n)"), ps[:, 2, 0:NSA_G * N_CMP]).then_inc(done, 1)
                dve.tensor_copy(n.vc[:].rearrange("p g n -> p (g n)"), ps[0:N_CMP, 3, 0:NSA_G * DH]).then_inc(done, 1)


def stage_nsa_cmp(g, a, n):
    nc = g.nc
    H4, W = 4, 16 * N_CMP
    with Stage(nc, "ncmp") as st:
        bias = [st.sb(f"bias{i}", [P, NSA_BIAS]) for i in range(4)]
        valid = st.sb("valid", [P, TT, N_CMP])
        s = [st.sb(f"s{i}", [P, H4, TT, N_CMP]) for i in range(2)]
        m, l, r = ([st.sb(f"{x}{i}", [P, H4, TT]) for i in range(2)] for x in "mlr")
        ps, pt = st.ps("ps", 4), st.ps("pt", 4)
        b_loaded = [st.sem(f"b_loaded{i}") for i in range(4)]
        ld, b_used, s_ready, v1, a1, p_done, t_done, out, step = (st.sem(x) for x in
            ("loaded", "b_used", "s_ready", "shifted", "exped", "p_done", "t_done", "out", "step"))
        with nc.Block() as block:
            @block.sync
            def _(sp):
                sp.dma_start(valid[:], a["c_cmp_valid"]).then_inc(ld, 16)
                for h in range(NSA_H):
                    if h >= 4:
                        sp.wait_ge(b_used, h - 3)
                    sp.dma_start(bias[h % 4][:], toeplitz(g.nsa_rows, h, NSA_BIAS)).then_inc(b_loaded[h % 4], 16)

            @block.tensor
            def _(pe):
                def scores(grp):
                    if grp >= 2:
                        pe.wait_ge(b_used, 4 * (grp - 1))
                    for hh in range(H4):
                        h = 4 * grp + hh
                        rows = slice(64 * (h % 2), 64 * (h % 2) + 64)
                        for t in range(TT):
                            c = (hh // 2 * TT + t) * N_CMP
                            mm = pe.matmul(ps[:, 2 * (grp % 2) + h % 2, c:c + N_CMP],
                                           n.qt[rows, h // 2, P * t:P * t + P],
                                           n.kct[rows, grp, :], start=True, stop=True)
                    mm.then_inc(s_ready, 1)
                scores(0)
                for grp in range(NSA_G):
                    if grp + 1 < NSA_G:
                        scores(grp + 1)
                    pe.wait_ge(p_done, grp + 1)
                    for hh in range(H4):
                        if grp >= 1:
                            pe.wait_ge(out, 4 * (grp - 1) + hh + 1)
                        for t in range(TT):
                            mm = pe.transpose(pt[0:N_CMP, hh, P * t:P * t + P], s[grp % 2][:, hh, t, :], g.ident[:])
                        mm.then_inc(t_done, 1)

            @block.vector
            def _(dve):
                link = Link(dve, step)
                dve.wait_ge(ld, 16)
                for grp in range(NSA_G):
                    x, mm_, ll, rr = s[grp % 2], m[grp % 2], l[grp % 2], r[grp % 2]
                    dve.wait_ge(s_ready, grp + 1)
                    if grp >= 2:
                        dve.wait_ge(t_done, 4 * (grp - 1))
                    for hh in range(H4):
                        h = 4 * grp + hh
                        dve.wait_ge(b_loaded[h % 4], 16 * (h // 4 + 1))
                        c = (hh // 2) * TT * N_CMP
                        for t in range(TT):
                            x0 = 384 - P * t + 31
                            ins = dve.tensor_tensor(x[:, hh, t, :], ps[:, 2 * (grp % 2) + h % 2, c + t * N_CMP:c + (t + 1) * N_CMP],
                                                    backwards(bias[h % 4], x0, N_CMP, 16), ALU.add)
                        ins.then_inc(b_used, 1)
                    dve.wait_ge(b_used, 4 * grp + 4)
                    link(dve.tensor_reduce(mm_[:], x[:], AX.X, ALU.min))
                    for hh in range(H4):
                        ins = dve.tensor_tensor(x[:, hh], x[:, hh], mm_[:, hh].unsqueeze(2).to_broadcast([P, TT, N_CMP]),
                                                ALU.subtract)
                    ins.then_inc(v1, 1)
                    dve.wait_ge(a1, grp + 1)
                    link(dve.tensor_reduce(ll[:], x[:], AX.X, ALU.add))
                    link(dve.reciprocal(rr[:], ll[:]))
                    gate = n.gate[:, :, 12 * grp:12 * grp + 12].rearrange("p t (h b) -> p h t b", b=3)[:, :, :, 0]
                    link(dve.tensor_tensor(rr[:], rr[:], gate, ALU.mult))
                    for hh in range(H4):
                        ins = dve.tensor_tensor(x[:, hh], x[:, hh], rr[:, hh].unsqueeze(2).to_broadcast([P, TT, N_CMP]),
                                                ALU.mult)
                    link(ins)
                    for hh in range(H4):
                        ins = dve.tensor_tensor(x[:, hh], x[:, hh], valid[:], ALU.mult)
                    ins.then_inc(p_done, 1)

            @block.scalar
            def _(act):
                for grp in range(NSA_G):
                    act.wait_ge(v1, grp + 1)
                    act.activation(s[grp % 2][:], s[grp % 2][:], ACT.Exp, scale=-1.0).then_inc(a1, 1)
                    for hh in range(H4):
                        act.wait_ge(t_done, 4 * grp + hh + 1)
                        act.activation(n.pct[:, 4 * grp + hh, :], pt[0:N_CMP, hh, :], ACT.Copy).then_inc(out, 1)


def attend(g, name, heads, branches, q, k, v, bias_rows, bias_width, bias, gate, extra, finish, mask=None):
    nc = g.nc
    nb = branches
    U = heads * TT
    with Stage(nc, name) as st:
        s = [st.sb(f"s{i}", [P, nb, T]) for i in range(3)]
        m, l, r = ([st.sb(f"{x}{i}", [P, nb]) for i in range(3)] for x in "mlr")
        ptb = [st.sb(f"pt{i}", [P, nb, T]) for i in range(2)]
        bt = [st.sb(f"bias{i}", [P, bias_width]) for i in range(2)]
        mt = st.sb("mask", [P, P]) if mask is not None else None
        fin = finish(st)
        ps_s, ps_t, ps_o = [st.ps(f"pss{i}", nb) for i in range(2)], [st.ps(f"pst{i}", nb) for i in range(2 if nb == 1 else 1)], \
            [st.ps(f"pso{i}", 1) for i in range(2)]
        m_loaded, masked = st.sem("m_loaded"), st.sem("masked")
        b_loaded = [st.sem(f"b_loaded{i}") for i in range(2)]
        s_ready, reduced, exped, normed, turned, copied, o_done, o_read, r_step = (st.sem(x) for x in
            ("s_ready", "reduced", "exped", "normed", "turned", "copied", "o_done", "o_read", "r_step"))
        fin.o_done = o_done
        nt = len(ps_t)

        def unit(u):
            return u // TT, u % TT, P * (u % TT + 1)

        with nc.Block() as block:
            @block.sync
            def _(sp):
                if mask is not None:
                    sp.dma_start(mt[:], mask[:, 0:P]).then_inc(m_loaded, 16)
                for h in range(heads):
                    if h >= 2:
                        sp.wait_ge(reduced, TT * (h - 1))
                    sp.dma_start(bt[h % 2][:], bias_rows(h)).then_inc(b_loaded[h % 2], 16)

            @block.gpsimd
            def _(pool):
                if mask is not None:
                    pool.wait_ge(m_loaded, 16)
                    for h in range(heads):
                        pool.wait_ge(b_loaded[h % 2], 16 * (h // 2 + 1))
                        diag = bt[h % 2][:, 0:P]
                        pool.tensor_tensor(diag, diag, mt[:], ALU.add).then_inc(masked, 1)

            @block.tensor
            def _(pe):
                for n in range(-1, U + 3):
                    u = n + 1
                    if u < U:
                        h, i, width = unit(u)
                        if u >= 2:
                            pe.wait_ge(reduced, u - 1)
                        for b in range(nb):
                            mm = pe.matmul(ps_s[u % 2][:, b, 0:width], q(h, i), k(h, b, width), start=True, stop=True)
                        mm.then_inc(s_ready, 1)
                    if 0 <= n - 2 < U:
                        u = n - 2
                        h, i, width = unit(u)
                        pe.wait_ge(normed, u + 1)
                        if u >= nt:
                            pe.wait_ge(copied, u - nt + 1)
                        for b in range(nb):
                            for kt in range(i + 1):
                                mm = pe.transpose(ps_t[u % nt][:, b, P * kt:P * kt + P], s[u % 3][:, b, P * kt:P * kt + P],
                                                  g.ident[:])
                        mm.then_inc(turned, 1)
                    if 0 <= n - 3:
                        u = n - 3
                        h, i, width = unit(u)
                        pe.wait_ge(copied, u + 1)
                        half = h % 2
                        if i == 0 and half == 0 and h >= 4:
                            pe.wait_ge(o_read, h // 2 - 1)
                        out = ps_o[(h // 2) % 2][64 * half:64 * half + 64, 0, P * i:P * i + P]
                        parts = [(v(h, b, kt), ptb[u % 2][:, b, P * kt:P * kt + P])
                                 for b in range(nb) for kt in range(i + 1)] + extra(h, i)
                        for j, (lhs, rhs) in enumerate(parts):
                            mm = pe.matmul(out, lhs, rhs, start=(j == 0), stop=(j == len(parts) - 1))
                        mm.then_inc(o_done, 1)

            @block.scalar
            def _(act):
                for n in range(U + 3):
                    if 0 <= n - 3 and (n - 3) % (2 * TT) == 2 * TT - 1:
                        fin.act(act, (n - 3) // (2 * TT), ps_o, o_done)
                    if 0 <= n - 2 < U:
                        u = n - 2
                        act.wait_ge(turned, u + 1)
                        if u >= 2:
                            act.wait_ge(o_done, u - 1)
                        width = unit(u)[2]
                        act.activation(ptb[u % 2][:, :, 0:width], ps_t[u % nt][:, :, 0:width], ACT.Copy).then_inc(copied, 1)
                    if n < U:
                        act.wait_ge(reduced, n + 1)
                        width = unit(n)[2]
                        for b in range(nb):
                            ins = act.activation(s[n % 3][:, b, 0:width], s[n % 3][:, b, 0:width], ACT.Exp, scale=-1.0,
                                                 bias=m[n % 3][:, b:b + 1], accum_out=l[n % 3][:, b:b + 1])
                        ins.then_inc(exped, 1)

            @block.vector
            def _(dve):
                for n in range(U + 3):
                    if n < U:
                        h, i, width = unit(n)
                        if mask is None:
                            dve.wait_ge(b_loaded[h % 2], 16 * (h // 2 + 1))
                        else:
                            dve.wait_ge(masked, h + 1)
                        dve.wait_ge(s_ready, n + 1)
                        if n >= 3:
                            dve.wait_ge(turned, n - 2)
                        bias_ap = bias(bt[h % 2], h, i, width)
                        for b in range(nb):
                            ins = dve.tensor_tensor_reduce(s[n % 3][:, b, 0:width], ps_s[n % 2][:, b, 0:width], bias_ap,
                                                           1.0, 3e38, ALU.add, ALU.min, m[n % 3][:, b:b + 1])
                        ins.then_inc(reduced, 1)
                    if 0 <= n - 1 < U:
                        u = n - 1
                        h, i, width = unit(u)
                        dve.wait_ge(exped, u + 1)
                        dve.reciprocal(r[u % 3][:], l[u % 3][:]).then_inc(r_step, 1)
                        steps = 2 if gate else 1
                        dve.wait_ge(r_step, steps * u + 1)
                        if gate:
                            dve.tensor_tensor(r[u % 3][:], r[u % 3][:], gate(h, i), ALU.mult).then_inc(r_step, 1)
                            dve.wait_ge(r_step, steps * u + 2)
                        for b in range(nb):
                            ins = dve.tensor_scalar(s[u % 3][:, b, 0:width], s[u % 3][:, b, 0:width],
                                                    r[u % 3][:, b:b + 1], None, ALU.mult)
                        ins.then_inc(normed, 1)
                    if 0 <= n - 3 and (n - 3) % (2 * TT) == 2 * TT - 1:
                        fin.dve(dve, (n - 3) // (2 * TT), ps_o, o_read)


class SplitOutput:

    def __init__(self, st, heads, hi, lo, factor=None):
        self.hi, self.lo, self.factor, self.heads = hi, lo, factor, heads
        self.hi_done, self.y_done = st.sem("hi_done"), st.sem("y_done")
        self.y = [st.sb(f"y{i}", [P, T]) for i in range(2)] if factor is not None else None

    def act(self, act, j, ps_o, o_done):
        if self.factor is None:
            act.wait_ge(o_done, 2 * TT * (j + 1))
            act.activation(self.hi[:, j, :], ps_o[j % 2][:, 0, :], ACT.Copy).then_inc(self.hi_done, 1)
        else:
            act.wait_ge(self.y_done, j + 1)
            act.activation(self.hi[:, j, :], self.y[j % 2][:], ACT.Copy).then_inc(self.hi_done, 1)

    def dve(self, dve, j, ps_o, o_read):
        if self.factor is None:
            dve.wait_ge(self.hi_done, j + 1)
            dve.tensor_tensor(self.lo[:, j, :], ps_o[j % 2][:, 0, :], self.hi[:, j, :].bitcast(F32),
                              ALU.subtract).then_inc(o_read, 1)
        else:
            dve.wait_ge(self.o_done, 2 * TT * (j + 1))
            dve.tensor_tensor(self.y[j % 2][:], ps_o[j % 2][:, 0, :], self.factor[:, j, :],
                              ALU.mult).then_inc(self.y_done, 1)
            dve.wait_ge(self.hi_done, j + 1)
            dve.tensor_tensor(self.lo[:, j, :], self.y[j % 2][:], self.hi[:, j, :].bitcast(F32),
                              ALU.subtract).then_inc(o_read, 1)


def stage_nsa_attend(g, a, n):
    def half(h):
        return slice(64 * (h % 2), 64 * (h % 2) + 64)
    attend(g, "natt", NSA_H, 2,
           q=lambda h, i: n.qt[half(h), h // 2, P * i:P * i + P],
           k=lambda h, b, w: n.kt[half(h), b, h // 4, 0:w],
           v=lambda h, b, kt: n.v[:, kt, 256 * b + DH * (h // 4):256 * b + DH * (h // 4) + DH],
           bias_rows=lambda h: toeplitz(g.nsa_rows, h, NSA_BIAS), bias_width=NSA_BIAS,
           bias=lambda t, h, i, w: backwards(t, 384 - P * i, w),
           gate=lambda h, i: n.gate[:, i, 3 * h + 1:3 * h + 3],
           extra=lambda h, i: [(n.vc[:, h // 4, :], n.pct[:, h, P * i:P * i + P])],
           finish=lambda st: SplitOutput(st, NSA_H, g.xh, g.xl))


BW = 512
BF = BW // P
MH = 8
MLA_NOPE, MLA_ROPE, MLA_QK = 64, 32, 96
MLA_SCALE = MLA_QK ** -0.5
COL = {"u": 0, "va": 512, "za": 1024, "mla": 1536, "zb": 1952, "qc": 2464, "kc": 2976, "vc": 3488,
       "zc": 4000, "g": 4512}
MLA_COLS = 256 + 128 + 32


PARTS = {"b": [("mla", False), ("zb", True)],
         "c": [("qc", True), ("kc", True), ("vc", False), ("zc", True)],
         "a": [("va", False), ("u", True), ("za", True)]}


def branch_run(slots, a, layer, part):
    w = a["w_in_2"][layer]

    def width(b):
        return MLA_COLS if PARTS[part][b][0] == "mla" else BW

    def source(b):
        c = COL[PARTS[part][b][0]]

        def src(u):
            rows = slice(HALF * P * u, HALF * P * (u + 1))
            return [(0, w[rows, c:c + width(b)].rearrange("(k p) n -> p k n", p=P))]
        return src
    return WeightRun(slots, len(PARTS[part]), source, cols=width)


def stage_branch_project(g, a, layer, s, part, run, nxt):
    nc = g.nc
    order = PARTS[part]
    with Stage(nc, f"bproj{part}{layer}") as st:
        ws = run.attach(st)
        latent_loaded = st.sem("latent_loaded")
        with nc.Block() as block:
            @block.sync
            def _(sp):
                for b in range(1, len(order)):
                    ws.load(sp, b)
                if part == "b":
                    load_latent(sp, a, layer, s.latent, latent_loaded)
                nxt.load_first(sp)
                if part == "b":
                    sp.wait_ge(latent_loaded, 16 * LATENT_LOADS)

            @block.tensor
            def _(pe):
                for b, (name, stationary) in enumerate(order):
                    ws.multiply(pe, b, g.xh, g.xl, stationary, ws.cols(b))

            @block.gpsimd
            def _(pool):
                ws.lo(pool, 0, (1,))
                for b in range(1, len(order)):
                    ws.lo(pool, b)
                nxt.lo_first(pool)

            @block.scalar
            def _(act):
                def next_hi(b, u):
                    if b + 1 < len(order):
                        ws.hi(act, b + 1, u)
                    else:
                        nxt.hi_first(act, before=ws)

                ws.hi(act, 0, 1)
                for b, (name, _) in enumerate(order):
                    next_hi(b, 0)
                    for t in range(4):
                        if name in ("za", "zb", "zc"):
                            act.wait_ge(ws.acc_ready, 4 * b + t + 1)
                            act.wait_ge(ws.evicted, 4 * b + t)
                            act.activation(s.t[name][:, t, :], ws.acc[:, t, :], ACT.Silu).then_inc(ws.evicted, 1)
                    if b + 1 < len(order):
                        next_hi(b, 1)

            @block.vector
            def _(dve):
                for b, (name, _) in enumerate(order):
                    for t in range(4):
                        if name in ("za", "zb", "zc"):
                            continue
                        dve.wait_ge(ws.acc_ready, 4 * b + t + 1)
                        dve.wait_ge(ws.evicted, 4 * b + t)
                        if name == "qc":
                            ins = dve.tensor_scalar(s.t[name][:, t, :], ws.acc[:, t, :], -(DH ** -0.5), None, ALU.mult)
                        elif name == "mla":
                            ins = dve.tensor_copy(s.t[name][:, t, :], ws.acc[:, t, 0:MLA_COLS])
                        else:
                            ins = dve.tensor_copy(s.t[name][:, t, :], ws.acc[:, t, :])
                        ins.then_inc(ws.evicted, 1)


def stage_spatial_gate(g, a, layer, s):
    nc = g.nc
    G = 8
    with Stage(nc, f"sgu{layer}") as st:
        wraw, wt = st.sb("wraw", [P, G, P]), st.sb("wt", [P, G, P])
        gain, shift = st.sb("gain", [P, BW]), st.sb("shift", [P, BW])
        bias = st.sb("bias", [P, BF, P])
        stats, mv = st.sb("stats", [P, TT, 6]), st.sb("mv", [P, TT, 2])
        root, inv = st.sb("root", [P, TT]), st.sb("inv", [P, TT])
        uz = st.sb("uz", [P, BF, T])
        y = st.sb("y", [P, BF, T])
        ps_w, ps_m = st.ps("w", 2), st.ps("m", 4)
        ld, step, agg, rooted, normed, shifted = (st.sem(x) for x in ("loaded", "step", "agg", "rooted", "normed", "shifted"))
        w_t, w_done, mixed, y_step, hi_done, lo_done, uz_done = (st.sem(x) for x in
            ("w_turned", "w_done", "mixed", "y_step", "hi_done", "lo_done", "uz_done"))
        va = s.t["va"]
        with nc.Block() as block:
            @block.sync
            def _(sp):
                sp.dma_start(wraw[:], a["sgu_w_2"][layer].rearrange("g t s -> t g s")).then_inc(ld, 16)
                sp.dma_start(gain[:], rows_of(a["sgu_ln_g_2"], layer * BW, BW)).then_inc(ld, 16)
                sp.dma_start(shift[:], rows_of(a["sgu_ln_b_2"], layer * BW, BW)).then_inc(ld, 16)
                b = a["sgu_b_2"]
                for half in range(2):
                    sp.dma_start(bias[64 * half:64 * half + 64],
                                 bass.AP(b.tensor, b.offset + (layer * G + half) * P, [[0, 64], [2 * P, BF], [1, P]])
                                 ).then_inc(ld, 16)

            @block.tensor
            def _(pe):
                pe.wait_ge(ld, 80)
                for j in range(G):
                    mm = pe.transpose(ps_w[:, j // 4, P * (j % 4):P * (j % 4) + P], wraw[:, j, :], g.ident[:])
                mm.then_inc(w_t, 1)
                pe.wait_ge(w_done, 2)
                pe.wait_ge(shifted, TT)
                for f in range(BF):
                    for t in range(TT):
                        for half in range(2):
                            j = 2 * f + half
                            mm = pe.matmul(ps_m[64 * half:64 * half + 64, f, P * t:P * t + P],
                                           va[:, t, 64 * j:64 * j + 64], wt[:, j, :], start=True, stop=True)
                    mm.then_inc(mixed, 1)

            @block.vector
            def _(dve):
                for t in range(TT):
                    dve.bn_stats(stats[:, t, :], va[:, t, :]).then_inc(step, 1)
                    dve.wait_ge(step, t + 1)
                    dve.bn_aggr(mv[:, t, :], stats[:, t, :]).then_inc(agg, 1)
                dve.wait_ge(rooted, 1)
                dve.reciprocal(inv[:], root[:]).then_inc(step, 1)
                dve.wait_ge(step, TT + 1)
                dve.wait_ge(ld, 80)
                for t in range(TT):
                    dve.tensor_scalar(va[:, t, :], va[:, t, :], mv[:, t, 0:1], inv[:, t:t + 1],
                                      ALU.subtract, ALU.mult).then_inc(step, 1)
                    dve.wait_ge(step, TT + 2 + t)
                    dve.tensor_tensor(va[:, t, :], va[:, t, :], gain[:], ALU.mult).then_inc(normed, 1)
                dve.wait_ge(w_t, 1)
                for j in range(2):
                    dve.tensor_tensor(wt[:, 4 * j:4 * j + 4, :], ps_w[:, j, :].rearrange("p (a n) -> p a n", a=4),
                                      g.triu[:].unsqueeze(1).to_broadcast([P, 4, P]), ALU.mult).then_inc(w_done, 1)
                for f in range(BF):
                    dve.wait_ge(mixed, f + 1)
                    dve.tensor_tensor(y[:, f, :].rearrange("p (t n) -> p t n", t=TT),
                                      ps_m[:, f, :].rearrange("p (t n) -> p t n", t=TT),
                                      bias[:, f:f + 1, :].to_broadcast([P, TT, P]), ALU.add).then_inc(y_step, 1)
                    dve.wait_ge(y_step, 2 * f + 1)
                    dve.wait_ge(uz_done, 1)
                    dve.tensor_tensor(y[:, f, :], y[:, f, :], uz[:, f, :], ALU.mult).then_inc(y_step, 1)
                    dve.wait_ge(hi_done, f + 1)
                    dve.tensor_tensor(s.yl[0][:, f, :], y[:, f, :], s.yh[0][:, f, :].bitcast(F32), ALU.subtract).then_inc(lo_done, 1)

            @block.gpsimd
            def _(pool):
                for t in range(TT):
                    pool.wait_ge(normed, t + 1)
                    pool.tensor_tensor(va[:, t, :], va[:, t, :], shift[:], ALU.add).then_inc(shifted, 1)
                pool.tensor_tensor(uz[:], s.t["u"][:], s.t["za"][:], ALU.mult).then_inc(uz_done, 1)

            @block.scalar
            def _(act):
                act.wait_ge(agg, TT)
                act.activation(root[:], mv[:, :, 1], ACT.Sqrt, bias=g.eps6[:]).then_inc(rooted, 1)
                for f in range(BF):
                    act.wait_ge(y_step, 2 * f + 2)
                    act.activation(s.yh[0][:, f, :], y[:, f, :], ACT.Copy).then_inc(hi_done, 1)


LATENT_LOADS = 13


def latent_tiles(sb):
    return (sb("uq", [P, 2, MH * MLA_QK]), sb("usw", [P, 2, MH, MLA_ROPE]), sb("kn", [P, MH, MLA_NOPE]),
            sb("kv", [P, MH, 64]), sb("gain", [P, 384]), sb("ropec", [P, T]), sb("ropes", [P, T]),
            sb("kcos", [P, TT, 16]), sb("ksin", [P, TT, 16]))


def load_latent(sp, a, layer, tiles, ld):
    uq, usw, kn, kv, gain, cq, sq_, kc, ks = tiles
    w_uq, w_kv = a["mla_w_uq_2"][layer], a["mla_w_ukv_2"][layer]
    sp.dma_start(gain[:, 0:256], rows_of(a["mla_q_norm_g_2"], layer * 256, 256)).then_inc(ld, 16)
    sp.dma_start(gain[:, 256:], rows_of(a["mla_kv_norm_g_2"], layer * 128, 128)).then_inc(ld, 16)
    sp.dma_start(kc[:], a["c_rope_cos"]).then_inc(ld, 16)
    sp.dma_start(ks[:], a["c_rope_sin"]).then_inc(ld, 16)
    sp.dma_start(cq[:], a["c_ropeq_cos"]).then_inc(ld, 16)
    sp.dma_start(sq_[:], a["c_ropeq_sin"]).then_inc(ld, 16)
    sp.dma_start(uq[:], w_uq.rearrange("(k p) n -> p k n", p=P)).then_inc(ld, 16)
    v = w_uq.rearrange("(k p) (h n) -> k p h n", p=P, n=MLA_QK)
    for k in range(2):
        sp.dma_start(usw[:, k, :, 0:16], v[k, :, :, 80:96]).then_inc(ld, 16)
        sp.dma_start(usw[:, k, :, 16:32], v[k, :, :, 64:80]).then_inc(ld, 16)
    v = w_kv.rearrange("p (h n) -> p h n", n=128)
    sp.dma_start(kn[:], v[:, :, 0:64]).then_inc(ld, 16)
    sp.dma_start(kv[:], v[:, :, 64:128]).then_inc(ld, 16)


def stage_latent(g, a, layer, s):
    nc = g.nc
    x = s.t["mla"]
    with Stage(nc, f"mla{layer}") as st:
        uq, usw, kn, kv, gain, cq, sq_, kc, ks = s.latent
        junk = st.sb("junk", [P, 256])
        ms, root, inv = st.sb("ms", [P, TT, 2]), st.sb("root", [P, TT, 2]), st.sb("inv", [P, TT, 2])
        kr, t1, t2 = st.sb("kr", [P, TT, MLA_QK]), st.sb("t1", [P, TT, 16]), st.sb("t2", [P, TT, 16])
        xt = st.sb("xt", [P, 3, T])
        r1, r2 = st.sb("r1", [P, T]), st.sb("r2", [P, T])
        ps_t, ps_q, ps_s, ps_k = st.ps("t", 2), st.ps("q", 2), st.ps("sw", 2), st.ps("k", 2)
        step, sq_done, rooted, zeroed = (st.sem(z) for z in ("step", "squared", "rooted", "zeroed"))
        ready, turned, taken, q_done, q_nope, q_rope = (st.sem(z) for z in
            ("ready", "turned", "taken", "q_done", "q_nope", "q_rope"))
        kv_taken = st.sem("kv_taken")
        k_done, k_out, sw_done, kr_out = st.sem("k_done"), st.sem("k_out"), st.sem("sw_done"), st.sem("kr_out")
        with nc.Block() as block:
            @block.gpsimd
            def _(pool):
                pool.memset(kr[:, :, 0:64], 0.0).then_inc(zeroed, 1)

            @block.scalar
            def _(act):
                for t in range(TT):
                    act.activation(junk[:], x[:, t, 0:256], ACT.Square, scale=1.0 / 16,
                                   accum_out=ms[:, t, 0:1]).then_inc(sq_done, 1)
                    act.wait_ge(sq_done, 2 * t + 1)
                    act.activation(junk[:, 0:128], x[:, t, 256:384], ACT.Square, scale=128 ** -0.5,
                                   accum_out=ms[:, t, 1:2]).then_inc(sq_done, 1)
                    act.wait_ge(sq_done, 2 * t + 2)
                act.activation(root[:], ms[:], ACT.Sqrt, bias=g.eps6[:]).then_inc(rooted, 1)
                act.wait_ge(turned, 3)
                act.activation(xt[:, 2, :], ps_t[:, 0, :], ACT.Copy).then_inc(kv_taken, 1)
                for h in range(MH):
                    act.wait_ge(q_done, h + 1)
                    act.activation(s.mq[0:64, h, :], ps_q[0:64, h % 2, :], ACT.Copy, scale=-MLA_SCALE).then_inc(q_nope, 1)

            @block.tensor
            def _(pe):
                pe.wait_ge(ready, 1)
                for j in range(3):
                    if j == 2:
                        pe.wait_ge(taken, 1)
                    for t in range(TT):
                        mm = pe.transpose(ps_t[:, j % 2, P * t:P * t + P], x[:, t, P * j:P * j + P], g.ident[:])
                    mm.then_inc(turned, 1)
                pe.wait_ge(taken, 2)
                for t in range(TT):
                    mm = pe.transpose(ps_t[0:MLA_QK, 1, P * t:P * t + P], kr[:, t, :], g.ident[:])
                mm.then_inc(turned, 1)
                pe.wait_ge(kv_taken, 1)
                for j in range(2):
                    for k in range(2):
                        mm = pe.matmul(ps_s[:, j, :], usw[:, k, 4 * j:4 * j + 4, :].rearrange("p h n -> p (h n)"),
                                       xt[:, k, :], start=(k == 0), stop=(k == 1))
                mm.then_inc(sw_done, 1)
                for h in range(MH):
                    if h >= 2:
                        pe.wait_ge(q_nope, h - 1)
                        pe.wait_ge(q_rope, h - 1)
                    for k in range(2):
                        mm = pe.matmul(ps_q[0:MLA_QK, h % 2, :], uq[:, k, MLA_QK * h:MLA_QK * h + MLA_QK], xt[:, k, :],
                                       start=(k == 0), stop=(k == 1))
                    mm.then_inc(q_done, 1)
                    if h >= 2:
                        pe.wait_ge(k_out, h - 1)
                    if h < 4:
                        mm = pe.matmul(ps_k[:, h % 2, :], kn[:, 2 * h:2 * h + 2, :].rearrange("p h n -> p (h n)"),
                                       xt[:, 2, :], start=True, stop=True)
                    else:
                        t = h - 4
                        mm = pe.matmul(ps_k[:, h % 2, :], xt[:, 2, P * t:P * t + P], kv[:].rearrange("p h n -> p (h n)"),
                                       start=True, stop=True)
                    mm.then_inc(k_done, 1)

            @block.vector
            def _(dve):
                link = Link(dve, step)
                dve.wait_ge(rooted, 1)
                dve.wait_ge(zeroed, 1)
                link(dve.reciprocal(inv[:], root[:]))
                for t in range(TT):
                    dve.scalar_tensor_tensor(x[:, t, 0:256], x[:, t, 0:256], inv[:, t, 0:1], gain[:, 0:256],
                                             ALU.mult, ALU.mult)
                    dve.scalar_tensor_tensor(x[:, t, 256:384], x[:, t, 256:384], inv[:, t, 1:2], gain[:, 256:],
                                             ALU.mult, ALU.mult)
                x1, x2 = x[:, :, 384:400], x[:, :, 400:416]
                dve.tensor_tensor(t1[:], x1, kc[:], ALU.mult)
                link(dve.tensor_tensor(t2[:], x2, ks[:], ALU.mult))
                link(dve.tensor_tensor(kr[:, :, 64:80], t1[:], t2[:], ALU.subtract))
                dve.tensor_tensor(t1[:], x1, ks[:], ALU.mult)
                link(dve.tensor_tensor(t2[:], x2, kc[:], ALU.mult))
                dve.tensor_tensor(kr[:, :, 80:96], t1[:], t2[:], ALU.add).then_inc(ready, 1)
                for j in range(2):
                    dve.wait_ge(turned, j + 1)
                    dve.tensor_copy(xt[:, j, :], ps_t[:, j, :]).then_inc(taken, 1)
                dve.wait_ge(turned, 4)
                for h in range(MH):
                    ins = dve.tensor_copy(s.mk[64:96, h, :], ps_t[64:96, 1, :])
                ins.then_inc(kr_out, 1)
                dve.wait_ge(sw_done, 1)
                n_step = link.n
                for h in range(MH):
                    if h < 4:
                        dve.wait_ge(k_done, h + 1)
                        dve.tensor_copy(s.mk[0:64, 2 * h, :], ps_k[0:64, h % 2, :])
                        dve.tensor_copy(s.mk[0:64, 2 * h + 1, :], ps_k[64:128, h % 2, :]).then_inc(k_out, 1)
                    else:
                        dve.wait_ge(k_done, h + 1)
                        dve.tensor_copy(s.mv[:, h - 4, :], ps_k[:, h % 2, :]).then_inc(k_out, 1)
                    dve.wait_ge(q_nope, h + 1)
                    j = 32 * (h % 4)
                    dve.tensor_tensor(r1[64:96, :], ps_q[64:96, h % 2, :], cq[64:96, :], ALU.mult)
                    link(dve.tensor_tensor(r2[64:96, :], ps_s[j:j + 32, h // 4, :], sq_[j:j + 32, :], ALU.mult))
                    dve.tensor_tensor(s.mq[64:96, h, :], r1[64:96, :], r2[64:96, :], ALU.add).then_inc(q_rope, 1)
                    dve.wait_ge(q_rope, h + 1)


def stage_latent_attend(g, a, layer, s):
    attend(g, f"matt{layer}", MH, 1,
           q=lambda h, i: s.mq[:, h, P * i:P * i + P],
           k=lambda h, b, w: s.mk[:, h, 0:w],
           v=lambda h, b, kt: s.mv[:, kt, 64 * h:64 * h + 64],
           bias_rows=lambda h: a["c_block_bias"], bias_width=T,
           bias=lambda t, h, i, w: backwards(t, 384 - P * i, w),
           gate=None, extra=lambda h, i: [],
           finish=lambda st: SplitOutput(st, MH, s.yh[1], s.yl[1], s.t["zb"]))


def stage_band_attend(g, a, layer, s):
    def half(h):
        return slice(64 * (h % 2), 64 * (h % 2) + 64)
    attend(g, f"batt{layer}", MH, 1,
           q=lambda h, i: s.t["qc"][half(h), h // 2, P * i:P * i + P],
           k=lambda h, b, w: s.t["kc"][half(h), h // 2, 0:w],
           v=lambda h, b, kt: s.t["vc"][:, kt, 64 * h:64 * h + 64],
           bias_rows=lambda h: toeplitz(g.ca_rows, MH * layer + h, T), bias_width=T,
           bias=lambda t, h, i, w: backwards(t, 384 - P * i, w),
           gate=None, extra=lambda h, i: [], mask=a["c_block_bias"],
           finish=lambda st: SplitOutput(st, MH, s.yh[2], s.yl[2], s.t["zc"]))


def gate_run(slots, a, layer):
    return WeightRun(slots, 6, lambda r: column_block(a["w_in_2"][layer], 0, COL["g"] + 512 * r))


def stage_merge(g, a, layer, s, run, nxt):
    nc = g.nc
    wb = a["w_branch_2"][layer]
    with Stage(nc, f"merge{layer}") as st:
        ws = run.attach(st)
        wf = st.sb("bwf", [P, HALF, 512])
        wh, wl = st.sb("bwh", [P, HALF, 512], F32R), st.sb("bwl", [P, HALF, 512], F32R)
        merged = st.sb("merged", [P, KT, T])
        gate, prod = st.sb("gate", [P, 4, T]), st.sb("prod", [P, 2, T])
        gb = st.sb("gb", [P, 3, KT])
        ps_b = st.ps("b", 4)
        ld, loaded, hi_ready, lo_ready = st.sem("loaded"), st.sem("bw_loaded"), st.sem("bw_hi"), st.sem("bw_lo")
        b_ready, b_out, added, hi_done, lo_done = (st.sem(x) for x in
            ("branch_acc", "branch_out", "added", "hi_done", "lo_done"))

        with nc.Block() as block:
            @block.sync
            def _(sp):
                for n in range(3):
                    sp.dma_start(gb[:, n, :], a["gate_b_2"][layer][n].rearrange("(k p) -> p k", p=P),
                                 allow_slow_non_contiguous=True).then_inc(ld, 16)
                for r in range(6):
                    n, j = r // 2, r % 2
                    if r > 0:
                        ws.load(sp, r)
                        sp.wait_ge(lo_ready, r)
                    sp.dma_start(wf[:], wb[n, :, 512 * j:512 * j + 512].rearrange("(k p) n -> p k n", p=P)) \
                        .then_inc(loaded, 16)
                nxt.load_first(sp)

            @block.tensor
            def _(pe):
                for r in range(6):
                    yh, yl = s.yh[r // 2], s.yl[r // 2]
                    ws.multiply(pe, r, g.xh, g.xl, True)
                    pe.wait_ge(lo_ready, r + 1)
                    for f in range(4):
                        if r > 0:
                            pe.wait_ge(b_out, 4 * (r - 1) + f + 1)
                        for k in range(HALF):
                            for m, (w, y) in enumerate(((wh, yh), (wh, yl), (wl, yh))):
                                mm = pe.matmul(ps_b[:, f, :], w[:, k, P * f:P * f + P], y[:, k, :],
                                               start=(k == 0 and m == 0), stop=(k == HALF - 1 and m == 2))
                        mm.then_inc(b_ready, 1)

            @block.gpsimd
            def _(pool):
                ws.lo(pool, 0, (1,))
                for r in range(6):
                    if r > 0:
                        ws.lo(pool, r)
                    pool.wait_ge(hi_ready, r + 1)
                    pool.tensor_tensor(wl[:], wf[:], wh[:].bitcast(F32), ALU.subtract).then_inc(lo_ready, 1)
                nxt.lo_first(pool)

            @block.scalar
            def _(act):
                ws.hi(act, 0, 1)
                act.wait_ge(ld, 48)

                def next_hi(r, u):
                    if r + 1 < 6:
                        ws.hi(act, r + 1, u)
                    elif u == 0:
                        nxt.hi_first(act, before=ws)

                for r in range(6):
                    n, j = r // 2, r % 2
                    act.wait_ge(loaded, 16 * (r + 1))
                    if r > 0:
                        act.wait_ge(b_ready, 4 * r)
                    act.activation(wh[:], wf[:], ACT.Copy).then_inc(hi_ready, 1)
                    next_hi(r, 0)
                    for f in range(4):
                        act.wait_ge(ws.acc_ready, 4 * r + f + 1)
                        if r > 0:
                            act.wait_ge(b_out, 4 * (r - 1) + f + 1)
                        act.activation(gate[:, f, :], ws.acc[:, f, :], ACT.Sigmoid,
                                       bias=gb[:, n, 4 * j + f:4 * j + f + 1]).then_inc(ws.evicted, 1)
                    next_hi(r, 1)
                act.wait_ge(b_ready, 24)
                for k in range(KT):
                    act.wait_ge(added, KT + k + 1)
                    act.activation(g.xh[:, k, :], merged[:, k, :], ACT.Copy).then_inc(hi_done, 1)

            @block.vector
            def _(dve):
                for r in range(6):
                    n, j = r // 2, r % 2
                    for f in range(4):
                        c = 4 * r + f + 1
                        dve.wait_ge(b_ready, c)
                        dve.wait_ge(ws.evicted, c)
                        out = merged[:, 4 * j + f, :]
                        if n == 0:
                            dve.tensor_tensor(out, gate[:, f, :], ps_b[:, f, :], ALU.mult).then_inc(b_out, 1)
                        else:
                            dve.tensor_tensor(prod[:, f % 2, :], gate[:, f, :], ps_b[:, f, :], ALU.mult).then_inc(b_out, 1)
                            dve.wait_ge(b_out, c)
                            dve.tensor_tensor(out, out, prod[:, f % 2, :], ALU.add).then_inc(added, 1)
                for k in range(KT):
                    dve.wait_ge(hi_done, k + 1)
                    dve.tensor_tensor(g.xl[:, k, :], merged[:, k, :], g.xh[:, k, :].bitcast(F32),
                                      ALU.subtract).then_inc(lo_done, 1)


def stage_branch_out(g, a, layer, run, nxt, store):
    nc = g.nc
    with Stage(nc, f"bout{layer}") as st:
        ws = run.attach(st)
        y, gain = st.sb("y", [P, TT, D]), st.sb("gain", [P, D])
        junk = st.sb("junk", [P, 512])
        ms, root, inv = st.sb("ms", [P, 2, TT]), st.sb("root", [P, TT]), st.sb("inv", [P, TT])
        ld, squared, summed, rooted, inverted, scaled, added, stored = (st.sem(x) for x in
            ("loaded", "squared", "summed", "rooted", "inverted", "scaled", "added", "stored"))
        with nc.Block() as block:
            @block.sync
            def _(sp):
                sp.dma_start(gain[:], rows_of(a["post_g_2"], layer * D, D)).then_inc(ld, 16)
                ws.load_rest(sp)
                if nxt is not None:
                    nxt.load_first(sp)
                if store is not None:
                    for t in range(TT):
                        sp.wait_ge(added, t + 1)
                        sp.dma_start(store[P * t:P * t + P, :], g.h[:, t, :]).then_inc(stored, 16)
                    sp.wait_ge(stored, 16 * TT)

            @block.tensor
            def _(pe):
                over(pe, 2, lambda b: ws.multiply(pe, b, g.xh, g.xl, False))

            @block.gpsimd
            def _(pool):
                ws.lo_rest(pool)
                if nxt is not None:
                    nxt.lo_first(pool)

            @block.scalar
            def _(act):
                def next_hi(b, u):
                    if b == 0:
                        ws.hi(act, 1, u)
                    elif nxt is not None:
                        nxt.hi_first(act, before=ws)

                ws.hi(act, 0, 1)
                for b in range(2):
                    next_hi(b, 0)
                    for t in range(TT):
                        n = 4 * b + t
                        act.wait_ge(ws.evicted, n + 1)
                        if n > 0:
                            act.wait_ge(squared, n)
                        act.activation(junk[:], y[:, t, 512 * b:512 * b + 512], ACT.Square,
                                       accum_out=ms[:, b, t:t + 1]).then_inc(squared, 1)
                    if b == 0:
                        next_hi(b, 1)
                act.wait_ge(summed, 1)
                act.activation(root[:], ms[:, 0, :], ACT.Sqrt, scale=1.0 / D, bias=g.eps6[:]).then_inc(rooted, 1)

            @block.vector
            def _(dve):
                def body(b):
                    for t in range(TT):
                        dve.wait_ge(ws.acc_ready, b * 4 + (t + 1))
                        dve.tensor_copy(y[:, t, bass.ds(b * 512, 512)], ws.acc[:, t, :]).then_inc(ws.evicted, 1)
                over(dve, 2, body)
                dve.wait_ge(squared, 2 * TT)
                dve.tensor_tensor(ms[:, 0, :], ms[:, 0, :], ms[:, 1, :], ALU.add).then_inc(summed, 1)
                dve.wait_ge(rooted, 1)
                dve.reciprocal(inv[:], root[:]).then_inc(inverted, 1)
                dve.wait_ge(inverted, 1)
                dve.wait_ge(ld, 16)
                for t in range(TT):
                    dve.scalar_tensor_tensor(y[:, t, :], y[:, t, :], inv[:, t:t + 1], gain[:],
                                             ALU.mult, ALU.mult).then_inc(scaled, 1)
                    dve.wait_ge(scaled, t + 1)
                    dve.tensor_tensor(g.h[:, t, :], g.h[:, t, :], y[:, t, :], ALU.add).then_inc(added, 1)


def layer_runs(slots, a, layer):
    return {**{part: branch_run(slots, a, layer, part) for part in "bca"}, "gates": gate_run(slots, a, layer),
            "out": WeightRun(slots, 2, lambda b: column_block(a["w_out_2"][layer], 0, b * 512))}


def branch_layer(g, a, layer, runs, nxt, store):
    nc = g.nc
    with ExitStack() as part:
        def psb(name, shape, dt=F32, ctx=part):
            return ctx.enter_context(nc.sbuf_tensor(f"br{layer}_{name}", shape, dt))
        s = Globals()
        s.yh, s.yl, s.t = [None] * 3, [None] * 3, {}
        with ExitStack() as inner:
            xn = psb("xn", [P, TT, D], ctx=inner)
            stage_norm(g, f"pre{layer}", g.h, xn, (a["pre_g_2"], layer * D), None, GDN_EPS, False)

        def outputs(n):
            s.yh[n], s.yl[n] = psb(f"yh{n}", [P, BF, T], F32R), psb(f"yl{n}", [P, BF, T], F32R)

        outputs(1)
        with ExitStack() as inner:
            s.t["zb"], s.t["mla"] = psb("zb", [P, BF, T], ctx=inner), psb("mla", [P, TT, MLA_COLS], ctx=inner)
            s.mq, s.mk = psb("mq", [MLA_QK, MH, T], ctx=inner), psb("mk", [MLA_QK, MH, T], ctx=inner)
            s.mv = psb("mv", [P, TT, MH * 64], ctx=inner)
            with ExitStack() as loads:
                s.latent = latent_tiles(lambda name, shape: psb(name, shape, ctx=loads))
                stage_branch_project(g, a, layer, s, "b", runs["b"], runs["c"])
                stage_latent(g, a, layer, s)
            stage_latent_attend(g, a, layer, s)
        outputs(2)
        with ExitStack() as inner:
            for x in ("qc", "kc", "vc", "zc"):
                s.t[x] = psb(x, [P, BF, T], ctx=inner)
            stage_branch_project(g, a, layer, s, "c", runs["c"], runs["a"])
            stage_band_attend(g, a, layer, s)
        outputs(0)
        with ExitStack() as inner:
            for x in ("u", "va", "za"):
                s.t[x] = psb(x, [P, BF, T], ctx=inner)
            stage_branch_project(g, a, layer, s, "a", runs["a"], runs["gates"])
            stage_spatial_gate(g, a, layer, s)
        stage_merge(g, a, layer, s, runs["gates"], runs["out"])
    stage_branch_out(g, a, layer, runs["out"], nxt, store)


class Globals:
    pass


def consts():
    i = np.arange(P)
    c = {}
    c["c_ident"] = np.eye(P, dtype=np.float32)
    c["c_ones"] = np.ones((P, P), np.float32)
    c["c_triu"] = (i[:, None] <= i[None, :]).astype(np.float32)
    c["c_neg_below"] = np.where(i[:, None] > i[None, :], np.float32(NEG), np.float32(0))
    sel = np.zeros((16, 16, P), np.float32)
    for r in range(16):
        sel[r, r, :] = 1
    c["c_sel"] = sel
    lev = np.zeros((LEVELS, P, P), np.float32)
    for l in range(LEVELS):
        s = 1 << l
        same = (i[:, None] // (2 * s)) == (i[None, :] // (2 * s))
        lev[l] = same & ((i[:, None] // s) % 2 == 0) & ((i[None, :] // s) % 2 == 1)
    c["c_levels"] = lev
    c["c_striu"] = (i[:, None] < i[None, :]).astype(np.float32)
    c["c_desc"] = np.arange(4, 0, -1, dtype=np.float32)[None]
    c["c_iota"] = np.tile(np.arange(2 * P, dtype=np.float32), (P, 1))
    c["c_iota_b"] = np.tile(np.arange(MAX_BLOCKS, dtype=np.float32)[None, :, None], (1, 1, N_EXP))
    dist = np.arange(NSA_ROW) - T
    near = np.maximum(dist, 0)
    far = np.maximum(near, 1).astype(np.float32)
    large = 16 + (np.log(far / np.float32(16)) / np.float32(math.log(128 / 16)) * np.float32(16)).astype(np.int32)
    bucket = np.where(near < 16, near, np.minimum(large, 31))
    c["c_t5_onehot"] = (bucket[None, :] == np.arange(32)[:, None]).astype(np.float32) * (dist >= 0)
    c["c_t5_onehot"] = c["c_t5_onehot"].astype(np.float32)
    c["c_t5_mask"] = np.where(dist < 0, np.float32(-NEG), np.float32(0))[None].astype(np.float32)
    tq = np.arange(TT)[None, :, None] * P + i[:, None, None]
    c["c_cmp_valid"] = (np.arange(N_CMP)[None, None, :] * 16 + 31 <= tq).astype(np.float32)
    bb = np.zeros((P, T), np.float32)
    bb[:64, :64] = -NEG
    c["c_block_bias"] = bb
    half = MLA_ROPE // 2
    inv = np.float32(10000.0) ** (-np.arange(half, dtype=np.float32) / np.float32(half))
    ang = (np.arange(T, dtype=np.float32)[:, None] * inv[None, :]).astype(np.float32)
    cos, sin = np.cos(ang).astype(np.float32), np.sin(ang).astype(np.float32)
    c["c_rope_cos"] = np.ascontiguousarray(cos.reshape(TT, P, half).transpose(1, 0, 2))
    c["c_rope_sin"] = np.ascontiguousarray(sin.reshape(TT, P, half).transpose(1, 0, 2))
    scale = np.float32(-MLA_SCALE)
    c["c_ropeq_cos"] = np.tile(np.concatenate([cos.T, cos.T]) * scale, (4, 1))
    c["c_ropeq_sin"] = np.tile(np.concatenate([-sin.T, sin.T]) * scale, (4, 1))
    return c


def nsa_layer(g, a, run, out_run):
    nc = g.nc
    with ExitStack() as part:
        n = Globals()

        def psb(name, shape):
            return part.enter_context(nc.sbuf_tensor("nsa_" + name, shape, F32))
        n.qt, n.kt = psb("qt", [P, NSA_H // 2, T]), psb("kt", [P, 2, NSA_G, T])
        n.v, n.gate = psb("v", [P, TT, 2 * NSA_G * DH]), psb("gate", [P, TT, 3 * NSA_H])
        n.kct, n.vc = psb("kct", [P, NSA_G, N_CMP]), psb("vc", [N_CMP, NSA_G, DH])
        with ExitStack() as inner:
            n.raw, n.w1, n.w2k, n.w2v = (inner.enter_context(nc.sbuf_tensor("nsa_" + x, shape, F32)) for x, shape in
                                         (("raw", [P, 2, NSA_G + 1, T]), ("w1", [P, 2, 16, P]),
                                          ("w2k", [P, 2, DH]), ("w2v", [P, DH])))
            stage_nsa_project(g, a, run, out_run, n)
            stage_nsa_compress(g, a, n)
        n.pct = psb("pct", [N_CMP, NSA_H, T])
        stage_nsa_cmp(g, a, n)
        stage_nsa_attend(g, a, n)
    stage_out_proj(g, "nwo", out_run, ALPHA)


def nsa_norm(g, a):
    stage_norm(g, "ln1", g.h, g.h, (a["ln_mix_g"], D), (a["ln_mix_b"], D), LN_EPS, True)


def moe_layer(g, a, layer):
    nc = g.nc
    with ExitStack() as part:
        rt = Globals()

        def psb(name, shape, dt=F32):
            return part.enter_context(nc.sbuf_tensor(f"rt{layer}_{name}", shape, dt))
        rt.slot, rt.slot_i, rt.weight = psb("slot", [P, TT, 2]), psb("slot_i", [P, TT, 2], I32), psb("weight", [P, TT, 2])
        rt.table = psb("table", [1, MAX_BLOCKS + 1], I32)
        rt.hh, rt.hl = g.xh[:].rearrange("p (t a) n -> p t (a n)", t=TT), g.xl[:].rearrange("p (t a) n -> p t (a n)", t=TT)
        stage_route(g, f"route{layer}", a, layer, rt)
        stage_experts(g, f"exp{layer}", a, layer, rt)


def ffn_norm(g, a, layer, nxt):
    stage_norm(g, f"ffn_ln{layer}", g.h, g.h, (a["ln_ffn_g"], layer * D), (a["ln_ffn_b"], layer * D), LN_EPS, True, nxt)


def program(nc, a):
    with ExitStack() as ctx:
        g = Globals()
        g.nc = nc

        def sb(name, shape, dt=F32):
            return ctx.enter_context(nc.sbuf_tensor(name, shape, dt))
        g.h = sb("h", [P, TT, D])
        g.xh, g.xl = sb("xh", [P, KT, T], F32R), sb("xl", [P, KT, T], F32R)
        g.ident, g.ones, g.triu, g.neg_below, g.striu = (sb(n, [P, P]) for n in
                                                        ("ident", "ones", "triu", "neg_below", "striu"))
        g.moe_rows = nc.dram_tensor("moe_rows", (MAX_BLOCKS * P, D), F32, kind="Internal").ap()
        g.nsa_rows = nc.dram_tensor("nsa_rows", (NSA_H, NSA_ROW), F32, kind="Internal").ap()
        g.ca_rows = nc.dram_tensor("ca_rows", (16, CA_ROW), F32, kind="Internal").ap()
        g.eps5, g.eps6 = sb("eps5", [P, 1]), sb("eps6", [P, 1])
        g.row = lambda r, n: g.sel[0:n, r, :]
        g.colsel = sb("colsel", [P, 31])
        g.column = lambda r, n: g.colsel[:, 15 - r:15 - r + n]

        with Stage(nc, "eps") as st:
            s, s2 = st.sem("set"), st.sem("cleared")
            with nc.Block() as block:
                @block.gpsimd
                def _(pool):
                    pool.memset(g.eps5[:], LN_EPS).then_inc(s, 1)
                    pool.memset(g.eps6[:], GDN_EPS).then_inc(s, 1)
                    pool.memset(g.colsel[:], 0.0).then_inc(s2, 1)
                    pool.wait_ge(s2, 1)
                    pool.memset(g.colsel[:, 15:16], 1.0).then_inc(s, 1)

        with ExitStack() as part:
            def psb(name, shape, dt=F32):
                return part.enter_context(nc.sbuf_tensor(name, shape, dt))
            qkvz = psb("qkvz", [P, 4 * GDN_H, T])
            ab = psb("ab", [P, TT, 16])
            gt = {x: psb("gt_" + x, [P, TT * GDN_H]) for x in
                  ("g", "beta", "neg_gc", "gl", "egc", "beta_egc", "rest", "tmp", "dlast", "krest")}
            g.sel = psb("sel", [16, 16, P], F32R)
            with Stage(nc, "in_weights") as region:
                slots = WeightSlots(region)
                run = WeightRun(slots, 8, lambda b: column_block(a["gdn_w_in"][0], 0, b * 512))
                stage_load(g, a, run)
                stage_gdn_project(g, a, run, qkvz, ab)
            stage_gdn_norm(g, a, qkvz)
            stage_gdn_gates(g, a, ab, gt)
            with ExitStack() as inner:
                qk_t = inner.enter_context(nc.sbuf_tensor("qk_t", [P, GDN_H, T], F32))
                k_dec = inner.enter_context(nc.sbuf_tensor("k_dec", [P, GDN_H, T], F32))
                stage_gdn_chunks(g, a, qkvz, gt, qk_t, k_dec)
                stage_gdn_scan(g, a, qkvz, gt, qk_t, k_dec)
            with Stage(nc, "gdn_out_weights") as region:
                run = WeightRun(WeightSlots(region), 2, lambda b: column_block(a["gdn_w_o"][0], 0, b * 512))
                stage_gdn_out(g, a, run, qkvz)
                stage_out_proj(g, "gwo", run, ALPHA)
        stage_norm(g, "ln0", g.h, g.h, (a["ln_mix_g"], 0), (a["ln_mix_b"], 0), LN_EPS, True)
        moe_layer(g, a, 0)
        with Stage(nc, "nsa_weights") as region:
            slots = WeightSlots(region)
            blocks = nsa_blocks(a)
            run = WeightRun(slots, len(blocks), lambda b: blocks[b][0], parts=2)
            out_run = WeightRun(slots, 2, lambda b: column_block(a["nsa_w_o"][0], 0, b * 512))
            ffn_norm(g, a, 0, run)
            stage_tables(g, a)
            nsa_layer(g, a, run, out_run)
        nsa_norm(g, a)
        moe_layer(g, a, 1)
        with Stage(nc, "branch_weights") as region:
            slots = WeightSlots(region)
            runs = [layer_runs(slots, a, layer) for layer in range(2)]
            ffn_norm(g, a, 1, runs[0]["b"])
            branch_layer(g, a, 0, runs[0], runs[1]["b"], None)
            branch_layer(g, a, 1, runs[1], None, a["out"][0])


IN_NAMES = [
    "x", "gdn_w_in", "gdn_conv_w", "gdn_a_log", "gdn_dt_bias", "gdn_norm_w", "gdn_w_o", "nsa_w_kv", "cmp_k_pos",
    "cmp_k_w1", "cmp_k_w2", "cmp_v_pos", "cmp_v_w1", "cmp_v_w2", "nsa_w_in", "nsa_w_o", "rel_bias", "ln_mix_g",
    "ln_mix_b", "ln_ffn_g", "ln_ffn_b", "moe_w_grp", "moe_b_grp", "moe_w_rt", "moe_b_rt", "moe_w_gate",
    "moe_w_up", "moe_w_down", "w_in_2", "pre_g_2", "post_g_2", "sgu_ln_g_2", "sgu_ln_b_2", "sgu_w_2", "sgu_b_2",
    "mla_q_norm_g_2", "mla_kv_norm_g_2", "mla_w_uq_2", "mla_w_ukv_2", "ca_rel_bias_2", "w_branch_2",
    "gate_b_2", "w_out_2",
]


def kernel(**inputs):
    import concourse.bacc as bacc
    from concourse.bass_utils import run_bass_kernel_spmd

    nc = bacc.Bacc("TRN2", target_bir_lowering=False, num_devices=1)
    arrays = {name: np.ascontiguousarray(inputs[name]) for name in IN_NAMES}
    arrays.update(consts())
    a = {name: nc.dram_tensor(name, x.shape, mybir.dt.from_np(x.dtype), kind="ExternalInput").ap()
         for name, x in arrays.items()}
    a["out"] = nc.dram_tensor("out", (1, T, D), F32, kind="ExternalOutput").ap()
    program(nc, a)
    result = run_bass_kernel_spmd(nc, [arrays], core_ids=[0])
    return result.results[0]["out"]
```
